# Optimizing a Trainium2 kernel written in Bass

```python
import jax, jax.numpy as jnp
from jax import lax
import numpy as np

D_MODEL = 1024
BATCH = 1
SEQ = 2048
DEPTH = 1

CTX_LEN = 256
GRID_W = 64
EPS = 1e-6
D_RNN = 512
RNN_BLOCKS = 8
RNN_BLOCK_W = D_RNN // RNN_BLOCKS
RNN_CONV_W = 4
RNN_CONV_LEFT = 2
LRU_C = 8.0
HEAD_DIM = 64
N_Q_HEADS = 8
N_KV_HEADS = 2
Q_PER_KV = N_Q_HEADS // N_KV_HEADS
D_ATTN = N_Q_HEADS * HEAD_DIM
D_KV = N_KV_HEADS * HEAD_DIM
D_MIX = D_RNN + D_ATTN
D_IN = 2 * D_RNN + D_ATTN + 2 * D_KV
IN_SPLITS = (D_RNN, 2 * D_RNN, 2 * D_RNN + D_ATTN, 2 * D_RNN + D_ATTN + D_KV)
WINDOW = 128
BLOCK_Q = 128
ROPE_THETA = 10000.0
NEG_INF = -1e30
D_FF = 2816
FFN_CONV_W = 3
FFN_CONV_LEFT = 1

kernel_name = "hybrid_rglru_swa_convffn_dit_layer"

def rms_norm(x, g):
    xf = x.astype(jnp.float32)
    y = xf * lax.rsqrt(jnp.mean(xf * xf, axis=-1, keepdims=True) + EPS)
    return (y * g.astype(jnp.float32)).astype(x.dtype)

def adaln(cond, w_mod, b_mod):
    m = (jax.nn.silu(cond) @ w_mod + b_mod)[..., None, :]
    return jnp.split(m, 6, axis=-1)

def modulate(h, shift, scale):
    return h * (1 + scale) + shift

def dwconv(x, w, b, left):
    k = w.shape[0]
    s = x.shape[1]
    xp = jnp.pad(x, ((0, 0), (left, k - 1 - left), (0, 0)))
    out = b
    for j in range(k):
        out = out + xp[:, j:j + s] * w[j]
    return out

def rope_1d(x, pos):
    half = x.shape[-1] // 2
    inv = ROPE_THETA ** (-jnp.arange(half, dtype=jnp.float32) / half)
    ang = pos.astype(jnp.float32)[:, None] * inv[None, :]
    cos = jnp.cos(ang)[:, None, :].astype(x.dtype)
    sin = jnp.sin(ang)[:, None, :].astype(x.dtype)
    x1, x2 = x[..., :half], x[..., half:]
    return jnp.concatenate([x1 * cos - x2 * sin, x2 * cos + x1 * sin], axis=-1)

def rope_2d(x, row, col):
    d = HEAD_DIM // 2
    return jnp.concatenate([rope_1d(x[..., :d], row), rope_1d(x[..., d:], col)], axis=-1)

def linear_scan(a, u, h0):
    def combine(l, r):
        return l[0] * r[0], r[0] * l[1] + r[1]
    a_cum, b_cum = lax.associative_scan(combine, (a, u), axis=1)
    return a_cum * h0[:, None, :] + b_cum

def rglru_coeffs(xr, w_a, b_a, w_i, b_i, lam):
    xf = xr.astype(jnp.float32)
    xb = xf.reshape(xf.shape[:-1] + (RNN_BLOCKS, RNN_BLOCK_W))
    r = jax.nn.sigmoid(jnp.einsum('bsnc,ncd->bsnd', xb, w_a.astype(jnp.float32)).reshape(xf.shape) + b_a.astype(jnp.float32))
    i = jax.nn.sigmoid(jnp.einsum('bsnc,ncd->bsnd', xb, w_i.astype(jnp.float32)).reshape(xf.shape) + b_i.astype(jnp.float32))
    log_a = -LRU_C * r * jax.nn.softplus(-lam.astype(jnp.float32))
    a = jnp.exp(log_a)
    u = jnp.sqrt(-jnp.expm1(2.0 * log_a)) * (i * xf)
    return a, u

def rglru_bidir(x_lat, x_ctx, w_a, b_a, w_i, b_i, lam, with_ctx_out):
    y_lat = jnp.zeros(x_lat.shape, jnp.float32)
    y_ctx = jnp.zeros(x_ctx.shape, jnp.float32)
    h0 = jnp.zeros((x_ctx.shape[0], D_RNN), jnp.float32)
    for d in range(2):
        a_c, u_c = rglru_coeffs(x_ctx, w_a[d], b_a[d], w_i[d], b_i[d], lam[d])
        a_l, u_l = rglru_coeffs(x_lat, w_a[d], b_a[d], w_i[d], b_i[d], lam[d])
        if d == 1:
            a_c, u_c, a_l, u_l = (jnp.flip(t, axis=1) for t in (a_c, u_c, a_l, u_l))
        h_c = linear_scan(a_c, u_c, h0)
        h_l = linear_scan(a_l, u_l, h_c[:, -1])
        if d == 1:
            h_c, h_l = jnp.flip(h_c, axis=1), jnp.flip(h_l, axis=1)
        y_lat = y_lat + h_l
        if with_ctx_out:
            y_ctx = y_ctx + h_c
    return y_lat.astype(x_lat.dtype), (y_ctx.astype(x_ctx.dtype) if with_ctx_out else None)

def windowed_attention(q, k, v, qc, kc, vc, sink, with_ctx_out):
    B, S = q.shape[:2]
    L = kc.shape[1]
    nb = S // BLOCK_Q
    scale = HEAD_DIM ** -0.5
    qb = q.reshape(B, nb, BLOCK_Q, N_KV_HEADS, Q_PER_KV, HEAD_DIM)

    def band(t):
        tp = jnp.pad(t, ((0, 0), (BLOCK_Q, BLOCK_Q), (0, 0), (0, 0)))
        tp = tp.reshape(B, nb + 2, BLOCK_Q, N_KV_HEADS, HEAD_DIM)
        return jnp.concatenate([tp[:, :-2], tp[:, 1:-1], tp[:, 2:]], axis=2)

    kb, vb = band(k), band(v)
    qpos = jnp.arange(nb)[:, None] * BLOCK_Q + jnp.arange(BLOCK_Q)[None, :]
    kpos = (jnp.arange(nb)[:, None] - 1) * BLOCK_Q + jnp.arange(3 * BLOCK_Q)[None, :]
    mask = ((jnp.abs(qpos[:, :, None] - kpos[:, None, :]) <= WINDOW)
            & (kpos[:, None, :] >= 0) & (kpos[:, None, :] < S))
    s_loc = jnp.einsum('bnqhgd,bnkhd->bnhgqk', qb, kb).astype(jnp.float32) * scale
    s_loc = jnp.where(mask[None, :, None, None], s_loc, NEG_INF)
    s_ctx = jnp.einsum('bnqhgd,blhd->bnhgql', qb, kc).astype(jnp.float32) * scale
    sink_hg = sink.astype(jnp.float32).reshape(N_KV_HEADS, Q_PER_KV)
    s_sink = jnp.broadcast_to(sink_hg[None, None, :, :, None, None], s_loc.shape[:-1] + (1,))
    p = jax.nn.softmax(jnp.concatenate([s_loc, s_ctx, s_sink], axis=-1), axis=-1)
    p_loc = p[..., :3 * BLOCK_Q].astype(v.dtype)
    p_ctx = p[..., 3 * BLOCK_Q:3 * BLOCK_Q + L].astype(v.dtype)
    o = jnp.einsum('bnhgqk,bnkhd->bnqhgd', p_loc, vb) + jnp.einsum('bnhgql,blhd->bnqhgd', p_ctx, vc)
    o_lat = o.reshape(B, S, D_ATTN)
    o_ctx = None
    if with_ctx_out:
        qcg = qc.reshape(B, L, N_KV_HEADS, Q_PER_KV, HEAD_DIM)
        sc = jnp.einsum('blhgd,bmhd->bhglm', qcg, kc).astype(jnp.float32) * scale
        sc_sink = jnp.broadcast_to(sink_hg[None, :, :, None, None], sc.shape[:-1] + (1,))
        pc = jax.nn.softmax(jnp.concatenate([sc, sc_sink], axis=-1), axis=-1)[..., :L].astype(vc.dtype)
        o_ctx = jnp.einsum('bhglm,bmhd->blhgd', pc, vc).reshape(B, L, D_ATTN)
    return o_lat, o_ctx

def token_mixer(h, hc, row, col, w_in, rnn_conv_w, rnn_conv_b, lru_w_a, lru_b_a, lru_w_i, lru_b_i,
                lru_lam, attn_sink, gn_rnn, gn_attn, w_out, with_ctx_out):
    B, S = h.shape[:2]
    L = hc.shape[1]
    xr, xg, q, k, v = jnp.split(h @ w_in, IN_SPLITS, axis=-1)
    xrc, xgc, qc, kc, vc = jnp.split(hc @ w_in, IN_SPLITS, axis=-1)
    xr = dwconv(xr, rnn_conv_w, rnn_conv_b, RNN_CONV_LEFT)
    xrc = dwconv(xrc, rnn_conv_w, rnn_conv_b, RNN_CONV_LEFT)
    y_l, y_c = rglru_bidir(xr, xrc, lru_w_a, lru_b_a, lru_w_i, lru_b_i, lru_lam, with_ctx_out)
    rnn_l = jax.nn.gelu(xg) * y_l
    q = rope_2d(q.reshape(B, S, N_Q_HEADS, HEAD_DIM), row, col)
    k = rope_2d(k.reshape(B, S, N_KV_HEADS, HEAD_DIM), row, col)
    v = v.reshape(B, S, N_KV_HEADS, HEAD_DIM)
    qc = qc.reshape(B, L, N_Q_HEADS, HEAD_DIM)
    kc = kc.reshape(B, L, N_KV_HEADS, HEAD_DIM)
    vc = vc.reshape(B, L, N_KV_HEADS, HEAD_DIM)
    a_l, a_c = windowed_attention(q, k, v, qc, kc, vc, attn_sink, with_ctx_out)
    out_l = jnp.concatenate([rms_norm(rnn_l, gn_rnn), rms_norm(a_l, gn_attn)], axis=-1) @ w_out
    out_c = None
    if with_ctx_out:
        rnn_c = jax.nn.gelu(xgc) * y_c
        out_c = jnp.concatenate([rms_norm(rnn_c, gn_rnn), rms_norm(a_c, gn_attn)], axis=-1) @ w_out
    return out_l, out_c

def conv_ffn(h, w_up, conv_w, conv_b, w_down):
    u = dwconv(h @ w_up, conv_w, conv_b, FFN_CONV_LEFT)
    gate, val = jnp.split(u, 2, axis=-1)
    return (jax.nn.silu(gate) * val) @ w_down

def setup_inputs(seed: int = 0) -> dict:
    key = jax.random.key(seed)
    ks = jax.random.split(key, 25)
    nrm = jax.random.normal
    f32 = jnp.float32
    a0 = jax.random.uniform(ks[14], (DEPTH, 2, D_RNN), f32, 0.9, 0.999)
    return {
        "x": nrm(ks[0], (BATCH, SEQ, D_MODEL), f32),
        "c": nrm(ks[1], (BATCH, D_MODEL), f32),
        "ctx": nrm(ks[2], (BATCH, CTX_LEN, D_MODEL), f32),
        "c_ctx": nrm(ks[3], (D_MODEL,), f32),
        "w_mod": nrm(ks[4], (DEPTH, D_MODEL, 6 * D_MODEL), f32) * (0.5 * D_MODEL ** -0.5),
        "b_mod": nrm(ks[5], (DEPTH, 6 * D_MODEL), f32) * 0.02,
        "norm1_g": 1.0 + 0.02 * nrm(ks[6], (DEPTH, D_MODEL), f32),
        "w_in": nrm(ks[7], (DEPTH, D_MODEL, D_IN), f32) * D_MODEL ** -0.5,
        "rnn_conv_w": nrm(ks[8], (DEPTH, RNN_CONV_W, D_RNN), f32) * RNN_CONV_W ** -0.5,
        "rnn_conv_b": nrm(ks[9], (DEPTH, D_RNN), f32) * 0.02,
        "lru_w_a": nrm(ks[10], (DEPTH, 2, RNN_BLOCKS, RNN_BLOCK_W, RNN_BLOCK_W), f32) * RNN_BLOCK_W ** -0.5,
        "lru_b_a": nrm(ks[11], (DEPTH, 2, D_RNN), f32) * 0.02,
        "lru_w_i": nrm(ks[12], (DEPTH, 2, RNN_BLOCKS, RNN_BLOCK_W, RNN_BLOCK_W), f32) * RNN_BLOCK_W ** -0.5,
        "lru_b_i": nrm(ks[13], (DEPTH, 2, D_RNN), f32) * 0.02,
        "lru_lam": jnp.log(a0) - jnp.log1p(-a0),
        "attn_sink": nrm(ks[15], (DEPTH, N_Q_HEADS), f32) * 0.5,
        "gn_rnn": 1.0 + 0.02 * nrm(ks[16], (DEPTH, D_RNN), f32),
        "gn_attn": 1.0 + 0.02 * nrm(ks[17], (DEPTH, D_ATTN), f32),
        "w_out": nrm(ks[18], (DEPTH, D_MIX, D_MODEL), f32) * D_MIX ** -0.5,
        "norm2_g": 1.0 + 0.02 * nrm(ks[19], (DEPTH, D_MODEL), f32),
        "w_up": nrm(ks[20], (DEPTH, D_MODEL, 2 * D_FF), f32) * D_MODEL ** -0.5,
        "ffn_conv_w": nrm(ks[21], (DEPTH, FFN_CONV_W, 2 * D_FF), f32) * FFN_CONV_W ** -0.5,
        "ffn_conv_b": nrm(ks[22], (DEPTH, 2 * D_FF), f32) * 0.02,
        "w_down": nrm(ks[23], (DEPTH, D_FF, D_MODEL), f32) * D_FF ** -0.5,
        "final_g": 1.0 + 0.02 * nrm(ks[24], (D_MODEL,), f32),
    }

def reference(x, c, ctx, c_ctx, w_mod, b_mod, norm1_g, w_in, rnn_conv_w, rnn_conv_b, lru_w_a, lru_b_a,
              lru_w_i, lru_b_i, lru_lam, attn_sink, gn_rnn, gn_attn, w_out, norm2_g, w_up, ffn_conv_w,
              ffn_conv_b, w_down, final_g):
    S = x.shape[1]
    rows = S // GRID_W
    row = jnp.repeat(jnp.arange(rows, dtype=jnp.int32), GRID_W)
    col = jnp.tile(jnp.arange(GRID_W, dtype=jnp.int32), rows)
    for l in range(DEPTH):
        update_ctx = l < DEPTH - 1
        sh1, sc1, g1, sh2, sc2, g2 = adaln(c, w_mod[l], b_mod[l])
        csh1, csc1, cg1, csh2, csc2, cg2 = adaln(c_ctx, w_mod[l], b_mod[l])
        h = modulate(rms_norm(x, norm1_g[l]), sh1, sc1)
        hc = modulate(rms_norm(ctx, norm1_g[l]), csh1, csc1)
        out_l, out_c = token_mixer(h, hc, row, col, w_in[l], rnn_conv_w[l], rnn_conv_b[l], lru_w_a[l],
                                   lru_b_a[l], lru_w_i[l], lru_b_i[l], lru_lam[l], attn_sink[l],
                                   gn_rnn[l], gn_attn[l], w_out[l], update_ctx)
        x = x + g1 * out_l
        x = x + g2 * conv_ffn(modulate(rms_norm(x, norm2_g[l]), sh2, sc2), w_up[l], ffn_conv_w[l],
                              ffn_conv_b[l], w_down[l])
        if update_ctx:
            ctx = ctx + cg1 * out_c
            ctx = ctx + cg2 * conv_ffn(modulate(rms_norm(ctx, norm2_g[l]), csh2, csc2), w_up[l],
                                       ffn_conv_w[l], ffn_conv_b[l], w_down[l])
    return rms_norm(x, final_g)


_drawn_inputs = setup_inputs


def setup_inputs(seed=0):
    import zlib

    import numpy as np

    out = dict(_drawn_inputs(seed))
    spreads = {}
    factors = {'norm1_g': 8.0,
     'rnn_conv_b': 4.119,
     'lru_b_a': 27.051,
     'lru_b_i': 24.215,
     'attn_sink': 8.0,
     'gn_rnn': 23.481,
     'gn_attn': 25.645,
     'norm2_g': 8.0,
     'ffn_conv_b': 8.0,
     'final_g': 8.141}
    for name, (base, spread) in spreads.items():
        noise = np.random.default_rng([zlib.crc32(name.encode()), seed]).standard_normal(out[name].shape)
        drawn = base * np.exp(spread * noise) if base else spread * noise
        out[name] = __import__('jax').numpy.asarray(drawn.astype(out[name].dtype))
    for name, factor in factors.items():
        out[name] = (out[name] * factor).astype(out[name].dtype)
    return out
```

```python
from contextlib import ExitStack

import numpy as np

import concourse.bass as bass
from concourse import mybir
from concourse.alu_op_type import AluOpType as ALU

F32 = mybir.dt.float32
F32R = mybir.dt.float32r
BF16 = mybir.dt.bfloat16
ACT = mybir.ActivationFunctionType
AX_X = mybir.AxisListType.X
ds = bass.ds

P = 128
D = 1024
KD = D // P
S = 2048
L = 256
T = S + L
GRID_W = 64
EPS = 1e-6
D_RNN = 512
RNN_TILES = D_RNN // P
D_ATTN = 512
HEAD = 64
N_HEADS = 8
N_KV = 2
PER_KV = N_HEADS // N_KV
SCALE = HEAD ** -0.5
ROPE_THETA = 10000.0
D_IN = 2 * D_RNN + D_ATTN + 2 * N_KV * HEAD
LRU_C = 8.0
D_FF = 2816
FT = D_FF // P
BQ = 128
NB = S // BQ
CH = 512
NCH = S // CH
NEG = -1e30
GELU_C = 2.0 * float(np.sqrt(2.0 / np.pi))
GELU_A = 0.044715


class Kit:

    def __init__(self, nc, ctx):
        self.nc, self.ctx = nc, ctx
        self.psum = ctx.enter_context(nc.psum_tensor("psum", [P, 8, CH], F32))
        self.phase_sems = []

    def sem(self, name):
        self.phase_sems.append(self.nc.alloc_semaphore(name))
        return self.phase_sems[-1]

    def next_phase(self):
        with self.nc.Block() as block:

            @block.gpsimd
            def _(pool):
                self.nc.clear_and_free_semaphores(self.phase_sems)

        self.phase_sems = []

    def dram(self, name, shape, dt):
        return self.nc.dram_tensor(name, shape, dt).ap()

    def keep(self, name, shape, dt):
        return self.ctx.enter_context(self.nc.sbuf_tensor(name, shape, dt))


def modulation_and_norm(k, a, hT_hi, hT_lo, keep, scratch):
    nc, psum = k.nc, k.psum
    ident, aff2 = keep["ident"], keep["aff2"]
    w_mod, b_mod, mod_rows = a["w_mod"], a["b_mod"], scratch["mod"]
    with ExitStack() as ctx:
        def sb(name, shape, dt=F32):
            return ctx.enter_context(nc.sbuf_tensor(name, shape, dt))

        w_slot = [sb(f"wmod{i}", [P, KD, CH]) for i in range(2)]
        row = [sb(f"mod_row{i}", [2, CH]) for i in range(2)]
        x_slot = [sb(f"xnorm{i}", [P, D]) for i in range(2)]
        junk = [sb(f"square_junk{i}", [P, D], BF16) for i in range(2)]
        vec_rows = sb("vec_rows", [4 * KD, P])
        mod_rows_sb = [sb(f"mod_rows_sb{i}", [4 * KD, P]) for i in range(2)]
        vec_cols = sb("vec_cols", [P, 4 * KD])
        mod_cols = [sb(f"mod_cols{i}", [P, 4 * KD]) for i in range(2)]
        cond_silu = sb("cond_silu", [P, 2, KD])
        aff1 = sb("aff1", [P, 2, 2, KD])
        sumsq, rstd, eps_col = sb("sumsq", [P, 20]), sb("rstd", [P, 20]), sb("eps_col", [P, 1])
        t32 = [sb(f"t32_{i}", [P, 2 * P]) for i in range(2)]

        s_vec = k.sem("vectors_landed")
        s_w = [k.sem(f"wmod_landed{i}") for i in range(2)]
        s_bias = [k.sem(f"bias_landed{i}") for i in range(2)]
        s_row_stored = [k.sem(f"mod_row_stored{i}") for i in range(2)]
        s_modrows = k.sem("mod_rows_landed")
        s_x = [k.sem(f"x_landed{i}") for i in range(2)]
        s_ident = k.sem("ident_ready")
        s_small = k.sem("small_transposed")
        s_cols = k.sem("cols_ready")
        s_silu = k.sem("silu_ready")
        s_row = k.sem("mod_row_in_psum")
        s_row_out = k.sem("mod_row_ready")
        s_aff = k.sem("affine_ready")
        s_sq = k.sem("sumsq_ready")
        s_std = k.sem("std_ready")
        s_rstd = k.sem("rstd_ready")
        s_xn = k.sem("xn_ready")
        s_tp = k.sem("x_transposed")
        s_t32 = k.sem("modulated_ready")
        s_hi = k.sem("hT_hi_ready")
        s_lo = k.sem("hT_lo_ready")

        ROW_BANK, SMALL_BANK, TP_BANK = (0, 1), 2, (3, 4, 5, 6)
        PAIRS = T // (2 * P)
        CHUNKS = 6 * D // CH

        with nc.Block() as block:

            @block.sync
            def _(sp):
                sp.dma_start(vec_rows[0:KD, :], a["c"].rearrange("a (k p) -> (a k) p", p=P)).then_inc(s_vec, 16)
                sp.dma_start(vec_rows[KD:2 * KD, :], a["c_ctx"].rearrange("(k p) -> k p", p=P)).then_inc(s_vec, 16)
                sp.dma_start(vec_rows[2 * KD:3 * KD, :], a["norm1_g"].rearrange("a (k p) -> (a k) p", p=P)).then_inc(s_vec, 16)
                sp.dma_start(vec_rows[3 * KD:4 * KD, :], a["norm2_g"].rearrange("a (k p) -> (a k) p", p=P)).then_inc(s_vec, 16)
                with sp.Fori(0, CHUNKS // 2) as i:
                    for slot in range(2):
                        sp.wait_ge(s_row_out, i * 2 + slot + 1)
                        sp.dma_start(w_slot[slot][:], w_mod[0, :, ds(i * 2 * CH + slot * CH, CH)].rearrange("(k p) n -> p k n", p=P)).then_inc(s_w[slot], 16)

            @block.gpsimd
            def _(pool):
                nc.gpsimd.memset(ident[:], 0.0).then_inc(s_ident, 1)
                pool.wait_ge(s_ident, 1)
                nc.gpsimd.affine_select(out=ident[:], in_=ident[:], compare_op=ALU.not_equal, fill=1.0, base=0,
                                        pattern=[[-1, P]], channel_multiplier=1).then_inc(s_ident, 1)

                def bias(q, slot):
                    pool.dma_start(row[slot][:], b_mod[0:1, ds(q * CH, CH)].broadcast_to([2, CH])).then_inc(s_bias[slot], 16)

                def store(q, slot, turn):
                    pool.wait_ge(s_row_out, q + 3)
                    pool.dma_start(mod_rows[:, ds(q * CH, CH)], row[slot][:]).then_inc(s_row_stored[slot], 16)
                    pool.wait_ge(s_row_stored[slot], turn * 16 + 16)

                def reload(part, first):
                    for z in range(2):
                        pool.dma_start(mod_rows_sb[part][z * 2 * KD:(z + 1) * 2 * KD, :],
                                       mod_rows[z, first:first + 2 * D].rearrange("(m p) -> m p", p=P)).then_inc(s_modrows, 16)

                bias(0, 0)
                bias(1, 1)
                for q in range(4):
                    store(q, q % 2, q // 2)
                    bias(q + 2, q % 2)
                reload(0, 0)
                with pool.Fori(2, CHUNKS // 2 - 1) as i:
                    for slot in range(2):
                        store(i * 2 + slot, slot, i)
                        bias(i * 2 + slot + 2, slot)
                for slot in range(2):
                    store(CHUNKS - 2 + slot, slot, CHUNKS // 2 - 1)
                reload(1, 3 * D)
                pool.wait_ge(s_modrows, 64)

            @block.scalar
            def _(act):
                for j in range(2):
                    act.dma_start(x_slot[j][:], a["x"][0, j * P:(j + 1) * P, :]).then_inc(s_x[j], 16)
                act.wait_ge(s_cols, 1)
                act.activation(cond_silu[:], vec_cols[:, 0:2 * KD].rearrange("p (a k) -> p a k", a=2), ACT.Silu).then_inc(s_silu, 1)
                act.wait_ge(s_rstd, 1)

                def pair(n, z, following):
                    for j in range(2):
                        act.wait_ge(s_x[j], n * 16 + 16)
                        act.activation(junk[j][:], x_slot[j][:], ACT.Square, accum_out=sumsq[:, ds(n * 2 + j, 1)]).then_inc(s_sq, 1)
                    act.wait_ge(s_sq, n * 2 + 2)
                    act.activation(rstd[:, ds(n * 2, 2)], sumsq[:, ds(n * 2, 2)], ACT.Sqrt, bias=eps_col[:], scale=1.0 / D).then_inc(s_std, 1)
                    if following != "context" or z == 0:
                        act.wait_ge(s_aff, 4)
                    for kt in range(KD):
                        act.wait_ge(s_tp, n * KD + kt + 1)
                        act.wait_ge(s_lo, n * KD + kt + 1)
                        act.activation(t32[kt % 2][:], psum[:, TP_BANK[kt % 4], 0:2 * P], ACT.Identity,
                                       bias=aff1[:, z, 1, kt:kt + 1], scale=aff1[:, z, 0, kt:kt + 1]).then_inc(s_t32, 1)
                    for j in range(2):
                        if following == "latent":
                            act.dma_start(x_slot[j][:], a["x"][0, ds(n * 2 * P + (2 + j) * P, P), :]).then_inc(s_x[j], 16)
                        elif following == "context":
                            act.dma_start(x_slot[j][:], a["ctx"][0, j * P:(j + 1) * P, :]).then_inc(s_x[j], 16)

                with act.Fori(0, PAIRS - 2) as n:
                    pair(n, 0, "latent")
                pair(PAIRS - 2, 0, "context")
                pair(PAIRS - 1, 1, None)

            @block.tensor
            def _(pe):
                pe.wait_ge(s_ident, 2)
                pe.wait_ge(s_vec, 64)
                pe.transpose(psum[:, SMALL_BANK, 0:4 * KD], vec_rows[:], ident[0:4 * KD, 0:4 * KD]).then_inc(s_small, 1)
                pe.wait_ge(s_silu, 1)

                def chunk(q, slot, turn):
                    pe.wait_ge(s_row_out, q + 1)
                    pe.wait_ge(s_w[slot], turn * 16 + 16)
                    for kt in range(KD):
                        mm = pe.matmul(psum[0:2, ROW_BANK[slot], :], cond_silu[:, :, kt], w_slot[slot][:, kt, :], start=(kt == 0), stop=(kt == KD - 1))
                    mm.then_inc(s_row, 1)

                def mod_columns(part):
                    pe.wait_ge(s_modrows, 32 * (part + 1))
                    pe.wait_ge(s_cols, part + 1)
                    pe.transpose(psum[:, SMALL_BANK, 0:4 * KD], mod_rows_sb[part][:], ident[0:4 * KD, 0:4 * KD]).then_inc(s_small, 1)

                def pair(n):
                    pe.wait_ge(s_xn, n * 2 + 2)
                    for kt in range(KD):
                        pe.wait_ge(s_t32, n * KD + kt + 1)
                        for j in range(2):
                            tp = pe.transpose(psum[:, TP_BANK[kt % 4], j * P:(j + 1) * P], x_slot[j][:, kt * P:(kt + 1) * P], ident[:])
                        tp.then_inc(s_tp, 1)

                for q in range(4):
                    chunk(q, q % 2, q // 2)
                mod_columns(0)
                with pe.Fori(0, 4) as n:
                    pair(n * 2)
                    chunk(n * 2 + 4, 0, n + 2)
                    pair(n * 2 + 1)
                    chunk(n * 2 + 5, 1, n + 2)
                pair(PAIRS - 1)
                mod_columns(1)

            @block.vector
            def _(dve):
                dve.sem_inc(s_row_out, 2)
                dve.sem_inc(s_lo, 2)
                dve.sem_inc(s_t32, 4)
                dve.memset(eps_col[:], EPS).then_inc(s_rstd, 1)
                dve.wait_ge(s_small, 1)
                dve.tensor_copy(vec_cols[:], psum[:, SMALL_BANK, 0:4 * KD]).then_inc(s_cols, 1)

                def take_row(q, slot, turn):
                    dve.wait_ge(s_row, q + 1)
                    dve.wait_ge(s_bias[slot], turn * 16 + 16)
                    dve.tensor_tensor(row[slot][:], psum[0:2, ROW_BANK[slot], :], row[slot][:], ALU.add).then_inc(s_row_out, 1)

                def take_columns(part):
                    dve.wait_ge(s_small, part + 2)
                    dve.tensor_copy(mod_cols[part][:], psum[:, SMALL_BANK, 0:4 * KD]).then_inc(s_cols, 1)
                    dve.wait_ge(s_cols, part + 2)

                for q in range(4):
                    take_row(q, q % 2, q // 2)
                take_columns(0)
                for z in range(2):
                    at = z * 2 * KD
                    dve.scalar_tensor_tensor(aff1[:, z, 0, :], mod_cols[0][:, at + KD:at + 2 * KD], 1.0, vec_cols[:, 2 * KD:3 * KD], ALU.add, ALU.mult).then_inc(s_aff, 1)
                    dve.tensor_copy(aff1[:, z, 1, :], mod_cols[0][:, at:at + KD]).then_inc(s_aff, 1)

                def pair(n):
                    dve.wait_ge(s_std, n + 1)
                    dve.reciprocal(rstd[:, ds(n * 2, 2)], rstd[:, ds(n * 2, 2)]).then_inc(s_rstd, 1)
                    dve.wait_ge(s_rstd, n + 2)
                    for j in range(2):
                        dve.tensor_scalar(x_slot[j][:], x_slot[j][:], rstd[:, ds(n * 2 + j, 1)], None, ALU.mult).then_inc(s_xn, 1)
                    for kt in range(KD):
                        dve.wait_ge(s_t32, n * KD + kt + 5)
                        hi = hT_hi[:, kt, ds(n * 2 * P, 2 * P)]
                        dve.tensor_copy(hi, t32[kt % 2][:]).then_inc(s_hi, 1)
                        dve.wait_ge(s_hi, n * KD + kt + 1)
                        dve.tensor_tensor(hT_lo[:, kt, ds(n * 2 * P, 2 * P)], t32[kt % 2][:], hi.bitcast(F32), ALU.subtract).then_inc(s_lo, 1)

                with dve.Fori(0, 4) as n:
                    pair(n * 2)
                    take_row(n * 2 + 4, 0, n + 2)
                    pair(n * 2 + 1)
                    take_row(n * 2 + 5, 1, n + 2)
                pair(PAIRS - 1)
                take_columns(1)
                dve.scalar_tensor_tensor(aff2[:, 0, :], mod_cols[1][:, KD:2 * KD], 1.0, vec_cols[:, 3 * KD:4 * KD], ALU.add, ALU.mult).then_inc(s_aff, 1)
                dve.tensor_copy(aff2[:, 1, :], mod_cols[1][:, 0:KD]).then_inc(s_aff, 1)


def input_projection(k, a, hT_hi, hT_lo, scratch):
    nc, psum = k.nc, k.psum
    w_in = a["w_in"]
    with ExitStack() as ctx:
        def sb(name, shape, dt=F32):
            return ctx.enter_context(nc.sbuf_tensor(name, shape, dt))

        w_raw = [sb(f"win_raw{i}", [P, KD, P]) for i in range(2)]
        w_hi = [sb(f"win_hi{i}", [P, KD, P], F32R) for i in range(2)]
        w_lo = [sb(f"win_lo{i}", [P, KD, P], F32R) for i in range(2)]
        cos, sin = sb("cos", [P, S]), sb("sin", [P, S])
        stage = [sb(f"stage{i}", [P, CH if i < NCH else L]) for i in range(NCH + 1)]
        swapped, turned = sb("swapped", [P, CH]), sb("turned", [P, CH])
        cut_hi = [sb(f"cut_hi{i}", [P, CH], F32R) for i in range(2)]
        cut_lo = [sb(f"cut_lo{i}", [P, CH], F32R) for i in range(2)]

        s_rope = k.sem("rope_tables_landed")
        s_w = [k.sem(f"win_landed{i}") for i in range(2)]
        s_hi = k.sem("win_hi_ready")
        s_lo = k.sem("win_lo_ready")
        s_acc = k.sem("projection_ready")
        s_stage = k.sem("stage_ready")
        s_free = [k.sem(f"stage_free{i}") for i in range(NCH + 1)]
        s_step = k.sem("rope_step")
        s_cut = k.sem("qk_cut")
        s_hi_cut = k.sem("qk_hi_ready")
        s_cut_stored = [k.sem(f"cut_stored{i}") for i in range(2)]

        KINDS = ((0, 4, True, False, scratch["xr"], 0, 0, 0), (4, 4, False, False, scratch["xg"], 4, 4, 0),
                 (8, 4, False, True, None, 8, 4, 0), (12, 1, True, True, None, 8, 4, 16),
                 (13, 1, True, False, scratch["v"], 13, 5, 21))
        LAST = 13

        def walk(body):
            def run(eng):
                unit = 0
                for m0, count, with_ctx, rope, dram, d0, ctx0, rope0 in KINDS:
                    per = NCH + with_ctx
                    if count > 1:
                        with eng.Fori(0, count // 2) as i:
                            for j in range(2):
                                body(eng, m0 + j + i * 2, j, i + m0 // 2, unit + per * j + i * (2 * per), with_ctx, rope, dram,
                                     j + i * 2 + (m0 - d0), ctx0 + j + i * 2, rope0 + j * NCH + i * (2 * NCH), False)
                    else:
                        body(eng, m0, m0 % 2, m0 // 2, unit, with_ctx, rope, dram, m0 - d0, ctx0, rope0, m0 == LAST)
                    unit += per * count
            return run

        def chunks(with_ctx):
            return [(c, c * CH, CH) for c in range(NCH)] + ([(NCH, S, L)] if with_ctx else [])

        def bank(slot, c):
            return 4 * slot + c if c < NCH else 4 * (1 - slot) + 3

        with nc.Block() as block:

            @block.sync
            def _(sp):
                def load(m, slot, turn):
                    sp.wait_ge(s_lo, m + 1)
                    sp.dma_start(w_raw[slot][:], w_in[0, :, ds(m * P, P)].rearrange("(k p) n -> p k n", p=P)).then_inc(s_w[slot], 16)

                def body(sp, m, slot, turn, unit, with_ctx, rope, dram, row, nctx, nrope, last):
                    if not last:
                        load(m + 1, 1 - slot, None)
                    for c, t0, n in chunks(with_ctx):
                        if rope:
                            half = c % 2
                            sp.wait_ge(s_cut, nrope + c + 1)
                            sp.sem_inc(s_free[c], 16)
                            dst = (ds(row * P, P), slice(t0, t0 + n))
                            sp.dma_start(scratch["qk_hi"][dst[0], dst[1]], cut_hi[half][:, 0:n].bitcast(F32)).then_inc(s_cut_stored[half], 16)
                            sp.dma_start(scratch["qk_lo"][dst[0], dst[1]], cut_lo[half][:, 0:n].bitcast(F32)).then_inc(s_cut_stored[half], 16)
                        else:
                            sp.wait_ge(s_stage, unit + c + 5)
                            sp.dma_start(dram[ds(row * P, P), t0:t0 + n], stage[c][:, 0:n]).then_inc(s_free[c], 16)

                sp.dma_start(cos[:], a["rope_cos"]).then_inc(s_rope, 16)
                sp.dma_start(sin[:], a["rope_sin"]).then_inc(s_rope, 16)
                load(0, 0, None)
                walk(body)(sp)
                for c in range(NCH):
                    sp.wait_ge(s_free[c], 16 * (14 + 1))
                sp.wait_ge(s_free[NCH], 16 * (6 + 1))
                sp.wait_ge(s_cut_stored[0], 32 * (8 + 3 + 1))
                sp.wait_ge(s_cut_stored[1], 32 * (8 + 2 + 1))

            @block.gpsimd
            def _(pool):
                pool.sem_inc(s_lo, 2)

                def cut(m, slot):
                    pool.wait_ge(s_hi, m + 1)
                    nc.gpsimd.tensor_tensor(w_lo[slot][:], w_raw[slot][:], w_hi[slot][:].bitcast(F32), ALU.subtract).then_inc(s_lo, 1)

                def body(pool, m, slot, turn, unit, with_ctx, rope, dram, row, nctx, nrope, last):
                    if not last:
                        cut(m + 1, 1 - slot)

                cut(0, 0)
                walk(body)(pool)

            @block.scalar
            def _(act):
                act.sem_inc(s_stage, 4)
                act.sem_inc(s_acc, 1)
                for c in range(NCH + 1):
                    act.sem_inc(s_free[c], 16)
                for half in range(2):
                    act.sem_inc(s_cut_stored[half], 32)

                def cut(slot, turn, units_before):
                    act.wait_ge(s_w[slot], turn * 16 + 16)
                    act.wait_ge(s_acc, units_before + 1)
                    act.activation(w_hi[slot][:], w_raw[slot][:], ACT.Copy).then_inc(s_hi, 1)

                def body(act, m, slot, turn, unit, with_ctx, rope, dram, row, nctx, nrope, last):
                    if not last:
                        cut(1 - slot, turn + slot, unit)
                    for c, t0, n in chunks(with_ctx):
                        act.wait_ge(s_acc, unit + c + 2)
                        act.wait_ge(s_free[c], ((m if c < NCH else nctx) + 1) * 16)
                        act.activation(stage[c][:, 0:n], psum[:, bank(slot, c), 0:n], ACT.Copy).then_inc(s_stage, 1)

                cut(0, 0, 0)
                walk(body)(act)

            @block.tensor
            def _(pe):
                def body(pe, m, slot, turn, unit, with_ctx, rope, dram, row, nctx, nrope, last):
                    pe.wait_ge(s_lo, m + 3)
                    for c, t0, n in chunks(with_ctx):
                        pe.wait_ge(s_stage, unit + c + 1)
                        for kt in range(KD):
                            for wp, hp in ((w_hi, hT_hi), (w_hi, hT_lo), (w_lo, hT_hi)):
                                mm = pe.matmul(psum[:, bank(slot, c), 0:n], wp[slot][:, kt, :], hp[:, kt, t0:t0 + n],
                                               start=(kt == 0 and wp is w_hi and hp is hT_hi), stop=(kt == KD - 1 and wp is w_lo))
                        mm.then_inc(s_acc, 1)

                walk(body)(pe)

            @block.vector
            def _(dve):
                dve.wait_ge(s_rope, 32)

                def rotated(dve, m, slot, turn, unit, with_ctx, rope, dram, row, nctx, nrope, last):
                    if not rope:
                        return
                    tq, nrope_half = row, row * 2
                    for c, t0, n in chunks(with_ctx):
                        half = c % 2
                        dve.wait_ge(s_stage, unit + c + 5)
                        done = nrope * 4 + c * 4
                        if c < NCH:
                            nc.vector.tensor_tensor(turned[:], stage[c][:], cos[:, t0:t0 + n], ALU.mult).then_inc(s_step, 1)
                            nc.vector.stream_shuffle(swapped[:], stage[c][:], [(i + 16) % 32 for i in range(32)]).then_inc(s_step, 1)
                            dve.wait_ge(s_step, done + 2)
                            nc.vector.tensor_tensor(swapped[:], swapped[:], sin[:, t0:t0 + n], ALU.mult).then_inc(s_step, 1)
                            dve.wait_ge(s_step, done + 3)
                            nc.vector.tensor_tensor(stage[c][:], turned[:], swapped[:], ALU.add).then_inc(s_step, 1)
                            dve.wait_ge(s_step, done + 4)
                        dve.wait_ge(s_cut_stored[half], nrope_half * 32 + (c // 2 + 1) * 32)
                        nc.vector.tensor_copy(cut_hi[half][:, 0:n], stage[c][:, 0:n]).then_inc(s_hi_cut, 1)
                        dve.wait_ge(s_hi_cut, nrope + c + 1)
                        nc.vector.tensor_tensor(cut_lo[half][:, 0:n], stage[c][:, 0:n], cut_hi[half][:, 0:n].bitcast(F32), ALU.subtract).then_inc(s_cut, 1)

                walk(rotated)(dve)


def mixers(k, a, keep, scratch):
    nc, psum = k.nc, k.psum
    ident = keep["ident"]
    GAP = 4
    LAT = L + GAP
    W = LAT + S
    KW = L + P + S + P
    SUB = 4
    HEADS = SUB * N_HEADS
    GROUPS = SUB * N_KV
    ROUNDS = NB // SUB
    GATE_UNITS = 4 * (NCH + 1)
    DVE_RNN = 13
    assert ROUNDS == RNN_TILES

    EVENTS = []
    for u in range(HEADS + 5):
        n8 = u % 8
        if n8 == 1 and u < HEADS:
            EVENTS.append(("v", u // 8))
        if u >= 6 and (u - 6) % 4 == 0 and (u - 6) // 4 < GROUPS:
            EVENTS.append(("pv", (u - 6) // 4))
        if u >= 7 and (u - 7) % 4 == 0 and (u - 7) // 4 < GROUPS:
            EVENTS.append(("turn", (u - 7) // 4))
        if u >= 12 and (u - 12) % 8 == 0 and (u - 12) // 8 < SUB:
            EVENTS.append(("out", (u - 12) // 8))
    PRE = 3

    def event(it, kind, index):
        return it * len(EVENTS) + EVENTS.index((kind, index)) + PRE

    with ExitStack() as ctx:
        def sb(name, shape, dt=F32):
            return ctx.enter_context(nc.sbuf_tensor(name, shape, dt))

        keys = sb("keys_hi_lo", [P, N_KV, KW], F32R)
        q_same = [sb(f"q_hi_lo{i}", [P, N_HEADS, P], F32R) for i in range(2)]
        q_cross = [sb(f"q_lo_hi{i}", [P, N_HEADS, P], F32R) for i in range(2)]
        prob = [sb(f"prob{i}", [P, 5 * P]) for i in range(2)]
        pT_hi = [sb(f"probT_hi{i}", [P, 5, PER_KV, P], F32R) for i in range(2)]
        pT_lo = [sb(f"probT_lo{i}", [P, 5, PER_KV, P], F32R) for i in range(2)]
        v_raw = [sb(f"v_raw{i}", [P, P]) for i in range(2)]
        v_ctx = sb("v_ctx", [P, 2, N_KV, 2 * HEAD], F32R)
        v_ring = sb("v_ring", [P, 4, N_KV, 2 * HEAD], F32R)
        oT = sb("oT", [P, CH])
        o_scaled = sb("o_scaled", [P, PER_KV, 2 * HEAD])
        o_tok = sb("o_tok", [P, D_ATTN])
        o_out = sb("o_out", [P, 4, P])
        ident_bf = sb("ident_bf", [P, P], BF16)
        mask_before, mask_after = sb("mask_before", [P, P], BF16), sb("mask_after", [P, P], BF16)
        mask_first, mask_last = sb("mask_first", [P, ROUNDS, P], BF16), sb("mask_last", [P, ROUNDS, P], BF16)
        sink = sb("sink", [P, N_HEADS])
        neg_sink = sb("neg_sink", [P, N_HEADS])
        row_max, neg_max, row_sum, sink_in, sink_exp, inv_sum = (
            [sb(f"{n}{i}", [P, N_HEADS]) for i in range(2)] for n in ("row_max", "neg_max", "row_sum", "sink_in", "sink_exp", "inv_sum"))
        gate_raw = sb("gate_raw", [P, 4, P])
        gate_hi, gate_lo = sb("gate_hi", [P, 4, P], F32R), sb("gate_lo", [P, 4, P], F32R)
        g_r = [sb("decay_gate0", [P, W + GAP]), sb("decay_gate1", [P, W + GAP])]
        g_i = [sb(f"input_gate{d}", [P, W]) for d in range(2)]
        th = [sb(f"tanh_half{d}", [P, W]) for d in range(2)]
        x_pad = g_r[1]
        xc, xc_hi, xc_lo = sb("xc", [P, W]), sb("xc_hi", [P, W], F32R), sb("xc_lo", [P, W], F32R)
        xg, gel = sb("xg_sb", [P, S]), sb("gelu_sb", [P, S])
        par_rows, par = sb("rnn_rows", [44, P]), sb("rnn_cols", [P, 44])
        sp_e, sp_s, sp_p, sp_pos = (sb(n, [P, 8]) for n in ("sp_e", "sp_s", "sp_p", "sp_pos"))
        c_exp, c_tanh = sb("c_exp", [P, 8]), sb("c_tanh", [P, 8])
        CONV_W, CONV_B, B_A, B_I, LAM = 0, 16, 20, 28, 36

        sem = k.sem
        s_setup, s_par, s_parT, s_parc = sem("setup_ready"), sem("params_landed"), sem("params_transposed"), sem("params_step")
        s_keys, s_pads, s_sink = sem("keys_landed"), sem("pads_ready"), sem("sink_landed")
        s_mask = sem("masks_ready")
        s_q = [sem(f"q_landed{i}") for i in range(2)]
        s_vraw = [sem(f"v_landed{i}") for i in range(2)]
        s_vt = sem("v_transposed")
        s_vhi = sem("v_hi_ready")
        s_misc = sem("shared_bank_taken")
        s_sc = sem("scores_ready")
        s_mx, s_nm = sem("row_max_ready"), sem("neg_max_ready")
        s_exp = sem("prob_ready")
        s_pt = sem("prob_transposed")
        s_pthi, s_ptlo = sem("probT_hi_ready"), sem("probT_lo_ready")
        s_pv, s_turn, s_out = sem("pv_ready"), sem("oT_turned"), sem("o_turned")
        s_sin, s_ses, s_den, s_inv = sem("sink_in_ready"), sem("sink_exp_ready"), sem("sum_ready"), sem("inv_sum_ready")
        s_tok, s_ssq, s_msq = sem("o_tok_ready"), sem("o_sumsq_ready"), sem("o_mean_square_ready")
        s_gbias, s_gelu_turn = sem("gate_biases_ready"), sem("gelu_square_seen")
        o_ssq, gate_bias = sb("o_ssq", [P, 1]), sb("gate_bias", [P, 4])
        s_ostored = sem("o_stored")
        s_gw, s_gwhi, s_gwlo = sem("gate_w_landed"), sem("gate_hi_ready"), sem("gate_lo_ready")
        s_gacc, s_gout = sem("gate_in_psum"), sem("gate_out")
        s_xr, s_xg = sem("xr_landed"), sem("xg_landed")
        s_pre, s_sg, s_gelu = sem("gelu_arg_ready"), sem("gelu_sigmoid_ready"), sem("gelu_ready")
        s_xi = sem("gated_x_ready")
        s_th, s_a, s_sq = sem("tanh_ready"), sem("decay_ready"), sem("sqrt_ready")
        s_v, s_hi, s_lo = sem("rnn_vector_step"), sem("xc_hi_ready"), sem("xc_lo_ready")
        s_y, s_ystored = sem("y_ready"), sem("y_stored")
        s_pad0 = sem("x_pad_zeroed")
        s_gap = sem("gaps_filled")
        s_series = sem("series_step")

        GATE_BANKS, S_BANK, PT_BANK, MISC = 4, (0, 2), 4, 6
        PT = psum[:, PT_BANK:PT_BANK + 2, :].rearrange("p b c -> p (b c)")[:, 0:5 * P]

        def S_cols(s, c0, c1):
            return psum[:, S_BANK[s]:S_BANK[s] + 2, :].rearrange("p b c -> p (b c)")[:, c0:c1]

        def rnn_chunks():
            return [(0, 0, L)] + [(1 + c, LAT + c * CH, CH) for c in range(NCH)]

        def rounds(eng, body):
            with eng.Fori(0, ROUNDS - 1) as it:
                body(it, False)
            body(ROUNDS - 1, True)

        with nc.Block() as block:

            @block.sync
            def _(sp):
                rows = (("rnn_conv_w", 16), ("rnn_conv_b", 4), ("lru_b_a", 8), ("lru_b_i", 8), ("lru_lam", 8))
                at = 0
                for name, n in rows:
                    src = a[name][0] if name != "rnn_conv_b" else a[name]
                    sp.dma_start(par_rows[at:at + n, :], src.rearrange("a (j p) -> (a j) p", p=P)).then_inc(s_par, 16)
                    at += n

                def load_q(n, par_):
                    tok = ds(n * P, P)
                    hi = scratch["qk_hi"][0:D_ATTN, tok].rearrange("(h d) t -> d h t", d=HEAD)
                    lo = scratch["qk_lo"][0:D_ATTN, tok].rearrange("(h d) t -> d h t", d=HEAD)
                    for tile, top, low in ((q_same, hi, lo), (q_cross, lo, hi)):
                        sp.dma_start(tile[par_][0:HEAD, :, :].bitcast(F32), top).then_inc(s_q[par_], 16)
                        sp.dma_start(tile[par_][HEAD:P, :, :].bitcast(F32), low).then_inc(s_q[par_], 16)

                def load_v(col, slot):
                    sp.dma_start(v_raw[slot][:], scratch["v"][:, col]).then_inc(s_vraw[slot], 16)

                load_v(ds(S, P), 0)
                load_v(ds(S + P, P), 1)
                load_q(0, 0)
                sp.wait_ge(s_vt, 1)
                load_v(ds(0, P), 0)

                def body(it, last):
                    for n in range(SUB):
                        sp.wait_ge(s_vt, it * SUB + n + 2)
                        load_v(ds(it * (SUB * P) + (n + 1) * P, P), (n + 1) % 2)
                        if not (last and n == SUB - 1):
                            sp.wait_ge(s_sc, it * HEADS + n * N_HEADS + 1)
                            load_q(it * SUB + n + 1, (n + 1) % 2)
                        if n:
                            store(it, n - 1)
                        if n == SUB - 1:
                            sp.wait_ge(s_y, it + 1)
                            sp.dma_start(scratch["mix"][ds(it * P, P), :], g_i[0][:, LAT:W]).then_inc(s_ystored, 16)
                    store(it, SUB - 1)

                def store(it, n):
                    sp.wait_ge(s_misc, event(it, "out", n) + 2)
                    sp.dma_start(scratch["mix"][D_RNN:D, ds(it * (SUB * P) + n * P, P)].rearrange("(f p) t -> p f t", p=P),
                                 o_out[:]).then_inc(s_ostored, 16)

                rounds(sp, body)
                sp.wait_ge(s_ostored, 16 * (NB + 1))
                sp.wait_ge(s_ystored, 16 * (ROUNDS + 1))

            @block.gpsimd
            def _(pool):
                nc.gpsimd.memset(gate_raw[:], 0.0).then_inc(s_setup, 1)
                pool.wait_ge(s_setup, 1)

                def load_gates(it):
                    for g, name in enumerate(("lru_w_a", "lru_w_i")):
                        for b in range(2):
                            pool.dma_start(gate_raw[b * 64:(b + 1) * 64, 2 * g:2 * g + 2, b * 64:(b + 1) * 64],
                                           a[name][0, :, ds(it * 2 + b, 1), :, :].rearrange("d o c e -> c (d o) e")).then_inc(s_gw, 16)

                def load_xr(it):
                    pool.dma_start(x_pad[:, 2:2 + L], scratch["xr"][ds(it * P, P), S:T]).then_inc(s_xr, 16)
                    pool.dma_start(x_pad[:, 2 + LAT:2 + W], scratch["xr"][ds(it * P, P), 0:S]).then_inc(s_xr, 16)

                def load_xg(it):
                    pool.dma_start(xg[:], scratch["xg"][ds(it * P, P), :]).then_inc(s_xg, 16)

                load_xr(0)
                load_gates(0)
                load_xg(0)
                nc.gpsimd.memset(mask_before[:], 0.0).then_inc(s_mask, 1)
                nc.gpsimd.memset(mask_after[:], 0.0).then_inc(s_mask, 1)
                nc.gpsimd.tensor_copy(ident_bf[:], ident[:]).then_inc(s_mask, 1)
                pool.wait_ge(s_mask, 3)
                nc.gpsimd.affine_select(out=mask_before[:], in_=mask_before[:], compare_op=ALU.is_ge, fill=NEG, base=0,
                                        pattern=[[1, P]], channel_multiplier=-1).then_inc(s_mask, 1)
                nc.gpsimd.affine_select(out=mask_after[:], in_=mask_after[:], compare_op=ALU.is_ge, fill=NEG, base=0,
                                        pattern=[[-1, P]], channel_multiplier=1).then_inc(s_mask, 1)
                pool.wait_ge(s_mask, 5)
                for r in range(ROUNDS):
                    if r == 0:
                        nc.gpsimd.memset(mask_first[:, r, :], NEG).then_inc(s_mask, 1)
                    else:
                        nc.gpsimd.tensor_copy(mask_first[:, r, :], mask_before[:]).then_inc(s_mask, 1)
                    if r == ROUNDS - 1:
                        nc.gpsimd.memset(mask_last[:, r, :], NEG).then_inc(s_mask, 1)
                    else:
                        nc.gpsimd.tensor_copy(mask_last[:, r, :], mask_after[:]).then_inc(s_mask, 1)

                def body(it, last):
                    pool.wait_ge(s_xg, it * 16 + 16)
                    nc.gpsimd.tensor_tensor(gel[:], xg[:], xg[:], ALU.mult).then_inc(s_pre, 1)
                    pool.wait_ge(s_pre, it * 3 + 1)
                    pool.sem_inc(s_gelu_turn, 1)
                    nc.gpsimd.tensor_scalar(gel[:], gel[:], GELU_A, 1.0, ALU.mult, ALU.add).then_inc(s_pre, 1)
                    pool.wait_ge(s_pre, it * 3 + 2)
                    nc.gpsimd.tensor_tensor(gel[:], gel[:], xg[:], ALU.mult).then_inc(s_pre, 1)
                    pool.wait_ge(s_gout, it * GATE_UNITS + GATE_UNITS + 4)
                    for d in range(2):
                        nc.gpsimd.tensor_tensor(g_i[d][:], g_i[d][:], xc[:], ALU.mult).then_inc(s_xi, 1)
                    pool.wait_ge(s_sg, it + 1)
                    nc.gpsimd.tensor_tensor(gel[:], gel[:], xg[:], ALU.mult).then_inc(s_gelu, 1)
                    if not last:
                        load_gates(it + 1)
                        pool.wait_ge(s_gelu, it + 1)
                        load_xg(it + 1)
                        pool.wait_ge(s_v, it * DVE_RNN + 4 + 8)
                        load_xr(it + 1)
                    pool.wait_ge(s_y, it + 1)

                rounds(pool, body)

            @block.scalar
            def _(act):
                for kv in range(N_KV):
                    rows = slice(D_ATTN + kv * HEAD, D_ATTN + (kv + 1) * HEAD)
                    for half, src in ((0, scratch["qk_hi"]), (1, scratch["qk_lo"])):
                        dst = keys[half * HEAD:(half + 1) * HEAD, kv, :].bitcast(F32)
                        act.dma_start(dst[:, 0:L], src[rows, S:T]).then_inc(s_keys, 16)
                        act.dma_start(dst[:, L + P:L + P + S], src[rows, 0:S]).then_inc(s_keys, 16)
                act.dma_start(sink[:], a["attn_sink"].broadcast_to([P, N_HEADS])).then_inc(s_sink, 16)
                act.wait_ge(s_parc, 1)
                act.activation(sp_e[:], par[:, LAM:LAM + 8], ACT.Abs).then_inc(s_parc, 1)
                act.wait_ge(s_parc, 2)
                act.activation(sp_e[:], sp_e[:], ACT.Exp, scale=-1.0).then_inc(s_parc, 1)
                act.sem_inc(s_gout, 4)
                act.sem_inc(s_exp, 2)
                act.sem_inc(s_misc, 1)
                act.sem_inc(s_ostored, 16)
                act.sem_inc(s_ystored, 16)

                def body(it, last):
                    act.wait_ge(s_ystored, it * 16 + 16)
                    act.wait_ge(s_gap, it + 4)
                    act.wait_ge(s_gbias, it + 1)
                    for g in range(2):
                        for d in range(2):
                            bias = gate_bias[:, g * 2 + d:g * 2 + d + 1]
                            for c, t0, n in rnn_chunks():
                                v = (g * 2 + d) * (NCH + 1) + c
                                act.wait_ge(s_gacc, it * GATE_UNITS + v + 1)
                                act.activation((g_r, g_i)[g][d][:, t0:t0 + n], psum[:, v % GATE_BANKS, 0:n], ACT.Sigmoid, bias=bias).then_inc(s_gout, 1)
                    act.wait_ge(s_pre, it * 3 + 3)
                    act.activation(gel[:], gel[:], ACT.Sigmoid, scale=GELU_C).then_inc(s_sg, 1)

                    for u in range(HEADS + 5):
                        if u < HEADS:
                            s, h, n = u % 2, u % 8, (u // 8) % 2
                            act.wait_ge(s_nm, it * HEADS + u + 1)
                            act.wait_ge(s_pt, it * HEADS + u + 1)
                            act.activation(prob[s][:], S_cols(s, P, 6 * P), ACT.Exp, bias=neg_max[n][:, h:h + 1], scale=SCALE,
                                           accum_out=row_sum[n][:, h:h + 1]).then_inc(s_exp, 1)
                        if 1 <= u <= HEADS:
                            w = u - 1
                            G = w // 4
                            act.wait_ge(s_pt, it * HEADS + w + 3)
                            act.wait_ge(s_pv, it * GROUPS + G + 1)
                            act.activation(pT_hi[G % 2][:, :, w % 4, :], PT.rearrange("p (b q) -> p b q", q=P), ACT.Copy).then_inc(s_pthi, 1)
                        if u % 4 == 0 and 4 <= u <= HEADS:
                            G = u // 4 - 1
                            n, kv = (G // 2) % 2, G % 2
                            act.wait_ge(s_sin, it * GROUPS + G + 1)
                            act.activation(sink_exp[n][:, kv * 4:kv * 4 + 4], sink_in[n][:, kv * 4:kv * 4 + 4], ACT.Exp).then_inc(s_ses, 1)
                        if u >= 6 and (u - 6) % 4 == 0 and (u - 6) // 4 < GROUPS:
                            G = (u - 6) // 4
                            act.wait_ge(s_pv, it * GROUPS + G + 3)
                            act.wait_ge(s_turn, it * GROUPS + G + 1)
                            act.activation(oT[:], psum[:, MISC, :], ACT.Copy).then_inc(s_misc, 1)
                        if u >= 12 and (u - 12) % 8 == 0 and (u - 12) // 8 < SUB:
                            n = (u - 12) // 8
                            act.wait_ge(s_out, it * SUB + n + 2)
                            act.wait_ge(s_ostored, (it * SUB + n) * 16 + 16)
                            act.activation(o_out[:].rearrange("p f t -> p (f t)"), psum[:, MISC, :], ACT.Copy).then_inc(s_misc, 1)
                        if u in (1, 2):
                            d = u - 1
                            act.activation(th[d][:], g_r[d][:, 0:W], ACT.Tanh, scale=c_tanh[:, ds(it + d * RNN_TILES, 1)]).then_inc(s_th, 1)
                        if u in (3, 4):
                            d = u - 3
                            act.wait_ge(s_th, it * 2 + d + 1)
                            act.activation(g_r[d][:, 0:W], g_r[d][:, 0:W], ACT.Exp, scale=c_exp[:, ds(it + d * RNN_TILES, 1)]).then_inc(s_a, 1)
                        if u == 5:
                            for d in range(2):
                                act.activation(th[d][:], th[d][:], ACT.Sqrt).then_inc(s_sq, 1)

                act.wait_ge(s_parc, 13)
                rounds(act, body)

            @block.tensor
            def _(pe):
                pe.wait_ge(s_par, 80)
                pe.transpose(psum[:, 7, 0:44], par_rows[:], ident[0:44, 0:44]).then_inc(s_parT, 1)

                def turn_v(e, slot, landed):
                    pe.wait_ge(s_vraw[slot], landed)
                    pe.wait_ge(s_misc, e + 1)
                    pe.transpose(psum[:, MISC, 0:P], v_raw[slot][:], ident[:]).then_inc(s_vt, 1)

                turn_v(0, 0, 16)
                turn_v(1, 1, 16)
                turn_v(2, 0, 32)
                pe.wait_ge(s_keys, 16 * 8)
                pe.wait_ge(s_pads, 2 * N_KV + 1)
                pe.wait_ge(s_mask, 5 + 2 * ROUNDS)

                def body(it, last):
                    pe.wait_ge(s_gwlo, it + 1)
                    pe.wait_ge(s_lo, it + 1)
                    pe.wait_ge(s_exp, it * HEADS + 2)
                    for g in range(2):
                        for d in range(2):
                            for c, t0, n in rnn_chunks():
                                v = (g * 2 + d) * (NCH + 1) + c
                                pe.wait_ge(s_gout, it * GATE_UNITS + v + 1)
                                for i, (wt, xt) in enumerate(((gate_hi, xc_hi), (gate_hi, xc_lo), (gate_lo, xc_hi))):
                                    mm = pe.matmul(psum[:, v % GATE_BANKS, 0:n], wt[:, g * 2 + d, :], xt[:, t0:t0 + n], start=(i == 0), stop=(i == 2))
                                mm.then_inc(s_gacc, 1)
                    pe.wait_ge(s_gout, it * GATE_UNITS + GATE_UNITS + 4)

                    for u in range(HEADS + 5):
                        if u < HEADS:
                            s, h, n = u % 2, u % 8, u // 8
                            kv, slot = h // PER_KV, n % 2
                            if h == 0:
                                pe.wait_ge(s_q[slot], (it * 2 + n // 2) * 64 + 64)
                            pe.wait_ge(s_exp, it * HEADS + u + 1)
                            local = ds(it * (SUB * P) + n * P + L, 3 * P)
                            before = mask_first[:, ds(it, 1), :].rearrange("p o c -> p (o c)") if n == 0 else mask_before[:]
                            after = mask_last[:, ds(it, 1), :].rearrange("p o c -> p (o c)") if n == SUB - 1 else mask_after[:]
                            pe.matmul(S_cols(s, P, 4 * P), q_same[slot][:, h, :], keys[:, kv, local], start=True, stop=False)
                            pe.matmul(S_cols(s, P, 4 * P), q_cross[slot][:, h, :], keys[:, kv, local], start=False, stop=False)
                            pe.matmul(S_cols(s, P, 2 * P), ident_bf[:], before, start=False, stop=False)
                            pe.matmul(S_cols(s, 3 * P, 4 * P), ident_bf[:], after, start=False, stop=True)
                            pe.matmul(S_cols(s, 4 * P, 6 * P), q_same[slot][:, h, :], keys[:, kv, 0:L], start=True, stop=False)
                            pe.matmul(S_cols(s, 4 * P, 6 * P), q_cross[slot][:, h, :], keys[:, kv, 0:L], start=False, stop=True).then_inc(s_sc, 1)
                        if 1 <= u <= HEADS:
                            w = u - 1
                            pe.wait_ge(s_exp, it * HEADS + w + 3)
                            pe.wait_ge(s_ptlo, it * HEADS + w + 1)
                            for b in range(5):
                                tp = pe.transpose(PT[:, b * P:(b + 1) * P], prob[w % 2][:, b * P:(b + 1) * P], ident[:])
                            tp.then_inc(s_pt, 1)
                        if u % 8 == 1 and u < HEADS:
                            n = u // 8
                            slot = (n + 1) % 2
                            turn_v(event(it, "v", n), slot, (it * 2 + n // 2) * 16 + (32 if slot == 1 else 48))
                        if u >= 6 and (u - 6) % 4 == 0 and (u - 6) // 4 < GROUPS:
                            G = (u - 6) // 4
                            n, kv = G // 2, G % 2
                            pe.wait_ge(s_ptlo, it * HEADS + 4 * G + 5)
                            e = event(it, "pv", G)
                            pe.wait_ge(s_misc, e + 1)
                            for b in range(5):
                                v_b = v_ring[:, (n - 1 + b) % 4, kv, :] if b < 3 else v_ctx[:, b - 3, kv, :]
                                for pT in (pT_hi, pT_lo):
                                    mm = pe.matmul(psum[:, MISC, :], v_b, pT[G % 2][:, b, :, :], start=(b == 0 and pT is pT_hi), stop=(b == 4 and pT is pT_lo))
                            mm.then_inc(s_pv, 1)
                        if u >= 7 and (u - 7) % 4 == 0 and (u - 7) // 4 < GROUPS:
                            G = (u - 7) // 4
                            pe.wait_ge(s_misc, event(it, "turn", G) + 1)
                            for h in range(PER_KV):
                                tp = pe.transpose(psum[:, MISC, h * P:(h + 1) * P], oT[:, h * P:(h + 1) * P], ident[:])
                            tp.then_inc(s_turn, 1)
                        if u >= 12 and (u - 12) % 8 == 0 and (u - 12) // 8 < SUB:
                            n = (u - 12) // 8
                            pe.wait_ge(s_tok, it * GROUPS + 2 * n + 2)
                            pe.wait_ge(s_misc, event(it, "out", n) + 1)
                            for f in range(4):
                                tp = pe.transpose(psum[:, MISC, f * P:(f + 1) * P], o_tok[:, f * P:(f + 1) * P], ident[:])
                            tp.then_inc(s_out, 1)

                rounds(pe, body)

            @block.vector
            def _(dve):
                dve.sem_inc(s_ptlo, 1)
                dve.sem_inc(s_pt, 2)
                dve.sem_inc(s_pv, 2)
                dve.sem_inc(s_turn, 1)
                dve.sem_inc(s_out, 1)
                dve.sem_inc(s_ssq, 1)
                dve.sem_inc(s_msq, 1)
                for kv in range(N_KV):
                    for at in (L, L + P + S):
                        dve.memset(keys[:, kv, at:at + P].bitcast(F32), 0.0).then_inc(s_pads, 1)
                dve.memset(v_ring[:, 3, :, :].bitcast(F32), 0.0).then_inc(s_pads, 1)
                for t in (g_r[0], g_i[0], g_i[1]):
                    dve.memset(t[:, L:LAT], 0.5).then_inc(s_gap, 1)
                dve.wait_ge(s_parT, 1)
                dve.tensor_copy(par[:], psum[:, 7, 0:44]).then_inc(s_parc, 1)
                dve.wait_ge(s_sink, 16)
                dve.tensor_scalar(neg_sink[:], sink[:], -1.0, None, ALU.mult).then_inc(s_mx, 1)
                dve.wait_ge(s_parc, 3)
                dve.tensor_scalar(sp_s[:], sp_e[:], 2.0, None, ALU.add).then_inc(s_parc, 1)
                dve.wait_ge(s_parc, 4)
                dve.reciprocal(sp_s[:], sp_s[:]).then_inc(s_parc, 1)
                dve.wait_ge(s_parc, 5)
                dve.tensor_tensor(sp_s[:], sp_s[:], sp_e[:], ALU.mult).then_inc(s_parc, 1)
                dve.wait_ge(s_parc, 6)
                dve.tensor_tensor(sp_e[:], sp_s[:], sp_s[:], ALU.mult).then_inc(s_parc, 1)
                dve.memset(sp_p[:], 1.0 / 17).then_inc(s_parc, 1)
                dve.wait_ge(s_parc, 8)
                for j, odd in enumerate((15, 13, 11, 9, 7, 5, 3, 1)):
                    dve.tensor_tensor(sp_p[:], sp_p[:], sp_e[:], ALU.mult).then_inc(s_series, 1)
                    dve.wait_ge(s_series, 2 * j + 1)
                    dve.tensor_scalar(sp_p[:], sp_p[:], 1.0 / odd, None, ALU.add).then_inc(s_series, 1)
                    dve.wait_ge(s_series, 2 * j + 2)
                dve.scalar_tensor_tensor(sp_p[:], sp_p[:], 2.0, sp_s[:], ALU.mult, ALU.mult).then_inc(s_parc, 1)
                dve.tensor_scalar(sp_pos[:], par[:, LAM:LAM + 8], -1.0, 0.0, ALU.mult, ALU.max).then_inc(s_parc, 1)
                dve.wait_ge(s_parc, 10)
                dve.tensor_tensor(sp_p[:], sp_p[:], sp_pos[:], ALU.add).then_inc(s_parc, 1)
                dve.wait_ge(s_parc, 11)
                dve.tensor_scalar(c_exp[:], sp_p[:], -LRU_C, None, ALU.mult).then_inc(s_parc, 1)
                dve.tensor_scalar(c_tanh[:], sp_p[:], LRU_C / 2, None, ALU.mult).then_inc(s_parc, 1)

                def cut_v(slot_ap, count):
                    dve.wait_ge(s_vt, count + 1)
                    src = psum[:, MISC, 0:P].rearrange("p (g d) -> p g d", g=N_KV)
                    dve.tensor_copy(slot_ap[:, :, 0:HEAD], src).then_inc(s_vhi, 1)
                    dve.wait_ge(s_vhi, count + 1)
                    dve.tensor_tensor(slot_ap[:, :, HEAD:2 * HEAD], src, slot_ap[:, :, 0:HEAD].bitcast(F32), ALU.subtract).then_inc(s_misc, 1)

                cut_v(v_ctx[:, 0], 0)
                cut_v(v_ctx[:, 1], 1)
                cut_v(v_ring[:, 0], 2)

                def convolve(it, done):
                    for at, n in ((0, 2), (2 + L, GAP), (2 + W, 1)):
                        dve.memset(x_pad[:, at:at + n], 0.0).then_inc(s_pad0, 1)
                    dve.wait_ge(s_pad0, it * 3 + 3)
                    dve.wait_ge(s_xr, it * 32 + 32)
                    dve.tensor_scalar(xc[:], x_pad[:, 0:W], par[:, ds(it + CONV_W, 1)], par[:, ds(it + CONV_B, 1)], ALU.mult, ALU.add).then_inc(s_v, 1)
                    for j in range(1, 4):
                        dve.wait_ge(s_v, done + j)
                        dve.scalar_tensor_tensor(xc[:], x_pad[:, j:j + W], par[:, ds(it + CONV_W + j * RNN_TILES, 1)], xc[:], ALU.mult, ALU.add).then_inc(s_v, 1)
                    dve.wait_ge(s_v, done + 4)
                    dve.memset(x_pad[:, L:LAT], 0.5).then_inc(s_gap, 1)

                def gate_biases(it):
                    dve.tensor_copy(gate_bias[:].rearrange("p (g o) -> p g o", o=1),
                                    par[:, B_A:B_A + 4 * RNN_TILES].rearrange("p (g f) -> p g f", f=RNN_TILES)[:, :, ds(it, 1)]).then_inc(s_gbias, 1)

                def cut_x(it):
                    dve.tensor_copy(xc_hi[:], xc[:]).then_inc(s_hi, 1)
                    dve.wait_ge(s_hi, it + 1)
                    dve.tensor_tensor(xc_lo[:], xc[:], xc_hi[:].bitcast(F32), ALU.subtract).then_inc(s_lo, 1)

                def cut_gates(it):
                    dve.wait_ge(s_gw, it * 64 + 64)
                    dve.tensor_copy(gate_hi[:], gate_raw[:]).then_inc(s_gwhi, 1)
                    dve.wait_ge(s_gwhi, it + 1)
                    dve.tensor_tensor(gate_lo[:], gate_raw[:], gate_hi[:].bitcast(F32), ALU.subtract).then_inc(s_gwlo, 1)

                convolve(0, 0)
                cut_x(0)
                cut_gates(0)
                gate_biases(0)

                def body(it, last):
                    base = it * DVE_RNN + 4
                    for u in range(HEADS + 5):
                        if u < HEADS:
                            s, h, n = u % 2, u % 8, (u // 8) % 2
                            dve.wait_ge(s_sc, it * HEADS + u + 1)
                            dve.reduce_max(row_max[n][:, h:h + 1], S_cols(s, P, 6 * P), AX_X).then_inc(s_mx, 1)
                            dve.wait_ge(s_mx, it * HEADS + u + 2)
                            dve.tensor_scalar(neg_max[n][:, h:h + 1], row_max[n][:, h:h + 1], -SCALE, neg_sink[:, h:h + 1], ALU.mult, ALU.min).then_inc(s_nm, 1)
                            if u % 4 == 3:
                                kv = h // 4
                                dve.wait_ge(s_nm, it * HEADS + u + 1)
                                dve.tensor_tensor(sink_in[n][:, kv * 4:kv * 4 + 4], sink[:, kv * 4:kv * 4 + 4], neg_max[n][:, kv * 4:kv * 4 + 4], ALU.add).then_inc(s_sin, 1)
                        if 1 <= u <= HEADS:
                            w = u - 1
                            G = w // 4
                            dve.wait_ge(s_pthi, it * HEADS + w + 1)
                            dve.tensor_tensor(pT_lo[G % 2][:, :, w % 4, :], PT.rearrange("p (b q) -> p b q", q=P),
                                              pT_hi[G % 2][:, :, w % 4, :].bitcast(F32), ALU.subtract).then_inc(s_ptlo, 1)
                        if u % 8 == 1 and u < HEADS:
                            n = u // 8
                            cut_v(v_ring[:, (n + 1) % 4], it * SUB + n + 3)
                        if u % 4 == 1 and 5 <= u <= HEADS + 1:
                            G = u // 4 - 1
                            n, kv = (G // 2) % 2, G % 2
                            cols = slice(kv * 4, kv * 4 + 4)
                            dve.wait_ge(s_ses, it * GROUPS + G + 1)
                            dve.tensor_tensor(inv_sum[n][:, cols], sink_exp[n][:, cols], row_sum[n][:, cols], ALU.add).then_inc(s_den, 1)
                            dve.wait_ge(s_den, it * GROUPS + G + 1)
                            dve.reciprocal(inv_sum[n][:, cols], inv_sum[n][:, cols]).then_inc(s_inv, 1)
                        if u >= 7 and (u - 7) % 4 == 0 and (u - 7) // 4 < GROUPS:
                            G = (u - 7) // 4
                            n, kv = (G // 2) % 2, G % 2
                            dve.wait_ge(s_turn, it * GROUPS + G + 2)
                            dve.wait_ge(s_inv, it * GROUPS + G + 1)
                            dve.wait_ge(s_ssq, it * SUB + G // 2 + 1)
                            dve.tensor_tensor(o_scaled[:], psum[:, MISC, :].rearrange("p (h d) -> p h d", h=PER_KV),
                                              inv_sum[n][:, kv * 4:kv * 4 + 4].rearrange("p (h o) -> p h o", o=1).broadcast_to([P, PER_KV, 2 * HEAD]), ALU.mult).then_inc(s_misc, 1)
                            dve.wait_ge(s_misc, event(it, "turn", G) + 2)
                            dve.wait_ge(s_out, it * SUB + G // 2 + 1)
                            dve.tensor_tensor(o_tok[:, kv * 256:(kv + 1) * 256].rearrange("p (h d) -> p h d", h=PER_KV),
                                              o_scaled[:, :, 0:HEAD], o_scaled[:, :, HEAD:2 * HEAD], ALU.add).then_inc(s_tok, 1)
                            if kv == 1:
                                dve.wait_ge(s_tok, it * GROUPS + G + 1)
                                dve.wait_ge(s_msq, it * SUB + G // 2 + 1)
                                dve.tensor_tensor_reduce(o_scaled[:].rearrange("p h d -> p (h d)"), o_tok[:], o_tok[:], 1.0, 0.0, ALU.mult, ALU.add,
                                                         o_ssq[:]).then_inc(s_ssq, 1)
                                dve.wait_ge(s_ssq, it * SUB + G // 2 + 2)
                                dve.tensor_scalar(keep["msq_attn"][:, ds(it * SUB + G // 2, 1)], o_ssq[:], 1.0 / D_ATTN, EPS, ALU.mult, ALU.add).then_inc(s_msq, 1)
                        if u in (8, 11):
                            d = u // 11
                            dve.wait_ge(s_sq, it * 2 + d + 1)
                            dve.wait_ge(s_a, it * 2 + d + 1)
                            dve.scalar_tensor_tensor(th[d][:], g_r[d][:, 0:W], 1.0, th[d][:], ALU.add, ALU.mult).then_inc(s_v, 1)
                        if u in (9, 12):
                            d = u // 12
                            dve.wait_ge(s_v, base + 1 + 4 * d)
                            dve.wait_ge(s_xi, it * 2 + d + 1)
                            dve.tensor_tensor(th[d][:], th[d][:], g_i[d][:], ALU.mult).then_inc(s_v, 1)
                        if u in (10, 13):
                            d = u // 13
                            dve.wait_ge(s_v, base + 2 + 4 * d)
                            step = 1 if d == 0 else -1

                            def seq(t, t0, n):
                                return t[:, t0:t0 + n] if step == 1 else t[:, t0:t0 + n][:, ::-1]

                            end = g_i[d][:, L - 1:L] if d == 0 else g_i[d][:, 0:1]
                            dve.tensor_tensor_scan(seq(g_i[d], 0, L), seq(g_r[d], 0, L), seq(th[d], 0, L), 0.0, ALU.mult, ALU.add).then_inc(s_v, 1)
                            dve.wait_ge(s_v, base + 3 + 4 * d)
                            dve.tensor_tensor_scan(seq(g_i[d], LAT, S), seq(g_r[d], LAT, S), seq(th[d], LAT, S), end, ALU.mult, ALU.add).then_inc(s_v, 1)
                        if u == 14:
                            dve.wait_ge(s_v, base + 8)
                            dve.tensor_tensor(g_i[0][:, LAT:W], g_i[0][:, LAT:W], g_i[1][:, LAT:W], ALU.add).then_inc(s_v, 1)
                        if u == 15:
                            dve.wait_ge(s_v, base + 9)
                            dve.wait_ge(s_gelu, it + 1)
                            dve.tensor_tensor(g_i[0][:, LAT:W], g_i[0][:, LAT:W], gel[:], ALU.mult).then_inc(s_y, 1)
                        if u == 22 and not last:
                            convolve(it + 1, base + 9)
                        if u == 25 and not last:
                            cut_x(it + 1)
                        if u == 28 and not last:
                            cut_gates(it + 1)
                            gate_biases(it + 1)

                rounds(dve, body)
                dve.wait_ge(s_msq, NB + 1)


def output_projection(k, a, x1, rstd2, keep, scratch):
    nc, psum = k.nc, k.psum
    with ExitStack() as ctx:
        def sb(name, shape, dt=F32):
            return ctx.enter_context(nc.sbuf_tensor(name, shape, dt))

        w_raw = [sb(f"wout_raw{i}", [P, D]) for i in range(2)]
        w_hi, w_lo = sb("wout_hi", [P, KD, D], F32R), sb("wout_lo", [P, KD, D], F32R)
        gain_rows, gain = sb("gain_rows", [KD, P]), sb("gain_cols", [P, KD])
        mix = [sb(f"mix{i}", [P, KD, P]) for i in range(2)]
        mix_hi = [sb(f"mix_hi{i}", [P, KD, P], F32R) for i in range(2)]
        mix_lo = [sb(f"mix_lo{i}", [P, KD, P], F32R) for i in range(2)]
        square, square_sum = sb("rnn_square", [P, RNN_TILES, P]), sb("rnn_square_sum", [P, P])
        x_in = [sb(f"x_in{i}", [P, D]) for i in range(2)]
        part = [sb(f"rnn_part{i}", [P, CH]) for i in range(2)]
        g1 = sb("g1_wide", [P, D])
        junk = [sb(f"x1_square_junk{i}", [P, D], BF16) for i in range(2)]
        ones, eps_col = sb("ones_col", [P, 1]), sb("eps_col4", [P, 1])
        rstd_a, rstd_r, ssq2 = sb("rstd_attn", [P, NB]), [sb(f"rstd_rnn{i}", [P, 1]) for i in range(2)], sb("ssq2", [P, NB])

        s_gain = k.sem("gains_landed")
        s_gainT = k.sem("gains_transposed")
        s_gainc = k.sem("gain_cols_ready")
        s_const = k.sem("out_constants_ready")
        s_w = [k.sem(f"wout_landed{i}") for i in range(2)]
        s_ws = k.sem("wout_scaled")
        s_whi = k.sem("wout_hi_ready")
        s_wlo = k.sem("wout_lo_ready")
        s_mix = [k.sem(f"mix_landed{i}") for i in range(2)]
        s_x = [k.sem(f"x_in_landed{i}") for i in range(2)]
        s_g1 = k.sem("g1_landed")
        s_hi = k.sem("mix_hi_ready")
        s_lo = k.sem("mix_lo_ready")
        s_sq = k.sem("rnn_squared")
        s_sqs = k.sem("rnn_squares_summed")
        s_ss = k.sem("rnn_sumsq_ready")
        s_std = k.sem("rnn_std_ready")
        s_rstd = k.sem("rnn_rstd_ready")
        s_rstda = k.sem("attn_rstd_ready")
        s_acc = k.sem("out_accumulated")
        s_part = k.sem("rnn_part_ready")
        s_mid = k.sem("parts_joined")
        s_gated = k.sem("mixer_gated")
        s_x1 = k.sem("x1_ready")
        s_ss2 = k.sem("x1_squared")
        s_x1st = k.sem("x1_stored")

        SS_BANK = 4

        with nc.Block() as block:

            @block.sync
            def _(sp):
                sp.dma_start(gain_rows[0:RNN_TILES, :], a["gn_rnn"].rearrange("a (k p) -> (a k) p", p=P)).then_inc(s_gain, 16)
                sp.dma_start(gain_rows[RNN_TILES:KD, :], a["gn_attn"].rearrange("a (k p) -> (a k) p", p=P)).then_inc(s_gain, 16)

                def load(n, s):
                    sp.wait_ge(s_lo, n + 1)
                    sp.wait_ge(s_sq, n + 1)
                    sp.dma_start(mix[s][:], scratch["mix"][:, ds(n * P, P)].rearrange("(k p) t -> p k t", p=P)).then_inc(s_mix[s], 16)
                    sp.wait_ge(s_x1, n + 1)
                    sp.dma_start(x_in[s][:], a["x"][0, ds(n * P, P), :]).then_inc(s_x[s], 16)

                def store(n):
                    sp.wait_ge(s_x1, n + 3)
                    sp.dma_start(scratch["x1"][ds(n * P, P), :], x1[:, ds(n, 1), :].rearrange("p o d -> p (o d)")).then_inc(s_x1st, 16)

                for kt in range(KD):
                    sp.wait_ge(s_wlo, kt + 1)
                    sp.dma_start(w_raw[kt % 2][:], a["w_out"][0, kt * P:(kt + 1) * P, :]).then_inc(s_w[kt % 2], 16)
                    if kt == 1:
                        load(0, 0)
                        load(1, 1)
                        sp.dma_start(g1[:], scratch["mod"][0:1, 2 * D:3 * D].broadcast_to([P, D])).then_inc(s_g1, 16)
                with sp.Fori(0, NB // 2 - 1) as i:
                    for s in range(2):
                        load(i * 2 + s + 2, s)
                        store(i * 2 + s)
                store(NB - 2)
                store(NB - 1)
                sp.wait_ge(s_x1st, 16 * NB)

            @block.gpsimd
            def _(pool):
                nc.gpsimd.memset(ones[:], 1.0).then_inc(s_const, 1)
                nc.gpsimd.memset(eps_col[:], EPS).then_inc(s_const, 1)

                def cut(n, s):
                    pool.wait_ge(s_hi, n + 1)
                    nc.gpsimd.tensor_tensor(mix_lo[s][:], mix[s][:], mix_hi[s][:].bitcast(F32), ALU.subtract).then_inc(s_lo, 1)

                def residual(n, s, turn):
                    pool.wait_ge(s_x[s], turn * 16 + 16)
                    pool.wait_ge(s_gated, n + 1)
                    tile = x1[:, ds(n, 1), :].rearrange("p o d -> p (o d)")
                    nc.gpsimd.tensor_tensor(tile, tile, x_in[s][:], ALU.add).then_inc(s_x1, 1)

                cut(0, 0)
                with pool.Fori(0, NB // 2 - 1) as i:
                    cut(i * 2 + 1, 1)
                    residual(i * 2, 0, i)
                    cut(i * 2 + 2, 0)
                    residual(i * 2 + 1, 1, i)
                cut(NB - 1, 1)
                residual(NB - 2, 0, NB // 2 - 1)
                residual(NB - 1, 1, NB // 2 - 1)

            @block.scalar
            def _(act):
                act.sem_inc(s_wlo, 2)
                act.sem_inc(s_lo, 2)
                act.sem_inc(s_sq, 2)
                act.sem_inc(s_x1, 2)
                act.sem_inc(s_acc, 4)
                act.sem_inc(s_mid, 2)
                act.sem_inc(s_sqs, 1)
                act.sem_inc(s_ss, 1)
                act.wait_ge(s_const, 2)
                act.activation(rstd_a[:], keep["msq_attn"][:], ACT.Sqrt).then_inc(s_rstda, 1)

                def cut(n, s, turn):
                    act.wait_ge(s_mix[s], turn * 16 + 16)
                    act.wait_ge(s_acc, n * 2 + 2)
                    act.activation(mix_hi[s][:], mix[s][:], ACT.Copy).then_inc(s_hi, 1)
                    act.wait_ge(s_sqs, n + 1)
                    act.activation(square[:], mix[s][:, 0:RNN_TILES, :], ACT.Square).then_inc(s_sq, 1)

                def finish(n, s):
                    act.wait_ge(s_ss, n + 2)
                    act.activation(rstd_r[s][:], psum[:, SS_BANK + s, 0:1], ACT.Sqrt, bias=eps_col[:], scale=1.0 / D_RNN).then_inc(s_std, 1)
                    act.wait_ge(s_rstd, n + 1)
                    for half in range(2):
                        act.wait_ge(s_acc, n * 2 + half + 5)
                        act.activation(part[half][:], psum[:, 2 * half, :], ACT.Copy, scale=rstd_r[s][:]).then_inc(s_part, 1)

                def square_x1(n, s):
                    act.wait_ge(s_x1, n + 3)
                    act.activation(junk[s][:], x1[:, ds(n, 1), :].rearrange("p o d -> p (o d)"), ACT.Square, accum_out=ssq2[:, ds(n, 1)]).then_inc(s_ss2, 1)

                cut(0, 0, 0)
                act.wait_ge(s_gainc, 1)
                for kt in range(KD):
                    act.wait_ge(s_w[kt % 2], (kt // 2) * 16 + 16)
                    act.activation(w_raw[kt % 2][:], w_raw[kt % 2][:], ACT.Copy, scale=gain[:, kt:kt + 1]).then_inc(s_ws, 1)
                    act.wait_ge(s_ws, kt + 1)
                    act.activation(w_hi[:, kt, :], w_raw[kt % 2][:], ACT.Copy).then_inc(s_whi, 1)
                cut(1, 1, 0)
                finish(0, 0)
                with act.Fori(0, NB // 2 - 1) as i:
                    cut(i * 2 + 2, 0, i + 1)
                    finish(i * 2 + 1, 1)
                    square_x1(i * 2, 0)
                    cut(i * 2 + 3, 1, i + 1)
                    finish(i * 2 + 2, 0)
                    square_x1(i * 2 + 1, 1)
                finish(NB - 1, 1)
                square_x1(NB - 2, 0)
                square_x1(NB - 1, 1)
                act.wait_ge(s_ss2, NB)
                act.activation(ssq2[:], ssq2[:], ACT.Sqrt, bias=eps_col[:], scale=1.0 / D).then_inc(s_ss2, 1)

            @block.tensor
            def _(pe):
                pe.wait_ge(s_gain, 32)
                pe.transpose(psum[:, SS_BANK, 0:KD], gain_rows[:], keep["ident"][0:KD, 0:KD]).then_inc(s_gainT, 1)

                def tile(n, s, first):
                    pe.wait_ge(s_sqs, n + 2)
                    if first:
                        pe.wait_ge(s_gainc, 1)
                        pe.wait_ge(s_const, 2)
                    pe.matmul(psum[:, SS_BANK + s, 0:1], square_sum[:], ones[:], start=True, stop=True).then_inc(s_ss, 1)
                    pe.wait_ge(s_lo, n + 3)
                    for half in range(2):
                        pe.wait_ge(s_mid, n * 2 + half + 1)
                        for group in range(2):
                            for kt in range(group * RNN_TILES, (group + 1) * RNN_TILES):
                                if first and half == 0:
                                    pe.wait_ge(s_wlo, kt + 3)
                                at, end = kt == group * RNN_TILES, kt == (group + 1) * RNN_TILES - 1
                                cols = slice(half * CH, (half + 1) * CH)
                                pe.matmul(psum[:, 2 * half + group, :], mix_hi[s][:, kt, :], w_hi[:, kt, cols], start=at, stop=False)
                                pe.matmul(psum[:, 2 * half + group, :], mix_hi[s][:, kt, :], w_lo[:, kt, cols], start=False, stop=False)
                                mm = pe.matmul(psum[:, 2 * half + group, :], mix_lo[s][:, kt, :], w_hi[:, kt, cols], start=False, stop=end)
                        mm.then_inc(s_acc, 1)

                tile(0, 0, True)
                with pe.Fori(0, NB // 2 - 1) as i:
                    tile(i * 2 + 1, 1, False)
                    tile(i * 2 + 2, 0, False)
                tile(NB - 1, 1, False)

            @block.vector
            def _(dve):
                dve.wait_ge(s_gainT, 1)
                dve.tensor_copy(gain[:], psum[:, SS_BANK, 0:KD]).then_inc(s_gainc, 1)
                dve.wait_ge(s_rstda, 1)
                dve.reciprocal(rstd_a[:], rstd_a[:]).then_inc(s_rstda, 1)
                dve.wait_ge(s_rstda, 2)

                def sum_squares(n):
                    dve.wait_ge(s_sq, n + 3)
                    dve.wait_ge(s_ss, n + 1)
                    dve.tensor_reduce(square_sum[:], square[:].rearrange("p f t -> p t f"), AX_X, ALU.add).then_inc(s_sqs, 1)

                def finish(n, s):
                    dve.wait_ge(s_std, n + 1)
                    dve.reciprocal(rstd_r[s][:], rstd_r[s][:]).then_inc(s_rstd, 1)
                    for half in range(2):
                        dve.wait_ge(s_part, n * 2 + half + 1)
                        dve.scalar_tensor_tensor(x1[:, ds(n, 1), half * CH:(half + 1) * CH].rearrange("p o d -> p (o d)"), psum[:, 2 * half + 1, :],
                                                 rstd_a[:, ds(n, 1)], part[half][:], ALU.mult, ALU.add).then_inc(s_mid, 1)
                    dve.wait_ge(s_mid, n * 2 + 4)
                    tile = x1[:, ds(n, 1), :].rearrange("p o d -> p (o d)")
                    dve.tensor_tensor(tile, tile, g1[:], ALU.mult).then_inc(s_gated, 1)

                sum_squares(0)
                for kt in range(KD):
                    dve.wait_ge(s_whi, kt + 1)
                    dve.tensor_tensor(w_lo[:, kt, :], w_raw[kt % 2][:], w_hi[:, kt, :].bitcast(F32), ALU.subtract).then_inc(s_wlo, 1)
                sum_squares(1)
                dve.wait_ge(s_g1, 16)
                finish(0, 0)
                with dve.Fori(0, NB // 2 - 1) as i:
                    sum_squares(i * 2 + 2)
                    finish(i * 2 + 1, 1)
                    sum_squares(i * 2 + 3)
                    finish(i * 2 + 2, 0)
                finish(NB - 1, 1)
                dve.wait_ge(s_ss2, NB + 1)
                dve.reciprocal(rstd2[:], ssq2[:])


def modulate_x1(k, x1, rstd2, h2T_hi, h2T_lo, keep):
    nc, psum = k.nc, k.psum
    ident, aff2 = keep["ident"], keep["aff2"]
    QUADS = NB // 4
    with ExitStack() as ctx:
        xn = [ctx.enter_context(nc.sbuf_tensor(f"x1_norm{i}", [P, 4, 2 * P], F32)) for i in range(2)]
        t32 = [ctx.enter_context(nc.sbuf_tensor(f"t2_{i}", [P, CH], F32)) for i in range(2)]
        s_xn = k.sem("x1_normalised")
        s_tp = k.sem("x1_transposed")
        s_t32 = k.sem("x1_modulated")
        s_hi = k.sem("h2T_hi_ready")
        s_lo = k.sem("h2T_lo_ready")

        with nc.Block() as block:

            @block.gpsimd
            def _(pool):
                with pool.Fori(0, QUADS) as q:
                    for pair in range(KD // 2):
                        pool.wait_ge(s_tp, q * KD + pair * 2 + 2)
                        nc.gpsimd.tensor_tensor(xn[pair % 2][:], x1[:, ds(q * 4, 4), pair * 2 * P:(pair + 1) * 2 * P],
                                                rstd2[:, ds(q * 4, 4)].rearrange("p (n o) -> p n o", o=1).broadcast_to([P, 4, 2 * P]), ALU.mult).then_inc(s_xn, 1)

            @block.tensor
            def _(pe):
                with pe.Fori(0, QUADS) as q:
                    for kt in range(KD):
                        pe.wait_ge(s_xn, q * (KD // 2) + kt // 2 + 1)
                        pe.wait_ge(s_t32, q * KD + kt + 1)
                        for j in range(4):
                            tp = pe.transpose(psum[:, kt, j * P:(j + 1) * P], xn[kt // 2 % 2][:, j, (kt % 2) * P:(kt % 2 + 1) * P], ident[:])
                        tp.then_inc(s_tp, 1)

            @block.scalar
            def _(act):
                act.sem_inc(s_t32, KD)
                act.sem_inc(s_tp, 4)
                act.sem_inc(s_lo, 2)
                with act.Fori(0, QUADS) as q:
                    for kt in range(KD):
                        act.wait_ge(s_tp, q * KD + kt + 5)
                        act.wait_ge(s_lo, q * KD + kt + 1)
                        act.activation(t32[kt % 2][:], psum[:, kt, :], ACT.Identity, bias=aff2[:, 1, kt:kt + 1], scale=aff2[:, 0, kt:kt + 1]).then_inc(s_t32, 1)

            @block.vector
            def _(dve):
                with dve.Fori(0, QUADS) as q:
                    for kt in range(KD):
                        dve.wait_ge(s_t32, q * KD + kt + 1 + KD)
                        hi = h2T_hi[:, kt, ds(q * CH, CH)]
                        dve.tensor_copy(hi, t32[kt % 2][:]).then_inc(s_hi, 1)
                        dve.wait_ge(s_hi, q * KD + kt + 1)
                        dve.tensor_tensor(h2T_lo[:, kt, ds(q * CH, CH)], t32[kt % 2][:], hi.bitcast(F32), ALU.subtract).then_inc(s_lo, 1)


def up_projection(k, a, h2T_hi, h2T_lo, keep, scratch):
    nc, psum = k.nc, k.psum
    with ExitStack() as ctx:
        def sb(name, shape, dt=F32):
            return ctx.enter_context(nc.sbuf_tensor(name, shape, dt))

        w_raw = [sb(f"wup_raw{g}", [P, KD, P]) for g in range(2)]
        w_hi = [sb(f"wup_hi{g}", [P, KD, P], F32R) for g in range(2)]
        w_lo = [sb(f"wup_lo{g}", [P, KD, P], F32R) for g in range(2)]
        u_pad = [sb(f"u_pad{g}", [P, S + 2]) for g in range(2)]
        acc = [sb(f"conv_acc{g}", [P, S]) for g in range(2)]
        act_out = [sb(f"act_out{i}", [P, S]) for i in range(2)]
        par_rows = [sb(f"conv_rows{i}", [4 * FT, P]) for i in range(2)]
        par = sb("conv_cols", [P, 8 * FT])

        s_par = k.sem("conv_params_landed")
        s_parT = k.sem("conv_params_transposed")
        s_parc = k.sem("conv_cols_ready")
        s_pad = k.sem("pad_columns_ready")
        s_w = [k.sem(f"wup_landed{g}") for g in range(2)]
        s_whi = k.sem("wup_hi_ready")
        s_wlo = k.sem("wup_lo_ready")
        s_mm = k.sem("up_accumulated")
        s_evac = k.sem("up_evacuated")
        s_tap = k.sem("conv_tap_added")
        s_conv = k.sem("conv_ready")
        s_silu = k.sem("gate_silu_ready")
        s_prod = k.sem("act_ready")
        s_stored = [k.sem(f"act_stored{i}") for i in range(2)]

        with nc.Block() as block:

            @block.sync
            def _(sp):
                sp.sem_inc(s_stored[0], 16)
                sp.sem_inc(s_stored[1], 16)

                def load(j, g):
                    sp.wait_ge(s_wlo, j * 2 + g + 1)
                    sp.dma_start(w_raw[g][:], a["w_up"][0, :, ds(j * P + g * D_FF, P)].rearrange("(k p) n -> p k n", p=P)).then_inc(s_w[g], 16)

                def store(j, i):
                    sp.wait_ge(s_prod, j + 2)
                    sp.dma_start(scratch["act"][:, :, ds(j, 1), :].rearrange("n p o t -> p (n o) t"),
                                 act_out[i][:].rearrange("p (n t) -> p n t", t=P)).then_inc(s_stored[i], 16)

                load(0, 0)
                load(0, 1)
                for i in range(2):
                    for half in range(2):
                        src = a["ffn_conv_b"] if (i, half) == (1, 1) else a["ffn_conv_w"][:, 2 * i + half, :]
                        sp.dma_start(par_rows[i][half * 2 * FT:(half + 1) * 2 * FT, :], src.rearrange("a (t p) -> (a t) p", p=P)).then_inc(s_par, 16)
                with sp.Fori(0, FT // 2 - 1) as i:
                    for m in range(2):
                        load(i * 2 + m + 1, 0)
                        load(i * 2 + m + 1, 1)
                        store(i * 2 + m, m)
                load(FT - 1, 0)
                load(FT - 1, 1)
                store(FT - 2, 0)
                store(FT - 1, 1)
                for i in range(2):
                    sp.wait_ge(s_stored[i], 16 + 16 * (FT // 2))

            @block.gpsimd
            def _(pool):
                with pool.Fori(0, FT) as j:
                    for g in range(2):
                        pool.wait_ge(s_whi, j * 2 + g + 1)
                        nc.gpsimd.tensor_tensor(w_lo[g][:], w_raw[g][:], w_hi[g][:].bitcast(F32), ALU.subtract).then_inc(s_wlo, 1)

            @block.scalar
            def _(act):
                act.sem_inc(s_wlo, 2)
                act.sem_inc(s_evac, 8)
                act.sem_inc(s_conv, 2)
                act.sem_inc(s_prod, 1)

                def cut(j, g):
                    act.wait_ge(s_w[g], j * 16 + 16)
                    act.activation(w_hi[g][:], w_raw[g][:], ACT.Copy).then_inc(s_whi, 1)

                def evacuate(j, g, c):
                    act.wait_ge(s_mm, j * 8 + g * 4 + c + 1)
                    if c == 0:
                        act.wait_ge(s_conv, j * 2 + g + 1)
                    act.activation(u_pad[g][:, 1 + c * CH:1 + (c + 1) * CH], psum[:, 4 * g + c, :], ACT.Copy).then_inc(s_evac, 1)

                def silu(j):
                    act.wait_ge(s_conv, j * 2 + 3)
                    act.activation(acc[0][:], acc[0][:], ACT.Silu).then_inc(s_silu, 1)

                def channels(j, last):
                    cut(j, 1)
                    for c in range(NCH):
                        evacuate(j, 0, c)
                    if not last:
                        cut(j + 1, 0)
                    evacuate(j, 1, 0)
                    evacuate(j, 1, 1)
                    silu(j)
                    evacuate(j, 1, 2)
                    evacuate(j, 1, 3)

                cut(0, 0)
                with act.Fori(0, FT - 1) as j:
                    channels(j, False)
                channels(FT - 1, True)

            @block.tensor
            def _(pe):
                pe.wait_ge(s_par, 64)
                for i in range(2):
                    tp = pe.transpose(psum[:, 7, i * 4 * FT:(i + 1) * 4 * FT], par_rows[i][:], keep["ident"][0:4 * FT, 0:4 * FT])
                tp.then_inc(s_parT, 1)
                pe.wait_ge(s_parc, 1)
                with pe.Fori(0, FT) as j:
                    for g in range(2):
                        pe.wait_ge(s_wlo, j * 2 + g + 3)
                        for c in range(NCH):
                            pe.wait_ge(s_evac, j * 8 + g * 4 + c + 1)
                            bank, cols = psum[:, 4 * g + c, :], slice(c * CH, (c + 1) * CH)
                            for kt in range(KD):
                                pe.matmul(bank, w_hi[g][:, kt, :], h2T_hi[:, kt, cols], start=(kt == 0), stop=False)
                                pe.matmul(bank, w_hi[g][:, kt, :], h2T_lo[:, kt, cols], start=False, stop=False)
                                mm = pe.matmul(bank, w_lo[g][:, kt, :], h2T_hi[:, kt, cols], start=False, stop=(kt == KD - 1))
                            mm.then_inc(s_mm, 1)

            @block.vector
            def _(dve):
                for g in range(2):
                    for at in (0, S + 1):
                        dve.memset(u_pad[g][:, at:at + 1], 0.0).then_inc(s_pad, 1)
                dve.wait_ge(s_parT, 1)
                dve.tensor_copy(par[:], psum[:, 7, 0:8 * FT]).then_inc(s_parc, 1)
                dve.wait_ge(s_parc, 1)
                dve.wait_ge(s_pad, 4)

                def col(which, j, g):
                    return par[:, ds(j + which * 2 * FT + g * FT, 1)]

                def convolve(j, g):
                    dve.wait_ge(s_evac, j * 8 + g * 4 + 12)
                    dve.wait_ge(s_prod, j + 1)
                    dve.tensor_scalar(acc[g][:], u_pad[g][:, 1:S + 1], col(1, j, g), col(3, j, g), ALU.mult, ALU.add).then_inc(s_tap, 1)
                    dve.wait_ge(s_tap, j * 4 + g * 2 + 1)
                    dve.scalar_tensor_tensor(acc[g][:], u_pad[g][:, 0:S], col(0, j, g), acc[g][:], ALU.mult, ALU.add).then_inc(s_tap, 1)
                    dve.wait_ge(s_tap, j * 4 + g * 2 + 2)
                    dve.scalar_tensor_tensor(acc[g][:], u_pad[g][:, 2:S + 2], col(2, j, g), acc[g][:], ALU.mult, ALU.add).then_inc(s_conv, 1)

                with dve.Fori(0, FT // 2) as i:
                    for m in range(2):
                        j = i * 2 + m
                        convolve(j, 0)
                        convolve(j, 1)
                        dve.wait_ge(s_silu, j + 1)
                        dve.wait_ge(s_conv, j * 2 + 4)
                        dve.wait_ge(s_stored[m], i * 16 + 16)
                        dve.tensor_tensor(act_out[m][:], acc[0][:], acc[1][:], ALU.mult).then_inc(s_prod, 1)


def down_projection(k, a, out, scratch):
    nc, psum = k.nc, k.psum
    with ExitStack() as ctx:
        def sb(name, shape, dt=F32):
            return ctx.enter_context(nc.sbuf_tensor(name, shape, dt))

        w_raw = [sb(f"wdown_raw{i}", [P, CH]) for i in range(2)]
        w_hi, w_lo = sb("wdown_hi", [P, FT, CH], F32R), sb("wdown_lo", [P, FT, CH], F32R)
        a_raw = [sb(f"act_raw{i}", [P, FT, P]) for i in range(2)]
        a_hi = [sb(f"act_hi{i}", [P, FT, P], F32R) for i in range(2)]
        a_lo = [sb(f"act_lo{i}", [P, FT, P], F32R) for i in range(2)]
        x2_left = sb("x2_left", [P, NB, CH])
        x2_right = [sb(f"x2_right{i}", [P, CH]) for i in range(2)]
        gated = sb("gated", [P, CH])
        g2, final_g = sb("g2_wide", [P, D]), sb("final_g_wide", [P, D])
        junk = [sb(f"x2_junk{i}", [P, CH], BF16) for i in range(2)]
        ssq = [sb(f"x2_ssq{half}", [P, NB]) for half in range(2)]
        rstd, eps_col = [sb(f"x2_rstd{i}", [P, 1]) for i in range(2)], sb("eps_col7", [P, 1])

        s_wide = k.sem("wide_vectors_landed")
        s_left = k.sem("x1_left_landed")
        s_right = [k.sem(f"x1_right_landed{i}") for i in range(2)]
        s_w = [k.sem(f"wdown_landed{i}") for i in range(2)]
        s_whi = k.sem("wdown_hi_ready")
        s_wlo = k.sem("wdown_lo_ready")
        s_a = [k.sem(f"act_landed{i}") for i in range(2)]
        s_hi = k.sem("act_hi_ready")
        s_lo = k.sem("act_lo_ready")
        s_mm = k.sem("down_accumulated")
        s_gated = k.sem("ffn_gated")
        s_x2 = k.sem("x2_ready")
        s_sq = k.sem("x2_squared")
        s_tot = k.sem("x2_sumsq_ready")
        s_std = k.sem("x2_std_ready")
        s_rstd = k.sem("x2_rstd_ready")
        s_out = k.sem("out_ready")
        s_stored = [k.sem(f"out_stored{i}") for i in range(2)]

        with nc.Block() as block:

            @block.sync
            def _(sp):
                sp.sem_inc(s_stored[0], 32)
                sp.sem_inc(s_stored[1], 32)

                def load(u, n, s):
                    sp.wait_ge(s_lo, u + 1)
                    sp.dma_start(a_raw[s][:], scratch["act"][ds(n, 1)].rearrange("o p k t -> p (o k) t")).then_inc(s_a[s], 16)

                def weights(half, first, last):
                    for kt in range(first, last):
                        sp.wait_ge(s_wlo, half * FT + kt + 1)
                        sp.dma_start(w_raw[kt % 2][:], a["w_down"][0, kt * P:(kt + 1) * P, half * CH:(half + 1) * CH]).then_inc(s_w[kt % 2], 16)

                load(0, 0, 0)
                weights(0, 0, 2)
                load(1, 1, 1)
                weights(0, 2, FT)
                for half, t in ((0, g2), (1, final_g)):
                    src = scratch["mod"][0:1, 5 * D:6 * D] if t is g2 else a["final_g"].rearrange("(o d) -> o d", o=1)
                    sp.dma_start(t[:], src.broadcast_to([P, D])).then_inc(s_wide, 16)
                sp.dma_start(x2_left[:], scratch["x1"][:, 0:CH].rearrange("(n p) d -> p n d", p=P)).then_inc(s_left, 16)
                with sp.Fori(0, NB // 2 - 1) as i:
                    for s in range(2):
                        load(i * 2 + s + 2, i * 2 + s + 2, s)
                for s in range(2):
                    load(NB + s, s, s)
                    sp.dma_start(x2_right[s][:], scratch["x1"][s * P:(s + 1) * P, CH:D]).then_inc(s_right[s], 16)
                weights(1, 0, FT)

                def store(n, s):
                    sp.wait_ge(s_out, n * 2 + 2)
                    sp.dma_start(out[0, ds(n * P, P), 0:CH], x2_left[:, ds(n, 1), :].rearrange("p o d -> p (o d)")).then_inc(s_stored[s], 16)
                    sp.dma_start(out[0, ds(n * P, P), CH:D], x2_right[s][:]).then_inc(s_stored[s], 16)

                with sp.Fori(0, NB // 2 - 1) as i:
                    for s in range(2):
                        load(i * 2 + s + NB + 2, i * 2 + s + 2, s)
                        store(i * 2 + s, s)
                        sp.wait_ge(s_stored[s], i * 32 + 64)
                        sp.dma_start(x2_right[s][:], scratch["x1"][ds(i * 2 * P + (s + 2) * P, P), CH:D]).then_inc(s_right[s], 16)
                for s in range(2):
                    store(NB - 2 + s, s)
                for s in range(2):
                    sp.wait_ge(s_stored[s], 32 + 32 * (NB // 2))

            @block.gpsimd
            def _(pool):
                nc.gpsimd.memset(eps_col[:], EPS).then_inc(s_rstd, 1)

            @block.scalar
            def _(act):
                act.sem_inc(s_lo, 2)
                act.sem_inc(s_wlo, 2)
                act.sem_inc(s_mm, 2)
                act.wait_ge(s_rstd, 1)

                def cut(u, s, turn):
                    act.wait_ge(s_a[s], turn * 16 + 16)
                    act.wait_ge(s_mm, u + 1)
                    act.activation(a_hi[s][:], a_raw[s][:], ACT.Copy).then_inc(s_hi, 1)

                def cut_weights(half):
                    if half:
                        act.wait_ge(s_mm, NB + 2)
                    for kt in range(FT):
                        act.wait_ge(s_w[kt % 2], (half * FT + kt) // 2 * 16 + 16)
                        act.activation(w_hi[:, kt, :], w_raw[kt % 2][:], ACT.Copy).then_inc(s_whi, 1)

                def square_left(n, s):
                    act.wait_ge(s_x2, n + 2)
                    act.activation(junk[s][:], x2_left[:, ds(n, 1), :].rearrange("p o d -> p (o d)"), ACT.Square, accum_out=ssq[0][:, ds(n, 1)]).then_inc(s_sq, 1)

                def square_right(n, s):
                    act.wait_ge(s_x2, n + NB + 2)
                    act.activation(junk[s][:], x2_right[s][:], ACT.Square, accum_out=ssq[1][:, ds(n, 1)]).then_inc(s_sq, 1)
                    act.wait_ge(s_tot, n + 1)
                    act.activation(rstd[s][:], rstd[s][:], ACT.Sqrt, bias=eps_col[:], scale=1.0 / D).then_inc(s_std, 1)

                cut(0, 0, 0)
                cut_weights(0)
                cut(1, 1, 0)
                with act.Fori(0, NB // 2 - 1) as i:
                    for s in range(2):
                        cut(i * 2 + s + 2, s, i + 1)
                        square_left(i * 2 + s, s)
                cut(NB, 0, NB // 2)
                square_left(NB - 2, 0)
                cut_weights(1)
                cut(NB + 1, 1, NB // 2)
                square_left(NB - 1, 1)
                with act.Fori(0, NB // 2 - 1) as i:
                    for s in range(2):
                        cut(i * 2 + s + NB + 2, s, i + NB // 2 + 1)
                        square_right(i * 2 + s, s)
                square_right(NB - 2, 0)
                square_right(NB - 1, 1)

            @block.tensor
            def _(pe):
                def tile(u, s, bank, first):
                    pe.wait_ge(s_gated, u + 1)
                    pe.wait_ge(s_lo, u + 3)
                    for kt in range(FT):
                        if first:
                            pe.wait_ge(s_wlo, (u // NB) * FT + kt + 3)
                        pe.matmul(psum[:, bank, :], a_hi[s][:, kt, :], w_hi[:, kt, :], start=(kt == 0), stop=False)
                        pe.matmul(psum[:, bank, :], a_hi[s][:, kt, :], w_lo[:, kt, :], start=False, stop=False)
                        mm = pe.matmul(psum[:, bank, :], a_lo[s][:, kt, :], w_hi[:, kt, :], start=False, stop=(kt == FT - 1))
                    mm.then_inc(s_mm, 1)

                for half in range(2):
                    tile(half * NB, 0, 0, True)
                    with pe.Fori(half * NB // 2, (half + 1) * NB // 2 - 1) as i:
                        tile(i * 2 + 1, 1, 1, False)
                        tile(i * 2 + 2, 0, 0, False)
                    tile(half * NB + NB - 1, 1, 1, False)

            @block.vector
            def _(dve):
                dve.sem_inc(s_gated, 2)
                dve.sem_inc(s_x2, 1)

                def cut(u, s):
                    dve.wait_ge(s_hi, u + 1)
                    dve.tensor_tensor(a_lo[s][:], a_raw[s][:], a_hi[s][:].bitcast(F32), ALU.subtract).then_inc(s_lo, 1)

                def cut_weights(half):
                    for kt in range(FT):
                        dve.wait_ge(s_whi, half * FT + kt + 1)
                        dve.tensor_tensor(w_lo[:, kt, :], w_raw[kt % 2][:], w_hi[:, kt, :].bitcast(F32), ALU.subtract).then_inc(s_wlo, 1)

                def residual(u, half, bank, x2):
                    dve.wait_ge(s_mm, u + 3)
                    dve.wait_ge(s_x2, u + 1)
                    dve.tensor_tensor(gated[:], psum[:, bank, :], g2[:, half * CH:(half + 1) * CH], ALU.mult).then_inc(s_gated, 1)
                    dve.wait_ge(s_gated, u + 3)
                    dve.tensor_tensor(x2, x2, gated[:], ALU.add).then_inc(s_x2, 1)

                def left(n, s):
                    residual(n, 0, s, x2_left[:, ds(n, 1), :].rearrange("p o d -> p (o d)"))

                def right(n, s, turn):
                    dve.wait_ge(s_right[s], turn * 16 + 16)
                    residual(n + NB, 1, s, x2_right[s][:])

                def finish(n, s):
                    dve.wait_ge(s_sq, n + NB + 1)
                    dve.tensor_tensor(rstd[s][:], ssq[0][:, ds(n, 1)], ssq[1][:, ds(n, 1)], ALU.add).then_inc(s_tot, 1)
                    dve.wait_ge(s_std, n + 1)
                    dve.reciprocal(rstd[s][:], rstd[s][:]).then_inc(s_rstd, 1)
                    dve.wait_ge(s_rstd, n + 2)
                    for tile, cols in ((x2_left[:, ds(n, 1), :].rearrange("p o d -> p (o d)"), slice(0, CH)), (x2_right[s][:], slice(CH, D))):
                        dve.scalar_tensor_tensor(tile, tile, rstd[s][:], final_g[:, cols], ALU.mult, ALU.mult).then_inc(s_out, 1)

                cut(0, 0)
                cut_weights(0)
                cut(1, 1)
                dve.wait_ge(s_wide, 32)
                dve.wait_ge(s_left, 16)
                with dve.Fori(0, NB // 2 - 1) as i:
                    for s in range(2):
                        left(i * 2 + s, s)
                        cut(i * 2 + s + 2, s)
                left(NB - 2, 0)
                cut(NB, 0)
                left(NB - 1, 1)
                cut_weights(1)
                cut(NB + 1, 1)
                with dve.Fori(0, NB // 2 - 1) as i:
                    for s in range(2):
                        right(i * 2 + s, s, i)
                        cut(i * 2 + s + NB + 2, s)
                        finish(i * 2 + s, s)
                for s in range(2):
                    right(NB - 2 + s, s, NB // 2 - 1)
                    finish(NB - 2 + s, s)


def build(nc, a, out):
    ctx = ExitStack()
    with ctx:
        k = Kit(nc, ctx)
        scratch = {n: k.dram(n, s, d) for n, s, d in (
            ("mod", [2, 6 * D], F32), ("xr", [D_RNN, T], F32), ("xg", [D_RNN, S], F32),
            ("qk_hi", [D_ATTN + N_KV * HEAD, T], F32), ("qk_lo", [D_ATTN + N_KV * HEAD, T], F32),
            ("v", [N_KV * HEAD, T], F32), ("mix", [D, S], F32), ("x1", [S, D], F32), ("act", [NB, P, FT, P], F32))}
        keep = {n: k.keep(n, s, F32) for n, s in (
            ("ident", [P, P]), ("aff2", [P, 2, KD]), ("msq_attn", [P, NB]))}
        with ExitStack() as features:
            hT_hi, hT_lo = (features.enter_context(nc.sbuf_tensor(n, [P, KD, T], F32R)) for n in ("hT_hi", "hT_lo"))
            modulation_and_norm(k, a, hT_hi, hT_lo, keep, scratch)
            k.next_phase()
            input_projection(k, a, hT_hi, hT_lo, scratch)
            k.next_phase()
        mixers(k, a, keep, scratch)
        k.next_phase()
        rstd2 = k.keep("rstd2", [P, NB], F32)
        x1_life, h2T_life = ExitStack(), ExitStack()
        x1 = x1_life.enter_context(nc.sbuf_tensor("x1_tiles", [P, NB, D], F32, side="right"))
        output_projection(k, a, x1, rstd2, keep, scratch)
        k.next_phase()
        h2T_hi, h2T_lo = (h2T_life.enter_context(nc.sbuf_tensor(n, [P, KD, S], F32R)) for n in ("h2T_hi", "h2T_lo"))
        modulate_x1(k, x1, rstd2, h2T_hi, h2T_lo, keep)
        k.next_phase()
        x1_life.close()
        up_projection(k, a, h2T_hi, h2T_lo, keep, scratch)
        k.next_phase()
        h2T_life.close()
        down_projection(k, a, out, scratch)


_INS = ["x", "c", "ctx", "c_ctx", "w_mod", "b_mod", "norm1_g", "w_in", "rnn_conv_w", "rnn_conv_b", "lru_w_a", "lru_b_a",
        "lru_w_i", "lru_b_i", "lru_lam", "attn_sink", "gn_rnn", "gn_attn", "w_out", "norm2_g", "w_up", "ffn_conv_w",
        "ffn_conv_b", "w_down", "final_g"]


def shape_tables():
    half = HEAD // 4
    inv = ROPE_THETA ** (-np.arange(half, dtype=np.float32) / half)
    t = np.arange(S)
    pos = np.stack([t // GRID_W, t % GRID_W]).astype(np.float32)
    p = np.arange(P) % HEAD
    ang = (pos[p // (HEAD // 2)] * inv[p % half][:, None]).astype(np.float32)
    sign = np.where(p % (HEAD // 2) < half, -1.0, 1.0).astype(np.float32)[:, None]
    return {"rope_cos": np.cos(ang).astype(np.float32), "rope_sin": (sign * np.sin(ang)).astype(np.float32)}


def kernel(**inputs):
    import concourse.bacc as _bacc
    from concourse.bass_utils import run_bass_kernel_spmd as _run

    nc = _bacc.Bacc("TRN2", target_bir_lowering=False, num_devices=1)
    arrays, aps = {}, {}
    for name, value in [(n, inputs[n]) for n in _INS] + list(shape_tables().items()):
        v = np.ascontiguousarray(value)
        arrays[f"in_{name}"] = v
        aps[name] = nc.dram_tensor(f"in_{name}", v.shape, mybir.dt.from_np(v.dtype), kind="ExternalInput").ap()
    out = nc.dram_tensor("out", (1, S, D), F32, kind="ExternalOutput").ap()
    build(nc, aps, out)
    result = _run(nc, [arrays], core_ids=[0])
    return result.results[0]["out"]
```

```python
from contextlib import ExitStack

import numpy as np

import concourse.bass as bass
from concourse import mybir
from concourse.alu_op_type import AluOpType as ALU

F32 = mybir.dt.float32
F32R = mybir.dt.float32r
BF16 = mybir.dt.bfloat16
ACT = mybir.ActivationFunctionType
AX_X = mybir.AxisListType.X
ds = bass.ds

P = 128
D = 1024
KD = D // P
S = 2048
L = 256
T = S + L
GRID_W = 64
EPS = 1e-6
D_RNN = 512
RNN_TILES = D_RNN // P
D_ATTN = 512
HEAD = 64
N_HEADS = 8
N_KV = 2
PER_KV = N_HEADS // N_KV
SCALE = HEAD ** -0.5
ROPE_THETA = 10000.0
D_IN = 2 * D_RNN + D_ATTN + 2 * N_KV * HEAD
LRU_C = 8.0
D_FF = 2816
FT = D_FF // P
BQ = 128
NB = S // BQ
CH = 512
NCH = S // CH
NEG = -1e30
GELU_C = 2.0 * float(np.sqrt(2.0 / np.pi))
GELU_A = 0.044715


class Kit:

    def __init__(self, nc, ctx):
        self.nc, self.ctx = nc, ctx
        self.psum = ctx.enter_context(nc.psum_tensor("psum", [P, 8, CH], F32))
        self.phase_sems = []

    def sem(self, name):
        self.phase_sems.append(self.nc.alloc_semaphore(name))
        return self.phase_sems[-1]

    def next_phase(self):
        with self.nc.Block() as block:

            @block.gpsimd
            def _(pool):
                self.nc.clear_and_free_semaphores(self.phase_sems)

        self.phase_sems = []

    def dram(self, name, shape, dt):
        return self.nc.dram_tensor(name, shape, dt).ap()

    def keep(self, name, shape, dt):
        return self.ctx.enter_context(self.nc.sbuf_tensor(name, shape, dt))


def refine_rsqrt(dve, r, v, t, step, done):
    dve.tensor_tensor(t, r, r, ALU.mult).then_inc(step, 1)
    dve.wait_ge(step, done + 1)
    dve.tensor_tensor(t, t, v, ALU.mult).then_inc(step, 1)
    dve.wait_ge(step, done + 2)
    dve.tensor_scalar(t, t, -0.5, 1.5, ALU.mult, ALU.add).then_inc(step, 1)
    dve.wait_ge(step, done + 3)
    dve.tensor_tensor(r, r, t, ALU.mult).then_inc(step, 1)
    dve.wait_ge(step, done + 4)


def modulation_and_norm(k, a, hT_hi, hT_lo, keep, scratch):
    nc, psum = k.nc, k.psum
    ident, aff2 = keep["ident"], keep["aff2"]
    w_mod, b_mod, mod_rows = a["w_mod"], a["b_mod"], scratch["mod"]
    with ExitStack() as ctx:
        def sb(name, shape, dt=F32):
            return ctx.enter_context(nc.sbuf_tensor(name, shape, dt))

        w_slot = [sb(f"wmod{i}", [P, KD, CH]) for i in range(2)]
        row = [sb(f"mod_row{i}", [2, CH]) for i in range(2)]
        x_slot = [sb(f"xnorm{i}", [P, D]) for i in range(2)]
        junk = [sb(f"square_junk{i}", [P, D], BF16) for i in range(2)]
        vec_rows = sb("vec_rows", [4 * KD, P])
        mod_rows_sb = [sb(f"mod_rows_sb{i}", [4 * KD, P]) for i in range(2)]
        vec_cols = sb("vec_cols", [P, 4 * KD])
        mod_cols = [sb(f"mod_cols{i}", [P, 4 * KD]) for i in range(2)]
        cond_silu = sb("cond_silu", [P, 2, KD])
        aff1 = sb("aff1", [P, 2, 2, KD])
        sumsq, rstd, eps_col = sb("sumsq", [P, 20]), sb("rstd", [P, 20]), sb("eps_col", [P, 1])
        t32 = [sb(f"t32_{i}", [P, 2 * P]) for i in range(2)]
        msq, newton = sb("msq", [P, 2]), sb("newton", [P, 2])

        s_vec = k.sem("vectors_landed")
        s_w = [k.sem(f"wmod_landed{i}") for i in range(2)]
        s_bias = [k.sem(f"bias_landed{i}") for i in range(2)]
        s_row_stored = [k.sem(f"mod_row_stored{i}") for i in range(2)]
        s_modrows = k.sem("mod_rows_landed")
        s_x = [k.sem(f"x_landed{i}") for i in range(2)]
        s_ident = k.sem("ident_ready")
        s_small = k.sem("small_transposed")
        s_cols = k.sem("cols_ready")
        s_silu = k.sem("silu_ready")
        s_row = k.sem("mod_row_in_psum")
        s_row_out = k.sem("mod_row_ready")
        s_aff = k.sem("affine_ready")
        s_sq = k.sem("sumsq_ready")
        s_std = k.sem("std_ready")
        s_rstd = k.sem("rstd_ready")
        s_root = k.sem("rsqrt_refined")
        s_xn = k.sem("xn_ready")
        s_tp = k.sem("x_transposed")
        s_t32 = k.sem("modulated_ready")
        s_hi = k.sem("hT_hi_ready")
        s_lo = k.sem("hT_lo_ready")

        ROW_BANK, SMALL_BANK, TP_BANK = (0, 1), 2, (3, 4, 5, 6)
        PAIRS = T // (2 * P)
        CHUNKS = 6 * D // CH

        with nc.Block() as block:

            @block.sync
            def _(sp):
                sp.dma_start(vec_rows[0:KD, :], a["c"].rearrange("a (k p) -> (a k) p", p=P)).then_inc(s_vec, 16)
                sp.dma_start(vec_rows[KD:2 * KD, :], a["c_ctx"].rearrange("(k p) -> k p", p=P)).then_inc(s_vec, 16)
                sp.dma_start(vec_rows[2 * KD:3 * KD, :], a["norm1_g"].rearrange("a (k p) -> (a k) p", p=P)).then_inc(s_vec, 16)
                sp.dma_start(vec_rows[3 * KD:4 * KD, :], a["norm2_g"].rearrange("a (k p) -> (a k) p", p=P)).then_inc(s_vec, 16)
                with sp.Fori(0, CHUNKS // 2) as i:
                    for slot in range(2):
                        sp.wait_ge(s_row_out, i * 2 + slot + 1)
                        sp.dma_start(w_slot[slot][:], w_mod[0, :, ds(i * 2 * CH + slot * CH, CH)].rearrange("(k p) n -> p k n", p=P)).then_inc(s_w[slot], 16)

            @block.gpsimd
            def _(pool):
                nc.gpsimd.memset(ident[:], 0.0).then_inc(s_ident, 1)
                pool.wait_ge(s_ident, 1)
                nc.gpsimd.affine_select(out=ident[:], in_=ident[:], compare_op=ALU.not_equal, fill=1.0, base=0,
                                        pattern=[[-1, P]], channel_multiplier=1).then_inc(s_ident, 1)

                def bias(q, slot):
                    pool.dma_start(row[slot][:], b_mod[0:1, ds(q * CH, CH)].broadcast_to([2, CH])).then_inc(s_bias[slot], 16)

                def store(q, slot, turn):
                    pool.wait_ge(s_row_out, q + 3)
                    pool.dma_start(mod_rows[:, ds(q * CH, CH)], row[slot][:]).then_inc(s_row_stored[slot], 16)
                    pool.wait_ge(s_row_stored[slot], turn * 16 + 16)

                def reload(part, first):
                    for z in range(2):
                        pool.dma_start(mod_rows_sb[part][z * 2 * KD:(z + 1) * 2 * KD, :],
                                       mod_rows[z, first:first + 2 * D].rearrange("(m p) -> m p", p=P)).then_inc(s_modrows, 16)

                bias(0, 0)
                bias(1, 1)
                for q in range(4):
                    store(q, q % 2, q // 2)
                    bias(q + 2, q % 2)
                reload(0, 0)
                with pool.Fori(2, CHUNKS // 2 - 1) as i:
                    for slot in range(2):
                        store(i * 2 + slot, slot, i)
                        bias(i * 2 + slot + 2, slot)
                for slot in range(2):
                    store(CHUNKS - 2 + slot, slot, CHUNKS // 2 - 1)
                reload(1, 3 * D)
                pool.wait_ge(s_modrows, 64)

            @block.scalar
            def _(act):
                for j in range(2):
                    act.dma_start(x_slot[j][:], a["x"][0, j * P:(j + 1) * P, :]).then_inc(s_x[j], 16)
                act.wait_ge(s_cols, 1)
                act.activation(cond_silu[:], vec_cols[:, 0:2 * KD].rearrange("p (a k) -> p a k", a=2), ACT.Silu).then_inc(s_silu, 1)
                act.wait_ge(s_rstd, 1)

                def pair(n, z, following):
                    for j in range(2):
                        act.wait_ge(s_x[j], n * 16 + 16)
                        act.activation(junk[j][:], x_slot[j][:], ACT.Square, accum_out=sumsq[:, ds(n * 2 + j, 1)]).then_inc(s_sq, 1)
                    act.wait_ge(s_sq, n * 2 + 2)
                    act.activation(rstd[:, ds(n * 2, 2)], sumsq[:, ds(n * 2, 2)], ACT.Sqrt, bias=eps_col[:], scale=1.0 / D).then_inc(s_std, 1)
                    if following != "context" or z == 0:
                        act.wait_ge(s_aff, 4)
                    for kt in range(KD):
                        act.wait_ge(s_tp, n * KD + kt + 1)
                        act.wait_ge(s_lo, n * KD + kt + 1)
                        act.activation(t32[kt % 2][:], psum[:, TP_BANK[kt % 4], 0:2 * P], ACT.Identity,
                                       bias=aff1[:, z, 1, kt:kt + 1], scale=aff1[:, z, 0, kt:kt + 1]).then_inc(s_t32, 1)
                    for j in range(2):
                        if following == "latent":
                            act.dma_start(x_slot[j][:], a["x"][0, ds(n * 2 * P + (2 + j) * P, P), :]).then_inc(s_x[j], 16)
                        elif following == "context":
                            act.dma_start(x_slot[j][:], a["ctx"][0, j * P:(j + 1) * P, :]).then_inc(s_x[j], 16)

                with act.Fori(0, PAIRS - 2) as n:
                    pair(n, 0, "latent")
                pair(PAIRS - 2, 0, "context")
                pair(PAIRS - 1, 1, None)

            @block.tensor
            def _(pe):
                pe.wait_ge(s_ident, 2)
                pe.wait_ge(s_vec, 64)
                pe.transpose(psum[:, SMALL_BANK, 0:4 * KD], vec_rows[:], ident[0:4 * KD, 0:4 * KD]).then_inc(s_small, 1)
                pe.wait_ge(s_silu, 1)

                def chunk(q, slot, turn):
                    pe.wait_ge(s_row_out, q + 1)
                    pe.wait_ge(s_w[slot], turn * 16 + 16)
                    for kt in range(KD):
                        mm = pe.matmul(psum[0:2, ROW_BANK[slot], :], cond_silu[:, :, kt], w_slot[slot][:, kt, :], start=(kt == 0), stop=(kt == KD - 1))
                    mm.then_inc(s_row, 1)

                def mod_columns(part):
                    pe.wait_ge(s_modrows, 32 * (part + 1))
                    pe.wait_ge(s_cols, part + 1)
                    pe.transpose(psum[:, SMALL_BANK, 0:4 * KD], mod_rows_sb[part][:], ident[0:4 * KD, 0:4 * KD]).then_inc(s_small, 1)

                def pair(n):
                    pe.wait_ge(s_xn, n * 2 + 2)
                    for kt in range(KD):
                        pe.wait_ge(s_t32, n * KD + kt + 1)
                        for j in range(2):
                            tp = pe.transpose(psum[:, TP_BANK[kt % 4], j * P:(j + 1) * P], x_slot[j][:, kt * P:(kt + 1) * P], ident[:])
                        tp.then_inc(s_tp, 1)

                for q in range(4):
                    chunk(q, q % 2, q // 2)
                mod_columns(0)
                with pe.Fori(0, 4) as n:
                    pair(n * 2)
                    chunk(n * 2 + 4, 0, n + 2)
                    pair(n * 2 + 1)
                    chunk(n * 2 + 5, 1, n + 2)
                pair(PAIRS - 1)
                mod_columns(1)

            @block.vector
            def _(dve):
                dve.sem_inc(s_row_out, 2)
                dve.sem_inc(s_lo, 2)
                dve.sem_inc(s_t32, 4)
                dve.memset(eps_col[:], EPS).then_inc(s_rstd, 1)
                dve.wait_ge(s_small, 1)
                dve.tensor_copy(vec_cols[:], psum[:, SMALL_BANK, 0:4 * KD]).then_inc(s_cols, 1)

                def take_row(q, slot, turn):
                    dve.wait_ge(s_row, q + 1)
                    dve.wait_ge(s_bias[slot], turn * 16 + 16)
                    dve.tensor_tensor(row[slot][:], psum[0:2, ROW_BANK[slot], :], row[slot][:], ALU.add).then_inc(s_row_out, 1)

                def take_columns(part):
                    dve.wait_ge(s_small, part + 2)
                    dve.tensor_copy(mod_cols[part][:], psum[:, SMALL_BANK, 0:4 * KD]).then_inc(s_cols, 1)
                    dve.wait_ge(s_cols, part + 2)

                for q in range(4):
                    take_row(q, q % 2, q // 2)
                take_columns(0)
                for z in range(2):
                    at = z * 2 * KD
                    dve.scalar_tensor_tensor(aff1[:, z, 0, :], mod_cols[0][:, at + KD:at + 2 * KD], 1.0, vec_cols[:, 2 * KD:3 * KD], ALU.add, ALU.mult).then_inc(s_aff, 1)
                    dve.tensor_copy(aff1[:, z, 1, :], mod_cols[0][:, at:at + KD]).then_inc(s_aff, 1)

                def pair(n):
                    dve.wait_ge(s_std, n + 1)
                    dve.reciprocal(rstd[:, ds(n * 2, 2)], rstd[:, ds(n * 2, 2)]).then_inc(s_rstd, 1)
                    dve.tensor_scalar(msq[:], sumsq[:, ds(n * 2, 2)], 1.0 / D, EPS, ALU.mult, ALU.add).then_inc(s_rstd, 1)
                    dve.wait_ge(s_rstd, n * 2 + 3)
                    refine_rsqrt(dve, rstd[:, ds(n * 2, 2)], msq[:], newton[:], s_root, n * 4)
                    for j in range(2):
                        dve.tensor_scalar(x_slot[j][:], x_slot[j][:], rstd[:, ds(n * 2 + j, 1)], None, ALU.mult).then_inc(s_xn, 1)
                    for kt in range(KD):
                        dve.wait_ge(s_t32, n * KD + kt + 5)
                        hi = hT_hi[:, kt, ds(n * 2 * P, 2 * P)]
                        dve.tensor_copy(hi, t32[kt % 2][:]).then_inc(s_hi, 1)
                        dve.wait_ge(s_hi, n * KD + kt + 1)
                        dve.tensor_tensor(hT_lo[:, kt, ds(n * 2 * P, 2 * P)], t32[kt % 2][:], hi.bitcast(F32), ALU.subtract).then_inc(s_lo, 1)

                with dve.Fori(0, 4) as n:
                    pair(n * 2)
                    take_row(n * 2 + 4, 0, n + 2)
                    pair(n * 2 + 1)
                    take_row(n * 2 + 5, 1, n + 2)
                pair(PAIRS - 1)
                take_columns(1)
                dve.scalar_tensor_tensor(aff2[:, 0, :], mod_cols[1][:, KD:2 * KD], 1.0, vec_cols[:, 3 * KD:4 * KD], ALU.add, ALU.mult).then_inc(s_aff, 1)
                dve.tensor_copy(aff2[:, 1, :], mod_cols[1][:, 0:KD]).then_inc(s_aff, 1)


def input_projection(k, a, hT_hi, hT_lo, scratch):
    nc, psum = k.nc, k.psum
    w_in = a["w_in"]
    with ExitStack() as ctx:
        def sb(name, shape, dt=F32):
            return ctx.enter_context(nc.sbuf_tensor(name, shape, dt))

        w_raw = [sb(f"win_raw{i}", [P, KD, P]) for i in range(2)]
        w_hi = [sb(f"win_hi{i}", [P, KD, P], F32R) for i in range(2)]
        w_lo = [sb(f"win_lo{i}", [P, KD, P], F32R) for i in range(2)]
        cos, sin = sb("cos", [P, S]), sb("sin", [P, S])
        stage = [sb(f"stage{i}", [P, CH if i < NCH else L]) for i in range(NCH + 1)]
        swapped, turned = sb("swapped", [P, CH]), sb("turned", [P, CH])
        cut_hi = [sb(f"cut_hi{i}", [P, CH], F32R) for i in range(2)]
        cut_lo = [sb(f"cut_lo{i}", [P, CH], F32R) for i in range(2)]

        s_rope = k.sem("rope_tables_landed")
        s_w = [k.sem(f"win_landed{i}") for i in range(2)]
        s_hi = k.sem("win_hi_ready")
        s_lo = k.sem("win_lo_ready")
        s_acc = k.sem("projection_ready")
        s_stage = k.sem("stage_ready")
        s_free = [k.sem(f"stage_free{i}") for i in range(NCH + 1)]
        s_step = k.sem("rope_step")
        s_cut = k.sem("qk_cut")
        s_hi_cut = k.sem("qk_hi_ready")
        s_cut_stored = [k.sem(f"cut_stored{i}") for i in range(2)]

        KINDS = ((0, 4, True, False, scratch["xr"], 0, 0, 0), (4, 4, False, False, scratch["xg"], 4, 4, 0),
                 (8, 4, False, True, None, 8, 4, 0), (12, 1, True, True, None, 8, 4, 16),
                 (13, 1, True, False, scratch["v"], 13, 5, 21))
        LAST = 13

        def walk(body):
            def run(eng):
                unit = 0
                for m0, count, with_ctx, rope, dram, d0, ctx0, rope0 in KINDS:
                    per = NCH + with_ctx
                    if count > 1:
                        with eng.Fori(0, count // 2) as i:
                            for j in range(2):
                                body(eng, m0 + j + i * 2, j, i + m0 // 2, unit + per * j + i * (2 * per), with_ctx, rope, dram,
                                     j + i * 2 + (m0 - d0), ctx0 + j + i * 2, rope0 + j * NCH + i * (2 * NCH), False)
                    else:
                        body(eng, m0, m0 % 2, m0 // 2, unit, with_ctx, rope, dram, m0 - d0, ctx0, rope0, m0 == LAST)
                    unit += per * count
            return run

        def chunks(with_ctx):
            return [(c, c * CH, CH) for c in range(NCH)] + ([(NCH, S, L)] if with_ctx else [])

        def bank(slot, c):
            return 4 * slot + c if c < NCH else 4 * (1 - slot) + 3

        with nc.Block() as block:

            @block.sync
            def _(sp):
                def load(m, slot, turn):
                    sp.wait_ge(s_lo, m + 1)
                    sp.dma_start(w_raw[slot][:], w_in[0, :, ds(m * P, P)].rearrange("(k p) n -> p k n", p=P)).then_inc(s_w[slot], 16)

                def body(sp, m, slot, turn, unit, with_ctx, rope, dram, row, nctx, nrope, last):
                    if not last:
                        load(m + 1, 1 - slot, None)
                    for c, t0, n in chunks(with_ctx):
                        if rope:
                            half = c % 2
                            sp.wait_ge(s_cut, nrope + c + 1)
                            sp.sem_inc(s_free[c], 16)
                            dst = (ds(row * P, P), slice(t0, t0 + n))
                            sp.dma_start(scratch["qk_hi"][dst[0], dst[1]], cut_hi[half][:, 0:n].bitcast(F32)).then_inc(s_cut_stored[half], 16)
                            sp.dma_start(scratch["qk_lo"][dst[0], dst[1]], cut_lo[half][:, 0:n].bitcast(F32)).then_inc(s_cut_stored[half], 16)
                        else:
                            sp.wait_ge(s_stage, unit + c + 5)
                            sp.dma_start(dram[ds(row * P, P), t0:t0 + n], stage[c][:, 0:n]).then_inc(s_free[c], 16)

                sp.dma_start(cos[:], a["rope_cos"]).then_inc(s_rope, 16)
                sp.dma_start(sin[:], a["rope_sin"]).then_inc(s_rope, 16)
                load(0, 0, None)
                walk(body)(sp)
                for c in range(NCH):
                    sp.wait_ge(s_free[c], 16 * (14 + 1))
                sp.wait_ge(s_free[NCH], 16 * (6 + 1))
                sp.wait_ge(s_cut_stored[0], 32 * (8 + 3 + 1))
                sp.wait_ge(s_cut_stored[1], 32 * (8 + 2 + 1))

            @block.gpsimd
            def _(pool):
                pool.sem_inc(s_lo, 2)

                def cut(m, slot):
                    pool.wait_ge(s_hi, m + 1)
                    nc.gpsimd.tensor_tensor(w_lo[slot][:], w_raw[slot][:], w_hi[slot][:].bitcast(F32), ALU.subtract).then_inc(s_lo, 1)

                def body(pool, m, slot, turn, unit, with_ctx, rope, dram, row, nctx, nrope, last):
                    if not last:
                        cut(m + 1, 1 - slot)

                cut(0, 0)
                walk(body)(pool)

            @block.scalar
            def _(act):
                act.sem_inc(s_stage, 4)
                act.sem_inc(s_acc, 1)
                for c in range(NCH + 1):
                    act.sem_inc(s_free[c], 16)
                for half in range(2):
                    act.sem_inc(s_cut_stored[half], 32)

                def cut(slot, turn, units_before):
                    act.wait_ge(s_w[slot], turn * 16 + 16)
                    act.wait_ge(s_acc, units_before + 1)
                    act.activation(w_hi[slot][:], w_raw[slot][:], ACT.Copy).then_inc(s_hi, 1)

                def body(act, m, slot, turn, unit, with_ctx, rope, dram, row, nctx, nrope, last):
                    if not last:
                        cut(1 - slot, turn + slot, unit)
                    for c, t0, n in chunks(with_ctx):
                        act.wait_ge(s_acc, unit + c + 2)
                        act.wait_ge(s_free[c], ((m if c < NCH else nctx) + 1) * 16)
                        act.activation(stage[c][:, 0:n], psum[:, bank(slot, c), 0:n], ACT.Copy).then_inc(s_stage, 1)

                cut(0, 0, 0)
                walk(body)(act)

            @block.tensor
            def _(pe):
                def body(pe, m, slot, turn, unit, with_ctx, rope, dram, row, nctx, nrope, last):
                    pe.wait_ge(s_lo, m + 3)
                    for c, t0, n in chunks(with_ctx):
                        pe.wait_ge(s_stage, unit + c + 1)
                        for kt in range(KD):
                            for wp, hp in ((w_hi, hT_hi), (w_hi, hT_lo), (w_lo, hT_hi)):
                                mm = pe.matmul(psum[:, bank(slot, c), 0:n], wp[slot][:, kt, :], hp[:, kt, t0:t0 + n],
                                               start=(kt == 0 and wp is w_hi and hp is hT_hi), stop=(kt == KD - 1 and wp is w_lo))
                        mm.then_inc(s_acc, 1)

                walk(body)(pe)

            @block.vector
            def _(dve):
                dve.wait_ge(s_rope, 32)

                def rotated(dve, m, slot, turn, unit, with_ctx, rope, dram, row, nctx, nrope, last):
                    if not rope:
                        return
                    tq, nrope_half = row, row * 2
                    for c, t0, n in chunks(with_ctx):
                        half = c % 2
                        dve.wait_ge(s_stage, unit + c + 5)
                        done = nrope * 4 + c * 4
                        if c < NCH:
                            nc.vector.tensor_tensor(turned[:], stage[c][:], cos[:, t0:t0 + n], ALU.mult).then_inc(s_step, 1)
                            nc.vector.stream_shuffle(swapped[:], stage[c][:], [(i + 16) % 32 for i in range(32)]).then_inc(s_step, 1)
                            dve.wait_ge(s_step, done + 2)
                            nc.vector.tensor_tensor(swapped[:], swapped[:], sin[:, t0:t0 + n], ALU.mult).then_inc(s_step, 1)
                            dve.wait_ge(s_step, done + 3)
                            nc.vector.tensor_tensor(stage[c][:], turned[:], swapped[:], ALU.add).then_inc(s_step, 1)
                            dve.wait_ge(s_step, done + 4)
                        dve.wait_ge(s_cut_stored[half], nrope_half * 32 + (c // 2 + 1) * 32)
                        nc.vector.tensor_copy(cut_hi[half][:, 0:n], stage[c][:, 0:n]).then_inc(s_hi_cut, 1)
                        dve.wait_ge(s_hi_cut, nrope + c + 1)
                        nc.vector.tensor_tensor(cut_lo[half][:, 0:n], stage[c][:, 0:n], cut_hi[half][:, 0:n].bitcast(F32), ALU.subtract).then_inc(s_cut, 1)

                walk(rotated)(dve)


def mixers(k, a, keep, scratch):
    nc, psum = k.nc, k.psum
    ident = keep["ident"]
    GAP = 4
    LAT = L + GAP
    W = LAT + S
    KW = L + P + S + P
    SUB = 4
    HEADS = SUB * N_HEADS
    GROUPS = SUB * N_KV
    ROUNDS = NB // SUB
    GATE_UNITS = 4 * (NCH + 1)
    PACKETS = 5 * GROUPS
    PV_AT, PV_END, COPY_AT, TURN_AT, V_AT = 7, 8, 9, 10, 5
    STEPS = HEADS + 7
    RING = PACKETS + SUB
    SCAN_AT, CONV_AT, CONV_STEPS = (12, 13, 15, 16), 20, 8
    DVE_RNN = CONV_STEPS + 4 + 6
    assert ROUNDS == RNN_TILES

    def ring(Q):
        return Q + (Q + 5) // 10

    def ring_v(n):
        return 11 * n + 5

    PRE = 3

    def event(it, kind, index):
        return (it * GROUPS + index) * 2 + (kind == "turn") + PRE

    with ExitStack() as ctx:
        def sb(name, shape, dt=F32):
            return ctx.enter_context(nc.sbuf_tensor(name, shape, dt))

        keys = sb("keys_hi_lo", [P, N_KV, KW], F32R)
        q_same = [sb(f"q_hi_lo{i}", [P, N_HEADS, P], F32R) for i in range(2)]
        q_cross = [sb(f"q_lo_hi{i}", [P, N_HEADS, P], F32R) for i in range(2)]
        prob = [sb(f"prob{i}", [P, 5 * P]) for i in range(2)]
        pT_hi = [sb(f"probT_hi{i}", [P, PER_KV, 5, P], F32R) for i in range(2)]
        pT_lo = [sb(f"probT_lo{i}", [P, PER_KV, 5, P], F32R) for i in range(2)]
        v_raw = [sb(f"v_raw{i}", [P, P]) for i in range(2)]
        v_ctx = sb("v_ctx", [P, 2, N_KV, 2 * HEAD], F32R)
        v_ring = sb("v_ring", [P, 4, N_KV, 2 * HEAD], F32R)
        oT = sb("oT", [P, CH])
        o_scaled = sb("o_scaled", [P, PER_KV, 2 * HEAD])
        o_tok = [sb(f"o_tok{i}", [P, D_ATTN]) for i in range(2)]
        ident_bf = sb("ident_bf", [P, P], BF16)
        mask_before, mask_after = sb("mask_before", [P, P], BF16), sb("mask_after", [P, P], BF16)
        mask_first, mask_last = sb("mask_first", [P, ROUNDS, P], BF16), sb("mask_last", [P, ROUNDS, P], BF16)
        sink = sb("sink", [P, N_HEADS])
        neg_sink = sb("neg_sink", [P, N_HEADS])
        row_max, neg_max, row_sum, sink_in, sink_exp, inv_sum = (
            [sb(f"{n}{i}", [P, N_HEADS]) for i in range(2)] for n in ("row_max", "neg_max", "row_sum", "sink_in", "sink_exp", "inv_sum"))
        gate_raw = sb("gate_raw", [P, 4, P])
        gate_hi, gate_lo = sb("gate_hi", [P, 4, P], F32R), sb("gate_lo", [P, 4, P], F32R)
        g_r = [sb("decay_gate0", [P, W + GAP]), sb("decay_gate1", [P, W + GAP])]
        g_i = [sb(f"input_gate{d}", [P, W]) for d in range(2)]
        th = [sb(f"tanh_half{d}", [P, W]) for d in range(2)]
        x_pad = g_r[1]
        xc, xc_hi, xc_lo = sb("xc", [P, W]), sb("xc_hi", [P, W], F32R), sb("xc_lo", [P, W], F32R)
        xg, gel = sb("xg_sb", [P, S]), sb("gelu_sb", [P, S])
        par_rows, par = sb("rnn_rows", [44, P]), sb("rnn_cols", [P, 44])
        sp_e, sp_s, sp_p, sp_pos = (sb(n, [P, 8]) for n in ("sp_e", "sp_s", "sp_p", "sp_pos"))
        c_exp, c_tanh = sb("c_exp", [P, 8]), sb("c_tanh", [P, 8])
        CONV_W, CONV_B, B_A, B_I, LAM = 0, 16, 20, 28, 36

        sem = k.sem
        s_setup, s_par, s_parT, s_parc = sem("setup_ready"), sem("params_landed"), sem("params_transposed"), sem("params_step")
        s_keys, s_pads, s_sink = sem("keys_landed"), sem("pads_ready"), sem("sink_landed")
        s_mask = sem("masks_ready")
        s_q = [sem(f"q_landed{i}") for i in range(2)]
        s_vraw = [sem(f"v_landed{i}") for i in range(2)]
        s_vt = sem("v_transposed")
        s_vhi = sem("v_hi_ready")
        s_misc = sem("shared_bank_taken")
        s_sc = sem("scores_ready")
        s_mx, s_nm = sem("row_max_ready"), sem("neg_max_ready")
        s_exp = sem("prob_ready")
        s_pt, s_pttail = sem("prob_packet_transposed"), sem("prob_tail_transposed")
        s_pthi, s_ptlo = sem("probT_hi_ready"), sem("probT_lo_ready")
        s_pv, s_turn = sem("pv_ready"), sem("oT_turned")
        s_sin, s_ses, s_den, s_inv = sem("sink_in_ready"), sem("sink_exp_ready"), sem("sum_ready"), sem("inv_sum_ready")
        s_tok, s_ssq, s_msq = sem("o_tok_ready"), sem("o_sumsq_ready"), sem("o_mean_square_ready")
        s_gbias, s_gelu_turn = sem("gate_biases_ready"), sem("gelu_square_seen")
        o_ssq, gate_bias = sb("o_ssq", [P, 1]), sb("gate_bias", [P, 4])
        s_ostored = [sem(f"o_stored{i}") for i in range(2)]
        s_gw, s_gwhi, s_gwlo = sem("gate_w_landed"), sem("gate_hi_ready"), sem("gate_lo_ready")
        s_gacc, s_gout = sem("gate_in_psum"), sem("gate_out")
        s_xr, s_xg = sem("xr_landed"), sem("xg_landed")
        s_pre, s_sg, s_gelu = sem("gelu_arg_ready"), sem("gelu_sigmoid_ready"), sem("gelu_ready")
        s_xi = sem("gated_x_ready")
        s_th, s_a, s_sq = sem("tanh_ready"), sem("decay_ready"), sem("sqrt_ready")
        s_v, s_hi, s_lo = sem("rnn_vector_step"), sem("xc_hi_ready"), sem("xc_lo_ready")
        s_u, s_both = sem("scan_input_ready"), sem("states_added")
        s_y, s_ystored = sem("y_ready"), sem("y_stored")
        s_pad0 = sem("x_pad_zeroed")
        s_gap = sem("gaps_filled")
        s_series = sem("series_step")

        GATE_BANKS, PT_BANKS, MISC = (0, 1, 2, 3), (4, 5, 7), 6
        S_SLOT = [psum[:, 2 * i:2 * i + 2, :].rearrange("p b c -> p (b c)")[:, P:6 * P] for i in range(2)]

        def packets_of(w):
            return [w // 4 * 5 + p for p in ((0,), (1,), (2,), (3, 4))[w % 4]]

        def packet_of(tile, Q):
            return tile[Q // 5 % 2][:].rearrange("p h b q -> p (h b q)")[:, (Q % 5) * CH:(Q % 5 + 1) * CH]

        def rnn_chunks():
            return [(0, 0, L)] + [(1 + c, LAT + c * CH, CH) for c in range(NCH)]

        def rounds(eng, body):
            with eng.Fori(0, ROUNDS - 1) as it:
                body(it, False)
            body(ROUNDS - 1, True)

        def unit_of(v):
            return v // (2 * (NCH + 1)), v // (NCH + 1) % 2, rnn_chunks()[v % (NCH + 1)]

        def gate_share(u):
            k0, steps = u - HEADS - 1, STEPS - HEADS - 1
            return k0 * GATE_UNITS // steps, (k0 + 1) * GATE_UNITS // steps

        with nc.Block() as block:

            @block.sync
            def _(sp):
                rows = (("rnn_conv_w", 16), ("rnn_conv_b", 4), ("lru_b_a", 8), ("lru_b_i", 8), ("lru_lam", 8))
                at = 0
                for name, n in rows:
                    src = a[name][0] if name != "rnn_conv_b" else a[name]
                    sp.dma_start(par_rows[at:at + n, :], src.rearrange("a (j p) -> (a j) p", p=P)).then_inc(s_par, 16)
                    at += n

                def load_q(n, par_):
                    tok = ds(n * P, P)
                    hi = scratch["qk_hi"][0:D_ATTN, tok].rearrange("(h d) t -> d h t", d=HEAD)
                    lo = scratch["qk_lo"][0:D_ATTN, tok].rearrange("(h d) t -> d h t", d=HEAD)
                    for tile, top, low in ((q_same, hi, lo), (q_cross, lo, hi)):
                        sp.dma_start(tile[par_][0:HEAD, :, :].bitcast(F32), top).then_inc(s_q[par_], 16)
                        sp.dma_start(tile[par_][HEAD:P, :, :].bitcast(F32), low).then_inc(s_q[par_], 16)

                def load_v(col, slot):
                    sp.dma_start(v_raw[slot][:], scratch["v"][:, col]).then_inc(s_vraw[slot], 16)

                load_v(ds(S, P), 0)
                load_v(ds(S + P, P), 1)
                load_q(0, 0)
                sp.wait_ge(s_vt, 1)
                load_v(ds(0, P), 0)

                def body(it, last):
                    for n in range(SUB):
                        sp.wait_ge(s_vt, it * SUB + n + 2)
                        load_v(ds(it * (SUB * P) + (n + 1) * P, P), (n + 1) % 2)
                        if not (last and n == SUB - 1):
                            sp.wait_ge(s_sc, it * HEADS + n * N_HEADS + 1)
                            load_q(it * SUB + n + 1, (n + 1) % 2)
                        if n:
                            store(it, n - 1)
                        if n == SUB - 1:
                            sp.wait_ge(s_y, it + 1)
                            sp.dma_start(scratch["mix"][ds(it * P, P), :], g_i[0][:, LAT:W]).then_inc(s_ystored, 16)
                    store(it, SUB - 1)

                def store(it, n):
                    sp.wait_ge(s_tok, it * GROUPS + 2 * n + 3)
                    sp.dma_start(scratch["att"][ds(it * (SUB * P) + n * P, P), :], o_tok[n % 2][:]).then_inc(s_ostored[n % 2], 16)

                rounds(sp, body)
                for i in range(2):
                    sp.wait_ge(s_ostored[i], 16 * (NB // 2 + 1))
                sp.wait_ge(s_ystored, 16 * (ROUNDS + 1))

            @block.gpsimd
            def _(pool):
                nc.gpsimd.memset(gate_raw[:], 0.0).then_inc(s_setup, 1)
                pool.wait_ge(s_setup, 1)

                def load_gates(it):
                    for g, name in enumerate(("lru_w_a", "lru_w_i")):
                        for b in range(2):
                            pool.dma_start(gate_raw[b * 64:(b + 1) * 64, 2 * g:2 * g + 2, b * 64:(b + 1) * 64],
                                           a[name][0, :, ds(it * 2 + b, 1), :, :].rearrange("d o c e -> c (d o) e")).then_inc(s_gw, 16)

                def load_xr(it):
                    pool.dma_start(x_pad[:, 2:2 + L], scratch["xr"][ds(it * P, P), S:T]).then_inc(s_xr, 16)
                    pool.dma_start(x_pad[:, 2 + LAT:2 + W], scratch["xr"][ds(it * P, P), 0:S]).then_inc(s_xr, 16)

                def load_xg(it):
                    pool.dma_start(xg[:], scratch["xg"][ds(it * P, P), :]).then_inc(s_xg, 16)

                load_xr(0)
                load_gates(0)
                load_xg(0)
                nc.gpsimd.memset(mask_before[:], 0.0).then_inc(s_mask, 1)
                nc.gpsimd.memset(mask_after[:], 0.0).then_inc(s_mask, 1)
                nc.gpsimd.tensor_copy(ident_bf[:], ident[:]).then_inc(s_mask, 1)
                pool.wait_ge(s_mask, 3)
                nc.gpsimd.affine_select(out=mask_before[:], in_=mask_before[:], compare_op=ALU.is_ge, fill=NEG, base=0,
                                        pattern=[[1, P]], channel_multiplier=-1).then_inc(s_mask, 1)
                nc.gpsimd.affine_select(out=mask_after[:], in_=mask_after[:], compare_op=ALU.is_ge, fill=NEG, base=0,
                                        pattern=[[-1, P]], channel_multiplier=1).then_inc(s_mask, 1)
                pool.wait_ge(s_mask, 5)
                for r in range(ROUNDS):
                    if r == 0:
                        nc.gpsimd.memset(mask_first[:, r, :], NEG).then_inc(s_mask, 1)
                    else:
                        nc.gpsimd.tensor_copy(mask_first[:, r, :], mask_before[:]).then_inc(s_mask, 1)
                    if r == ROUNDS - 1:
                        nc.gpsimd.memset(mask_last[:, r, :], NEG).then_inc(s_mask, 1)
                    else:
                        nc.gpsimd.tensor_copy(mask_last[:, r, :], mask_after[:]).then_inc(s_mask, 1)

                def gelu_argument(it):
                    pool.wait_ge(s_xg, it * 16 + 16)
                    nc.gpsimd.tensor_tensor(gel[:], xg[:], xg[:], ALU.mult).then_inc(s_pre, 1)
                    pool.wait_ge(s_pre, it * 3 + 1)
                    pool.sem_inc(s_gelu_turn, 1)
                    nc.gpsimd.tensor_scalar(gel[:], gel[:], GELU_A, 1.0, ALU.mult, ALU.add).then_inc(s_pre, 1)
                    pool.wait_ge(s_pre, it * 3 + 2)
                    nc.gpsimd.tensor_tensor(gel[:], gel[:], xg[:], ALU.mult).then_inc(s_pre, 1)

                gelu_argument(0)

                def body(it, last):
                    pool.wait_ge(s_gout, it * GATE_UNITS + GATE_UNITS + 4)
                    for d in range(2):
                        nc.gpsimd.tensor_tensor(g_i[d][:], g_i[d][:], xc[:], ALU.mult).then_inc(s_xi, 1)
                    pool.wait_ge(s_sg, it + 1)
                    nc.gpsimd.tensor_tensor(gel[:], gel[:], xg[:], ALU.mult).then_inc(s_gelu, 1)
                    if not last:
                        load_gates(it + 1)
                        pool.wait_ge(s_gelu, it + 1)
                        load_xg(it + 1)
                    for d in range(2):
                        pool.wait_ge(s_xi, it * 2 + d + 1)
                        pool.wait_ge(s_v, it * DVE_RNN + CONV_STEPS + 2 * d + 2)
                        nc.gpsimd.tensor_tensor(th[d][:], th[d][:], g_i[d][:], ALU.mult).then_inc(s_u, 1)
                    pool.wait_ge(s_v, it * DVE_RNN + CONV_STEPS + 10)
                    if not last:
                        load_xr(it + 1)
                    nc.gpsimd.tensor_tensor(g_i[0][:, LAT:W], g_i[0][:, LAT:W], g_i[1][:, LAT:W], ALU.add).then_inc(s_both, 1)
                    pool.wait_ge(s_both, it + 1)
                    nc.gpsimd.tensor_tensor(g_i[0][:, LAT:W], g_i[0][:, LAT:W], gel[:], ALU.mult).then_inc(s_y, 1)
                    pool.wait_ge(s_y, it + 1)
                    if not last:
                        gelu_argument(it + 1)
                        pool.wait_ge(s_hi, it + 2)
                        nc.gpsimd.tensor_tensor(xc_lo[:], xc[:], xc_hi[:].bitcast(F32), ALU.subtract).then_inc(s_lo, 1)

                rounds(pool, body)

            @block.scalar
            def _(act):
                for kv in range(N_KV):
                    rows = slice(D_ATTN + kv * HEAD, D_ATTN + (kv + 1) * HEAD)
                    for half, src in ((0, scratch["qk_hi"]), (1, scratch["qk_lo"])):
                        dst = keys[half * HEAD:(half + 1) * HEAD, kv, :].bitcast(F32)
                        act.dma_start(dst[:, 0:L], src[rows, S:T]).then_inc(s_keys, 16)
                        act.dma_start(dst[:, L + P:L + P + S], src[rows, 0:S]).then_inc(s_keys, 16)
                act.dma_start(sink[:], a["attn_sink"].broadcast_to([P, N_HEADS])).then_inc(s_sink, 16)
                act.wait_ge(s_parc, 1)
                act.activation(sp_e[:], par[:, LAM:LAM + 8], ACT.Abs).then_inc(s_parc, 1)
                act.wait_ge(s_parc, 2)
                act.activation(sp_e[:], sp_e[:], ACT.Exp, scale=-1.0).then_inc(s_parc, 1)
                act.sem_inc(s_gout, 4)
                act.sem_inc(s_exp, 2)
                act.sem_inc(s_misc, 1)
                act.sem_inc(s_ostored[0], 16)
                act.sem_inc(s_ostored[1], 16)
                act.sem_inc(s_ystored, 16)

                def gates(it, first, end):
                    if first == 0:
                        act.wait_ge(s_ystored, it * 16 + 16)
                        act.wait_ge(s_gap, it + 4)
                        act.wait_ge(s_gbias, it + 1)
                    for v in range(first, end):
                        g, d, (c, t0, n) = unit_of(v)
                        act.wait_ge(s_gacc, it * GATE_UNITS + v + 1)
                        act.activation((g_r, g_i)[g][d][:, t0:t0 + n], psum[:, GATE_BANKS[v % 4], 0:n], ACT.Sigmoid,
                                       bias=gate_bias[:, g * 2 + d:g * 2 + d + 1]).then_inc(s_gout, 1)
                    if end == GATE_UNITS:
                        act.wait_ge(s_pre, it * 3 + 3)
                        act.activation(gel[:], gel[:], ACT.Sigmoid, scale=GELU_C).then_inc(s_sg, 1)

                def body(it, last):
                    for u in range(STEPS):
                        if u >= COPY_AT and (u - COPY_AT) % 4 == 0 and (u - COPY_AT) // 4 < GROUPS:
                            G = (u - COPY_AT) // 4
                            act.wait_ge(s_pv, it * GROUPS + G + 3)
                            act.wait_ge(s_turn, it * GROUPS + G + 1)
                            act.activation(oT[:], psum[:, MISC, :], ACT.Copy).then_inc(s_misc, 1)
                        if 3 <= u < HEADS + 3:
                            for Q in packets_of(u - 3):
                                act.wait_ge(s_pt, it * PACKETS + Q + 1)
                                act.wait_ge(s_pv, it * GROUPS + Q // 5 + 1)
                                act.activation(packet_of(pT_hi, Q), psum[:, PT_BANKS[ring(Q) % 3], :], ACT.Copy).then_inc(s_pthi, 1)
                        if 1 <= u <= HEADS:
                            w = u - 1
                            s, h, n = w % 2, w % 8, (w // 8) % 2
                            act.wait_ge(s_nm, it * HEADS + w + 1)
                            if w % 4 == 1 and w > 4:
                                act.wait_ge(s_pt, it * PACKETS + w // 4 * 5)
                            elif w >= 2:
                                act.wait_ge(s_pttail, it * 3 * GROUPS + (w - 2) // 4 * 3 + (w - 2) % 4 + 1)
                            act.activation(prob[s][:], S_SLOT[s], ACT.Exp, bias=neg_max[n][:, h:h + 1], scale=SCALE,
                                           accum_out=row_sum[n][:, h:h + 1]).then_inc(s_exp, 1)
                        if u % 4 == 0 and 4 <= u <= HEADS:
                            G = u // 4 - 1
                            n, kv = (G // 2) % 2, G % 2
                            act.wait_ge(s_sin, it * GROUPS + G + 1)
                            act.activation(sink_exp[n][:, kv * 4:kv * 4 + 4], sink_in[n][:, kv * 4:kv * 4 + 4], ACT.Exp).then_inc(s_ses, 1)
                        if u in (1, 2):
                            d = u - 1
                            act.activation(th[d][:], g_r[d][:, 0:W], ACT.Tanh, scale=c_tanh[:, ds(it + d * RNN_TILES, 1)]).then_inc(s_th, 1)
                        if u in (3, 4):
                            d = u - 3
                            act.wait_ge(s_th, it * 2 + d + 1)
                            act.activation(g_r[d][:, 0:W], g_r[d][:, 0:W], ACT.Exp, scale=c_exp[:, ds(it + d * RNN_TILES, 1)]).then_inc(s_a, 1)
                        if u == 5:
                            for d in range(2):
                                act.activation(th[d][:], th[d][:], ACT.Sqrt).then_inc(s_sq, 1)
                        if u > HEADS and not last:
                            gates(it + 1, *gate_share(u))

                act.wait_ge(s_parc, 13)
                gates(0, 0, GATE_UNITS)
                rounds(act, body)

            @block.tensor
            def _(pe):
                pe.wait_ge(s_par, 80)
                pe.transpose(psum[:, 7, 0:44], par_rows[:], ident[0:44, 0:44]).then_inc(s_parT, 1)

                def turn_v(bank, slot, landed):
                    pe.wait_ge(s_vraw[slot], landed)
                    pe.transpose(psum[:, bank, 0:P], v_raw[slot][:], ident[:]).then_inc(s_vt, 1)

                for i, slot in enumerate((0, 1, 0)):
                    pe.wait_ge(s_misc, i + 1)
                    turn_v(MISC, slot, i // 2 * 16 + 16)
                pe.wait_ge(s_keys, 16 * 8)
                pe.wait_ge(s_pads, 2 * N_KV + 1)
                pe.wait_ge(s_mask, 5 + 2 * ROUNDS)

                def gates(it, first, end):
                    if first == 0:
                        pe.wait_ge(s_gwlo, it + 1)
                        pe.wait_ge(s_lo, it + 1)
                        pe.wait_ge(s_exp, it * HEADS + 2)
                    for v in range(first, end):
                        g, d, (c, t0, n) = unit_of(v)
                        pe.wait_ge(s_gout, it * GATE_UNITS + v + 1)
                        for i, (wt, xt) in enumerate(((gate_hi, xc_hi), (gate_hi, xc_lo), (gate_lo, xc_hi))):
                            mm = pe.matmul(psum[:, GATE_BANKS[v % 4], 0:n], wt[:, g * 2 + d, :], xt[:, t0:t0 + n], start=(i == 0), stop=(i == 2))
                        mm.then_inc(s_gacc, 1)
                    if end == GATE_UNITS:
                        pe.wait_ge(s_gout, it * GATE_UNITS + GATE_UNITS + 4)

                gates(0, 0, GATE_UNITS)

                def body(it, last):
                    def times_v(G, blocks):
                        n, kv = G // 2, G % 2
                        for b in blocks:
                            v_b = v_ring[:, (n - 1 + b) % 4, kv, :] if b < 3 else v_ctx[:, b - 3, kv, :]
                            for pT in (pT_hi, pT_lo):
                                mm = pe.matmul(psum[:, MISC, :], v_b, pT[G % 2][:, :, b, :], start=(b == 0 and pT is pT_hi), stop=(b == 4 and pT is pT_lo))
                        return mm

                    for u in range(STEPS):
                        if u >= TURN_AT and (u - TURN_AT) % 4 == 0 and (u - TURN_AT) // 4 < GROUPS:
                            G = (u - TURN_AT) // 4
                            pe.wait_ge(s_misc, event(it, "turn", G) + 1)
                            for h in range(PER_KV):
                                tp = pe.transpose(psum[:, MISC, h * P:(h + 1) * P], oT[:, h * P:(h + 1) * P], ident[:])
                            tp.then_inc(s_turn, 1)
                        if u < HEADS:
                            s, h, n = u % 2, u % 8, u // 8
                            kv, slot = h // PER_KV, n % 2
                            if h == 0:
                                pe.wait_ge(s_q[slot], (it * 2 + n // 2) * 64 + 64)
                            pe.wait_ge(s_exp, it * HEADS + u + 1)
                            local = ds(it * (SUB * P) + n * P + L, 3 * P)
                            before = mask_first[:, ds(it, 1), :].rearrange("p o c -> p (o c)") if n == 0 else mask_before[:]
                            after = mask_last[:, ds(it, 1), :].rearrange("p o c -> p (o c)") if n == SUB - 1 else mask_after[:]
                            band, context = S_SLOT[s][:, 0:3 * P], S_SLOT[s][:, 3 * P:5 * P]
                            pe.matmul(band, q_same[slot][:, h, :], keys[:, kv, local], start=True, stop=False)
                            pe.matmul(band, q_cross[slot][:, h, :], keys[:, kv, local], start=False, stop=False)
                            pe.matmul(band[:, 0:P], ident_bf[:], before, start=False, stop=False)
                            pe.matmul(band[:, 2 * P:3 * P], ident_bf[:], after, start=False, stop=True)
                            pe.matmul(context, q_same[slot][:, h, :], keys[:, kv, 0:L], start=True, stop=False)
                            pe.matmul(context, q_cross[slot][:, h, :], keys[:, kv, 0:L], start=False, stop=True).then_inc(s_sc, 1)
                        if 2 <= u < HEADS + 2:
                            w = u - 2
                            pe.wait_ge(s_exp, it * HEADS + w + 3)
                            for b in range(5):
                                i = w % 4 * 5 + b
                                Q = w // 4 * 5 + i // 4
                                if i % 4 == 0:
                                    pe.wait_ge(s_ptlo, it * RING + ring(Q) + 1)
                                tp = pe.transpose(psum[:, PT_BANKS[ring(Q) % 3], i % 4 * P:(i % 4 + 1) * P], prob[w % 2][:, b * P:(b + 1) * P], ident[:])
                                if i % 4 == 3:
                                    tp.then_inc(s_pt, 1)
                                elif b == 4:
                                    tp.then_inc(s_pttail, 1)
                        if u % 8 == V_AT and u < HEADS:
                            n = u // 8
                            slot = (n + 1) % 2
                            pe.wait_ge(s_ptlo, it * RING + ring_v(n) + 1)
                            turn_v(PT_BANKS[ring_v(n) % 3], slot, (it * 2 + n // 2) * 16 + (32 if slot == 1 else 48))
                        if u >= PV_AT and (u - PV_AT) % 4 == 0 and (u - PV_AT) // 4 < GROUPS:
                            G = (u - PV_AT) // 4
                            n, kv = G // 2, G % 2
                            pe.wait_ge(s_ptlo, it * RING + (ring_v(n) if kv == 0 else ring(5 * G + 4)) + 4)
                            pe.wait_ge(s_misc, event(it, "pv", G) + 1)
                            times_v(G, (0, 1))
                        if u >= PV_END and (u - PV_END) % 4 == 0 and (u - PV_END) // 4 < GROUPS:
                            times_v((u - PV_END) // 4, (2, 3, 4)).then_inc(s_pv, 1)
                        if u > HEADS and not last:
                            gates(it + 1, *gate_share(u))

                rounds(pe, body)

            @block.vector
            def _(dve):
                dve.sem_inc(s_ptlo, 3)
                dve.sem_inc(s_pv, 2)
                dve.sem_inc(s_turn, 1)
                dve.sem_inc(s_ssq, 1)
                dve.sem_inc(s_tok, 1)
                dve.sem_inc(s_msq, 1)
                for kv in range(N_KV):
                    for at in (L, L + P + S):
                        dve.memset(keys[:, kv, at:at + P].bitcast(F32), 0.0).then_inc(s_pads, 1)
                dve.memset(v_ring[:, 3, :, :].bitcast(F32), 0.0).then_inc(s_pads, 1)
                for t in (g_r[0], g_i[0], g_i[1]):
                    dve.memset(t[:, L:LAT], 0.5).then_inc(s_gap, 1)
                dve.wait_ge(s_parT, 1)
                dve.tensor_copy(par[:], psum[:, 7, 0:44]).then_inc(s_parc, 1)
                dve.wait_ge(s_sink, 16)
                dve.tensor_scalar(neg_sink[:], sink[:], -1.0, None, ALU.mult).then_inc(s_mx, 1)
                dve.wait_ge(s_parc, 3)
                dve.tensor_scalar(sp_s[:], sp_e[:], 2.0, None, ALU.add).then_inc(s_parc, 1)
                dve.wait_ge(s_parc, 4)
                dve.reciprocal(sp_s[:], sp_s[:]).then_inc(s_parc, 1)
                dve.wait_ge(s_parc, 5)
                dve.tensor_tensor(sp_s[:], sp_s[:], sp_e[:], ALU.mult).then_inc(s_parc, 1)
                dve.wait_ge(s_parc, 6)
                dve.tensor_tensor(sp_e[:], sp_s[:], sp_s[:], ALU.mult).then_inc(s_parc, 1)
                dve.memset(sp_p[:], 1.0 / 17).then_inc(s_parc, 1)
                dve.wait_ge(s_parc, 8)
                for j, odd in enumerate((15, 13, 11, 9, 7, 5, 3, 1)):
                    dve.tensor_tensor(sp_p[:], sp_p[:], sp_e[:], ALU.mult).then_inc(s_series, 1)
                    dve.wait_ge(s_series, 2 * j + 1)
                    dve.tensor_scalar(sp_p[:], sp_p[:], 1.0 / odd, None, ALU.add).then_inc(s_series, 1)
                    dve.wait_ge(s_series, 2 * j + 2)
                dve.scalar_tensor_tensor(sp_p[:], sp_p[:], 2.0, sp_s[:], ALU.mult, ALU.mult).then_inc(s_parc, 1)
                dve.tensor_scalar(sp_pos[:], par[:, LAM:LAM + 8], -1.0, 0.0, ALU.mult, ALU.max).then_inc(s_parc, 1)
                dve.wait_ge(s_parc, 10)
                dve.tensor_tensor(sp_p[:], sp_p[:], sp_pos[:], ALU.add).then_inc(s_parc, 1)
                dve.wait_ge(s_parc, 11)
                dve.tensor_scalar(c_exp[:], sp_p[:], -LRU_C, None, ALU.mult).then_inc(s_parc, 1)
                dve.tensor_scalar(c_tanh[:], sp_p[:], LRU_C / 2, None, ALU.mult).then_inc(s_parc, 1)

                def cut_v(slot_ap, count, bank, s_free):
                    dve.wait_ge(s_vt, count + 1)
                    src = psum[:, bank, 0:P].rearrange("p (g d) -> p g d", g=N_KV)
                    dve.tensor_copy(slot_ap[:, :, 0:HEAD], src).then_inc(s_vhi, 1)
                    dve.wait_ge(s_vhi, count + 1)
                    dve.tensor_tensor(slot_ap[:, :, HEAD:2 * HEAD], src, slot_ap[:, :, 0:HEAD].bitcast(F32), ALU.subtract).then_inc(s_free, 1)

                cut_v(v_ctx[:, 0], 0, MISC, s_misc)
                cut_v(v_ctx[:, 1], 1, MISC, s_misc)
                cut_v(v_ring[:, 0], 2, MISC, s_misc)

                def convolve(it, step):
                    j, half = step // 2, slice(step % 2 * (W // 2), (step % 2 + 1) * (W // 2))
                    shifted = x_pad[:, half.start + j:half.stop + j]
                    if step == 0:
                        for at, n in ((0, 2), (2 + L, GAP), (2 + W, 1)):
                            dve.memset(x_pad[:, at:at + n], 0.0).then_inc(s_pad0, 1)
                        dve.wait_ge(s_pad0, it * 3 + 3)
                        dve.wait_ge(s_xr, it * 32 + 32)
                    if j == 0:
                        dve.tensor_scalar(xc[:, half], shifted, par[:, ds(it + CONV_W, 1)], par[:, ds(it + CONV_B, 1)], ALU.mult, ALU.add).then_inc(s_v, 1)
                    else:
                        dve.wait_ge(s_v, it * DVE_RNN + step - 1)
                        dve.scalar_tensor_tensor(xc[:, half], shifted, par[:, ds(it + CONV_W + j * RNN_TILES, 1)], xc[:, half], ALU.mult, ALU.add).then_inc(s_v, 1)
                    if step == CONV_STEPS - 1:
                        dve.wait_ge(s_v, it * DVE_RNN + CONV_STEPS)
                        dve.memset(x_pad[:, L:LAT], 0.5).then_inc(s_gap, 1)

                def gate_biases(it):
                    dve.tensor_copy(gate_bias[:].rearrange("p (g o) -> p g o", o=1),
                                    par[:, B_A:B_A + 4 * RNN_TILES].rearrange("p (g f) -> p g f", f=RNN_TILES)[:, :, ds(it, 1)]).then_inc(s_gbias, 1)

                def cut_x(it):
                    dve.tensor_copy(xc_hi[:], xc[:]).then_inc(s_hi, 1)

                def cut_gates(it):
                    dve.wait_ge(s_gw, it * 64 + 64)
                    dve.tensor_copy(gate_hi[:], gate_raw[:]).then_inc(s_gwhi, 1)
                    dve.wait_ge(s_gwhi, it + 1)
                    dve.tensor_tensor(gate_lo[:], gate_raw[:], gate_hi[:].bitcast(F32), ALU.subtract).then_inc(s_gwlo, 1)

                for step in range(CONV_STEPS):
                    convolve(0, step)
                cut_x(0)
                dve.wait_ge(s_hi, 1)
                dve.tensor_tensor(xc_lo[:], xc[:], xc_hi[:].bitcast(F32), ALU.subtract).then_inc(s_lo, 1)
                cut_gates(0)
                gate_biases(0)

                def body(it, last):
                    base = it * DVE_RNN + CONV_STEPS
                    for u in range(STEPS):
                        if u < HEADS:
                            s, h, n = u % 2, u % 8, (u // 8) % 2
                            dve.wait_ge(s_sc, it * HEADS + u + 1)
                            dve.reduce_max(row_max[n][:, h:h + 1], S_SLOT[s], AX_X).then_inc(s_mx, 1)
                        if 3 <= u < HEADS + 3:
                            for Q in packets_of(u - 3):
                                dve.wait_ge(s_pthi, it * PACKETS + Q + 1)
                                dve.tensor_tensor(packet_of(pT_lo, Q), psum[:, PT_BANKS[ring(Q) % 3], :],
                                                  packet_of(pT_hi, Q).bitcast(F32), ALU.subtract).then_inc(s_ptlo, 1)
                        if u % 8 == V_AT + 1 and u < HEADS:
                            block_n = u // 8
                            cut_v(v_ring[:, (block_n + 1) % 4], it * SUB + block_n + 3, PT_BANKS[ring_v(block_n) % 3], s_ptlo)
                        if u < HEADS:
                            dve.wait_ge(s_mx, it * HEADS + u + 2)
                            dve.tensor_scalar(neg_max[n][:, h:h + 1], row_max[n][:, h:h + 1], -SCALE, neg_sink[:, h:h + 1], ALU.mult, ALU.min).then_inc(s_nm, 1)
                            if u % 4 == 3:
                                kv = h // 4
                                dve.wait_ge(s_nm, it * HEADS + u + 1)
                                dve.tensor_tensor(sink_in[n][:, kv * 4:kv * 4 + 4], sink[:, kv * 4:kv * 4 + 4], neg_max[n][:, kv * 4:kv * 4 + 4], ALU.add).then_inc(s_sin, 1)
                        if u % 4 == 1 and 5 <= u <= HEADS + 1:
                            G = u // 4 - 1
                            n, kv = (G // 2) % 2, G % 2
                            cols = slice(kv * 4, kv * 4 + 4)
                            dve.wait_ge(s_ses, it * GROUPS + G + 1)
                            dve.tensor_tensor(inv_sum[n][:, cols], sink_exp[n][:, cols], row_sum[n][:, cols], ALU.add).then_inc(s_den, 1)
                            dve.wait_ge(s_den, it * GROUPS + G + 1)
                            dve.reciprocal(inv_sum[n][:, cols], inv_sum[n][:, cols]).then_inc(s_inv, 1)
                        if u >= TURN_AT and (u - TURN_AT) % 4 == 0 and (u - TURN_AT) // 4 < GROUPS:
                            G = (u - TURN_AT) // 4
                            n, kv = (G // 2) % 2, G % 2
                            dve.wait_ge(s_turn, it * GROUPS + G + 2)
                            dve.wait_ge(s_inv, it * GROUPS + G + 1)
                            dve.wait_ge(s_tok, it * GROUPS + G + 1)
                            dve.wait_ge(s_ssq, it * SUB + G // 2 + 1)
                            dve.tensor_tensor(o_scaled[:], psum[:, MISC, :].rearrange("p (h d) -> p h d", h=PER_KV),
                                              inv_sum[n][:, kv * 4:kv * 4 + 4].rearrange("p (h o) -> p h o", o=1).broadcast_to([P, PER_KV, 2 * HEAD]), ALU.mult).then_inc(s_misc, 1)
                            dve.wait_ge(s_misc, event(it, "turn", G) + 2)
                            dve.wait_ge(s_ostored[n], (it * 2 + G // 4) * 16 + 16)
                            dve.tensor_tensor(o_tok[n][:, kv * 256:(kv + 1) * 256].rearrange("p (h d) -> p h d", h=PER_KV),
                                              o_scaled[:, :, 0:HEAD], o_scaled[:, :, HEAD:2 * HEAD], ALU.add).then_inc(s_tok, 1)
                            if kv == 1:
                                dve.wait_ge(s_tok, it * GROUPS + G + 2)
                                dve.wait_ge(s_msq, it * SUB + G // 2 + 1)
                                dve.tensor_tensor_reduce(o_scaled[:].rearrange("p h d -> p (h d)"), o_tok[n][:], o_tok[n][:], 1.0, 0.0, ALU.mult, ALU.add,
                                                         o_ssq[:]).then_inc(s_ssq, 1)
                                dve.wait_ge(s_ssq, it * SUB + G // 2 + 2)
                                dve.tensor_scalar(keep["msq_attn"][:, ds(it * SUB + G // 2, 1)], o_ssq[:], 1.0 / D_ATTN, EPS, ALU.mult, ALU.add).then_inc(s_msq, 1)
                        if 7 <= u < 11:
                            d, half = (u - 7) // 2, slice((u - 7) % 2 * (W // 2), ((u - 7) % 2 + 1) * (W // 2))
                            dve.wait_ge(s_sq, it * 2 + d + 1)
                            dve.wait_ge(s_a, it * 2 + d + 1)
                            dve.scalar_tensor_tensor(th[d][:, half], g_r[d][:, half], 1.0, th[d][:, half], ALU.add, ALU.mult).then_inc(s_v, 1)
                        if u in SCAN_AT:
                            d, part = SCAN_AT.index(u) // 2, SCAN_AT.index(u) % 2
                            dve.wait_ge(s_u, it * 2 + d + 1)
                            if d == 0:
                                pieces = ((0, L, 0.0), (LAT, S // 2, g_i[0][:, L - 1:L]), (LAT + S // 2, S // 2, g_i[0][:, LAT + S // 2 - 1:LAT + S // 2]))
                            else:
                                pieces = ((0, L, 0.0), (LAT + S // 2, S // 2, g_i[1][:, 0:1]), (LAT, S // 2, g_i[1][:, LAT + S // 2:LAT + S // 2 + 1]))
                            for i in ((0, 1), (2,))[part]:
                                t0, n, state = pieces[i]
                                dve.wait_ge(s_v, base + 4 + 3 * d + i)
                                tok, forward = slice(t0, t0 + n), slice(None, None, 1 - 2 * d)
                                dve.tensor_tensor_scan(g_i[d][:, tok][:, forward], g_r[d][:, tok][:, forward], th[d][:, tok][:, forward], state, ALU.mult, ALU.add).then_inc(s_v, 1)
                        if CONV_AT <= u < CONV_AT + CONV_STEPS and not last:
                            convolve(it + 1, u - CONV_AT)
                        if u == CONV_AT + CONV_STEPS and not last:
                            cut_x(it + 1)
                        if u == CONV_AT + CONV_STEPS + 1 and not last:
                            cut_gates(it + 1)
                            gate_biases(it + 1)

                rounds(dve, body)
                dve.wait_ge(s_msq, NB + 1)


def output_projection(k, a, x1, rstd2, keep, scratch):
    nc, psum = k.nc, k.psum
    with ExitStack() as ctx:
        def sb(name, shape, dt=F32):
            return ctx.enter_context(nc.sbuf_tensor(name, shape, dt))

        w_raw = [sb(f"wout_raw{i}", [P, D]) for i in range(2)]
        w_hi, w_lo = sb("wout_hi", [P, KD, D], F32R), sb("wout_lo", [P, KD, D], F32R)
        gain_rows, gain = sb("gain_rows", [KD, P]), sb("gain_cols", [P, KD])
        rnn = [sb(f"rnn{i}", [P, RNN_TILES, P]) for i in range(2)]
        att = [sb(f"att{i}", [P, D_ATTN]) for i in range(2)]
        mix_hi = [sb(f"mix_hi{i}", [P, KD, P], F32R) for i in range(2)]
        mix_lo = [sb(f"mix_lo{i}", [P, KD, P], F32R) for i in range(2)]
        square, square_sum = sb("rnn_square", [P, RNN_TILES, P]), sb("rnn_square_sum", [P, P])
        x_in = [sb(f"x_in{i}", [P, D]) for i in range(2)]
        part = [sb(f"rnn_part{i}", [P, CH]) for i in range(2)]
        g1 = sb("g1_wide", [P, D])
        junk = [sb(f"x1_square_junk{i}", [P, D], BF16) for i in range(2)]
        ones, eps_col = sb("ones_col", [P, 1]), sb("eps_col4", [P, 1])
        newton, msq_r = sb("newton4", [P, NB]), sb("rnn_msq", [P, 1])
        rstd_a, rstd_r, ssq2 = sb("rstd_attn", [P, NB]), [sb(f"rstd_rnn{i}", [P, 1]) for i in range(2)], sb("ssq2", [P, NB])

        s_gain = k.sem("gains_landed")
        s_gainT = k.sem("gains_transposed")
        s_gainc = k.sem("gain_cols_ready")
        s_const = k.sem("out_constants_ready")
        s_w = [k.sem(f"wout_landed{i}") for i in range(2)]
        s_ws = k.sem("wout_scaled")
        s_whi = k.sem("wout_hi_ready")
        s_wlo = k.sem("wout_lo_ready")
        s_mix = [k.sem(f"rnn_landed{i}") for i in range(2)]
        s_att = [k.sem(f"att_landed{i}") for i in range(2)]
        s_turn = k.sem("att_turned")
        s_ahi = k.sem("att_hi_ready")
        s_alo = k.sem("att_lo_ready")
        s_root = k.sem("mixer_rsqrt_refined")
        s_x = [k.sem(f"x_in_landed{i}") for i in range(2)]
        s_g1 = k.sem("g1_landed")
        s_hi = k.sem("rnn_hi_ready")
        s_lo = k.sem("rnn_lo_ready")
        s_sq = k.sem("rnn_squared")
        s_sqs = k.sem("rnn_squares_summed")
        s_ss = k.sem("rnn_sumsq_ready")
        s_std = k.sem("rnn_std_ready")
        s_rstd = k.sem("rnn_rstd_ready")
        s_rstda = k.sem("attn_rstd_ready")
        s_acc = k.sem("out_accumulated")
        s_part = k.sem("rnn_part_ready")
        s_mid = k.sem("parts_joined")
        s_gated = k.sem("mixer_gated")
        s_x1 = k.sem("x1_ready")
        s_ss2 = k.sem("x1_squared")
        s_x1st = k.sem("x1_stored")

        SS_BANK, TURN_BANK = 4, 6

        with nc.Block() as block:

            @block.sync
            def _(sp):
                sp.dma_start(gain_rows[0:RNN_TILES, :], a["gn_rnn"].rearrange("a (k p) -> (a k) p", p=P)).then_inc(s_gain, 16)
                sp.dma_start(gain_rows[RNN_TILES:KD, :], a["gn_attn"].rearrange("a (k p) -> (a k) p", p=P)).then_inc(s_gain, 16)

                def load(n, s):
                    sp.wait_ge(s_lo, n + 1)
                    sp.wait_ge(s_sq, n + 1)
                    sp.dma_start(rnn[s][:], scratch["mix"][:, ds(n * P, P)].rearrange("(k p) t -> p k t", p=P)).then_inc(s_mix[s], 16)
                    sp.wait_ge(s_turn, n + 1)
                    sp.dma_start(att[s][:], scratch["att"][ds(n * P, P), :]).then_inc(s_att[s], 16)
                    sp.wait_ge(s_x1, n + 1)
                    sp.dma_start(x_in[s][:], a["x"][0, ds(n * P, P), :]).then_inc(s_x[s], 16)

                def store(n):
                    sp.wait_ge(s_x1, n + 3)
                    sp.dma_start(scratch["x1"][ds(n * P, P), :], x1[:, ds(n, 1), :].rearrange("p o d -> p (o d)")).then_inc(s_x1st, 16)

                for kt in range(KD):
                    sp.wait_ge(s_wlo, kt + 1)
                    sp.dma_start(w_raw[kt % 2][:], a["w_out"][0, kt * P:(kt + 1) * P, :]).then_inc(s_w[kt % 2], 16)
                    if kt == 1:
                        load(0, 0)
                        load(1, 1)
                        sp.dma_start(g1[:], scratch["mod"][0:1, 2 * D:3 * D].broadcast_to([P, D])).then_inc(s_g1, 16)
                with sp.Fori(0, NB // 2 - 1) as i:
                    for s in range(2):
                        load(i * 2 + s + 2, s)
                        store(i * 2 + s)
                store(NB - 2)
                store(NB - 1)
                sp.wait_ge(s_x1st, 16 * NB)

            @block.gpsimd
            def _(pool):
                nc.gpsimd.memset(ones[:], 1.0).then_inc(s_const, 1)
                nc.gpsimd.memset(eps_col[:], EPS).then_inc(s_const, 1)

                def cut(n, s):
                    pool.wait_ge(s_hi, n + 1)
                    nc.gpsimd.tensor_tensor(mix_lo[s][:, 0:RNN_TILES, :], rnn[s][:], mix_hi[s][:, 0:RNN_TILES, :].bitcast(F32), ALU.subtract).then_inc(s_lo, 1)

                def residual(n, s, turn):
                    pool.wait_ge(s_x[s], turn * 16 + 16)
                    pool.wait_ge(s_gated, n + 1)
                    tile = x1[:, ds(n, 1), :].rearrange("p o d -> p (o d)")
                    nc.gpsimd.tensor_tensor(tile, tile, x_in[s][:], ALU.add).then_inc(s_x1, 1)

                cut(0, 0)
                with pool.Fori(0, NB // 2 - 1) as i:
                    cut(i * 2 + 1, 1)
                    residual(i * 2, 0, i)
                    cut(i * 2 + 2, 0)
                    residual(i * 2 + 1, 1, i)
                cut(NB - 1, 1)
                residual(NB - 2, 0, NB // 2 - 1)
                residual(NB - 1, 1, NB // 2 - 1)

            @block.scalar
            def _(act):
                act.sem_inc(s_wlo, 2)
                act.sem_inc(s_lo, 2)
                act.sem_inc(s_sq, 2)
                act.sem_inc(s_x1, 2)
                act.sem_inc(s_acc, 4)
                act.sem_inc(s_turn, 2)
                act.sem_inc(s_alo, 2)
                act.sem_inc(s_mid, 2)
                act.sem_inc(s_sqs, 1)
                act.sem_inc(s_ss, 1)
                act.wait_ge(s_const, 2)
                act.activation(rstd_a[:], keep["msq_attn"][:], ACT.Sqrt).then_inc(s_rstda, 1)

                def cut(n, s, turn):
                    act.wait_ge(s_mix[s], turn * 16 + 16)
                    act.wait_ge(s_acc, n * 2 + 2)
                    act.activation(mix_hi[s][:, 0:RNN_TILES, :], rnn[s][:], ACT.Copy).then_inc(s_hi, 1)
                    act.wait_ge(s_sqs, n + 1)
                    act.activation(square[:], rnn[s][:], ACT.Square).then_inc(s_sq, 1)
                    act.wait_ge(s_turn, n + 3)
                    act.activation(mix_hi[s][:, RNN_TILES:KD, :].rearrange("p k t -> p (k t)"), psum[:, TURN_BANK + s, :], ACT.Copy).then_inc(s_ahi, 1)

                def finish(n, s):
                    act.wait_ge(s_ss, n + 2)
                    act.activation(rstd_r[s][:], psum[:, SS_BANK + s, 0:1], ACT.Sqrt, bias=eps_col[:], scale=1.0 / D_RNN).then_inc(s_std, 1)
                    act.wait_ge(s_root, n * 4 + 8)
                    for half in range(2):
                        act.wait_ge(s_acc, n * 2 + half + 5)
                        act.activation(part[half][:], psum[:, 2 * half, :], ACT.Copy, scale=rstd_r[s][:]).then_inc(s_part, 1)

                def square_x1(n, s):
                    act.wait_ge(s_x1, n + 3)
                    act.activation(junk[s][:], x1[:, ds(n, 1), :].rearrange("p o d -> p (o d)"), ACT.Square, accum_out=ssq2[:, ds(n, 1)]).then_inc(s_ss2, 1)

                cut(0, 0, 0)
                act.wait_ge(s_gainc, 1)
                for kt in range(KD):
                    act.wait_ge(s_w[kt % 2], (kt // 2) * 16 + 16)
                    act.activation(w_raw[kt % 2][:], w_raw[kt % 2][:], ACT.Copy, scale=gain[:, kt:kt + 1]).then_inc(s_ws, 1)
                    act.wait_ge(s_ws, kt + 1)
                    act.activation(w_hi[:, kt, :], w_raw[kt % 2][:], ACT.Copy).then_inc(s_whi, 1)
                cut(1, 1, 0)
                finish(0, 0)
                with act.Fori(0, NB // 2 - 1) as i:
                    cut(i * 2 + 2, 0, i + 1)
                    finish(i * 2 + 1, 1)
                    square_x1(i * 2, 0)
                    cut(i * 2 + 3, 1, i + 1)
                    finish(i * 2 + 2, 0)
                    square_x1(i * 2 + 1, 1)
                finish(NB - 1, 1)
                square_x1(NB - 2, 0)
                square_x1(NB - 1, 1)
                act.wait_ge(s_ss2, NB)
                act.activation(rstd2[:], ssq2[:], ACT.Sqrt, bias=eps_col[:], scale=1.0 / D).then_inc(s_ss2, 1)

            @block.tensor
            def _(pe):
                pe.wait_ge(s_gain, 32)
                pe.transpose(psum[:, SS_BANK, 0:KD], gain_rows[:], keep["ident"][0:KD, 0:KD]).then_inc(s_gainT, 1)

                def turn(n, s, turn_count):
                    pe.wait_ge(s_att[s], turn_count * 16 + 16)
                    pe.wait_ge(s_alo, n + 1)
                    for f in range(KD - RNN_TILES):
                        tp = pe.transpose(psum[:, TURN_BANK + s, f * P:(f + 1) * P], att[s][:, f * P:(f + 1) * P], keep["ident"][:])
                    tp.then_inc(s_turn, 1)

                def tile(n, s, first):
                    pe.wait_ge(s_sqs, n + 2)
                    if first:
                        pe.wait_ge(s_gainc, 1)
                        pe.wait_ge(s_const, 2)
                    pe.matmul(psum[:, SS_BANK + s, 0:1], square_sum[:], ones[:], start=True, stop=True).then_inc(s_ss, 1)
                    pe.wait_ge(s_lo, n + 3)
                    pe.wait_ge(s_alo, n + 3)
                    for half in range(2):
                        pe.wait_ge(s_mid, n * 2 + half + 1)
                        for group in range(2):
                            for kt in range(group * RNN_TILES, (group + 1) * RNN_TILES):
                                if first and half == 0:
                                    pe.wait_ge(s_wlo, kt + 3)
                                at, end = kt == group * RNN_TILES, kt == (group + 1) * RNN_TILES - 1
                                cols = slice(half * CH, (half + 1) * CH)
                                pe.matmul(psum[:, 2 * half + group, :], mix_hi[s][:, kt, :], w_hi[:, kt, cols], start=at, stop=False)
                                pe.matmul(psum[:, 2 * half + group, :], mix_hi[s][:, kt, :], w_lo[:, kt, cols], start=False, stop=False)
                                mm = pe.matmul(psum[:, 2 * half + group, :], mix_lo[s][:, kt, :], w_hi[:, kt, cols], start=False, stop=end)
                        mm.then_inc(s_acc, 1)

                turn(0, 0, 0)
                turn(1, 1, 0)
                tile(0, 0, True)
                with pe.Fori(0, NB // 2 - 1) as i:
                    turn(i * 2 + 2, 0, i + 1)
                    tile(i * 2 + 1, 1, False)
                    turn(i * 2 + 3, 1, i + 1)
                    tile(i * 2 + 2, 0, False)
                tile(NB - 1, 1, False)

            @block.vector
            def _(dve):
                dve.wait_ge(s_gainT, 1)
                dve.tensor_copy(gain[:], psum[:, SS_BANK, 0:KD]).then_inc(s_gainc, 1)
                dve.wait_ge(s_rstda, 1)
                dve.reciprocal(rstd_a[:], rstd_a[:]).then_inc(s_rstda, 1)
                dve.wait_ge(s_rstda, 2)
                refine_rsqrt(dve, rstd_a[:], keep["msq_attn"][:], newton[:], s_root, 0)

                def cut(n, s):
                    dve.wait_ge(s_ahi, n + 1)
                    hi = mix_hi[s][:, RNN_TILES:KD, :].rearrange("p k t -> p (k t)")
                    dve.tensor_tensor(mix_lo[s][:, RNN_TILES:KD, :].rearrange("p k t -> p (k t)"), psum[:, TURN_BANK + s, :], hi.bitcast(F32), ALU.subtract).then_inc(s_alo, 1)

                def sum_squares(n):
                    dve.wait_ge(s_sq, n + 3)
                    dve.wait_ge(s_ss, n + 1)
                    dve.tensor_reduce(square_sum[:], square[:].rearrange("p f t -> p t f"), AX_X, ALU.add).then_inc(s_sqs, 1)

                def finish(n, s):
                    dve.wait_ge(s_std, n + 1)
                    dve.tensor_scalar(msq_r[:], psum[:, SS_BANK + s, 0:1], 1.0 / D_RNN, EPS, ALU.mult, ALU.add).then_inc(s_rstd, 1)
                    dve.reciprocal(rstd_r[s][:], rstd_r[s][:]).then_inc(s_rstd, 1)
                    dve.wait_ge(s_rstd, n * 2 + 2)
                    refine_rsqrt(dve, rstd_r[s][:], msq_r[:], newton[:, 0:1], s_root, n * 4 + 4)
                    for half in range(2):
                        dve.wait_ge(s_part, n * 2 + half + 1)
                        dve.scalar_tensor_tensor(x1[:, ds(n, 1), half * CH:(half + 1) * CH].rearrange("p o d -> p (o d)"), psum[:, 2 * half + 1, :],
                                                 rstd_a[:, ds(n, 1)], part[half][:], ALU.mult, ALU.add).then_inc(s_mid, 1)
                    dve.wait_ge(s_mid, n * 2 + 4)
                    tile = x1[:, ds(n, 1), :].rearrange("p o d -> p (o d)")
                    dve.tensor_tensor(tile, tile, g1[:], ALU.mult).then_inc(s_gated, 1)

                sum_squares(0)
                cut(0, 0)
                for kt in range(KD):
                    dve.wait_ge(s_whi, kt + 1)
                    dve.tensor_tensor(w_lo[:, kt, :], w_raw[kt % 2][:], w_hi[:, kt, :].bitcast(F32), ALU.subtract).then_inc(s_wlo, 1)
                sum_squares(1)
                cut(1, 1)
                dve.wait_ge(s_g1, 16)
                finish(0, 0)
                with dve.Fori(0, NB // 2 - 1) as i:
                    sum_squares(i * 2 + 2)
                    cut(i * 2 + 2, 0)
                    finish(i * 2 + 1, 1)
                    sum_squares(i * 2 + 3)
                    cut(i * 2 + 3, 1)
                    finish(i * 2 + 2, 0)
                finish(NB - 1, 1)
                dve.wait_ge(s_ss2, NB + 1)
                dve.reciprocal(rstd2[:], rstd2[:]).then_inc(s_rstda, 1)
                dve.tensor_scalar(ssq2[:], ssq2[:], 1.0 / D, EPS, ALU.mult, ALU.add).then_inc(s_rstda, 1)
                dve.wait_ge(s_rstda, 4)
                refine_rsqrt(dve, rstd2[:], ssq2[:], newton[:], s_root, 4 + 4 * NB)


def modulate_x1(k, x1, rstd2, h2T_hi, h2T_lo, keep):
    nc, psum = k.nc, k.psum
    ident, aff2 = keep["ident"], keep["aff2"]
    QUADS = NB // 4
    with ExitStack() as ctx:
        xn = [ctx.enter_context(nc.sbuf_tensor(f"x1_norm{i}", [P, 4, 2 * P], F32)) for i in range(2)]
        t32 = [ctx.enter_context(nc.sbuf_tensor(f"t2_{i}", [P, CH], F32)) for i in range(2)]
        s_xn = k.sem("x1_normalised")
        s_tp = k.sem("x1_transposed")
        s_t32 = k.sem("x1_modulated")
        s_hi = k.sem("h2T_hi_ready")
        s_lo = k.sem("h2T_lo_ready")

        with nc.Block() as block:

            @block.gpsimd
            def _(pool):
                with pool.Fori(0, QUADS) as q:
                    for pair in range(KD // 2):
                        pool.wait_ge(s_tp, q * KD + pair * 2 + 2)
                        nc.gpsimd.tensor_tensor(xn[pair % 2][:], x1[:, ds(q * 4, 4), pair * 2 * P:(pair + 1) * 2 * P],
                                                rstd2[:, ds(q * 4, 4)].rearrange("p (n o) -> p n o", o=1).broadcast_to([P, 4, 2 * P]), ALU.mult).then_inc(s_xn, 1)

            @block.tensor
            def _(pe):
                with pe.Fori(0, QUADS) as q:
                    for kt in range(KD):
                        pe.wait_ge(s_xn, q * (KD // 2) + kt // 2 + 1)
                        pe.wait_ge(s_t32, q * KD + kt + 1)
                        for j in range(4):
                            tp = pe.transpose(psum[:, kt, j * P:(j + 1) * P], xn[kt // 2 % 2][:, j, (kt % 2) * P:(kt % 2 + 1) * P], ident[:])
                        tp.then_inc(s_tp, 1)

            @block.scalar
            def _(act):
                act.sem_inc(s_t32, KD)
                act.sem_inc(s_tp, 4)
                act.sem_inc(s_lo, 2)
                with act.Fori(0, QUADS) as q:
                    for kt in range(KD):
                        act.wait_ge(s_tp, q * KD + kt + 5)
                        act.wait_ge(s_lo, q * KD + kt + 1)
                        act.activation(t32[kt % 2][:], psum[:, kt, :], ACT.Identity, bias=aff2[:, 1, kt:kt + 1], scale=aff2[:, 0, kt:kt + 1]).then_inc(s_t32, 1)

            @block.vector
            def _(dve):
                with dve.Fori(0, QUADS) as q:
                    for kt in range(KD):
                        dve.wait_ge(s_t32, q * KD + kt + 1 + KD)
                        hi = h2T_hi[:, kt, ds(q * CH, CH)]
                        dve.tensor_copy(hi, t32[kt % 2][:]).then_inc(s_hi, 1)
                        dve.wait_ge(s_hi, q * KD + kt + 1)
                        dve.tensor_tensor(h2T_lo[:, kt, ds(q * CH, CH)], t32[kt % 2][:], hi.bitcast(F32), ALU.subtract).then_inc(s_lo, 1)


def up_projection(k, a, h2T_hi, h2T_lo, keep, scratch):
    nc, psum = k.nc, k.psum
    with ExitStack() as ctx:
        def sb(name, shape, dt=F32):
            return ctx.enter_context(nc.sbuf_tensor(name, shape, dt))

        w_raw = [sb(f"wup_raw{g}", [P, KD, P]) for g in range(2)]
        w_hi = [sb(f"wup_hi{g}", [P, KD, P], F32R) for g in range(2)]
        w_lo = [sb(f"wup_lo{g}", [P, KD, P], F32R) for g in range(2)]
        u_pad = [sb(f"u_pad{g}", [P, S + 2]) for g in range(2)]
        acc = [sb(f"conv_acc{g}", [P, S]) for g in range(2)]
        act_out = [sb(f"act_out{i}", [P, S]) for i in range(2)]
        par_rows = [sb(f"conv_rows{i}", [4 * FT, P]) for i in range(2)]
        par = sb("conv_cols", [P, 8 * FT])

        s_par = k.sem("conv_params_landed")
        s_parT = k.sem("conv_params_transposed")
        s_parc = k.sem("conv_cols_ready")
        s_pad = k.sem("pad_columns_ready")
        s_w = [k.sem(f"wup_landed{g}") for g in range(2)]
        s_whi = k.sem("wup_hi_ready")
        s_wlo = k.sem("wup_lo_ready")
        s_mm = k.sem("up_accumulated")
        s_evac = k.sem("up_evacuated")
        s_tap = k.sem("conv_tap_added")
        s_conv = k.sem("conv_ready")
        s_silu = k.sem("gate_silu_ready")
        s_prod = k.sem("act_ready")
        s_stored = [k.sem(f"act_stored{i}") for i in range(2)]

        with nc.Block() as block:

            @block.sync
            def _(sp):
                sp.sem_inc(s_stored[0], 16)
                sp.sem_inc(s_stored[1], 16)

                def load(j, g):
                    sp.wait_ge(s_wlo, j * 2 + g + 1)
                    sp.dma_start(w_raw[g][:], a["w_up"][0, :, ds(j * P + g * D_FF, P)].rearrange("(k p) n -> p k n", p=P)).then_inc(s_w[g], 16)

                def store(j, i):
                    sp.wait_ge(s_prod, j + 2)
                    sp.dma_start(scratch["act"][:, :, ds(j, 1), :].rearrange("n p o t -> p (n o) t"),
                                 act_out[i][:].rearrange("p (n t) -> p n t", t=P)).then_inc(s_stored[i], 16)

                load(0, 0)
                load(0, 1)
                for i in range(2):
                    for half in range(2):
                        src = a["ffn_conv_b"] if (i, half) == (1, 1) else a["ffn_conv_w"][:, 2 * i + half, :]
                        sp.dma_start(par_rows[i][half * 2 * FT:(half + 1) * 2 * FT, :], src.rearrange("a (t p) -> (a t) p", p=P)).then_inc(s_par, 16)
                with sp.Fori(0, FT // 2 - 1) as i:
                    for m in range(2):
                        load(i * 2 + m + 1, 0)
                        load(i * 2 + m + 1, 1)
                        store(i * 2 + m, m)
                load(FT - 1, 0)
                load(FT - 1, 1)
                store(FT - 2, 0)
                store(FT - 1, 1)
                for i in range(2):
                    sp.wait_ge(s_stored[i], 16 + 16 * (FT // 2))

            @block.gpsimd
            def _(pool):
                with pool.Fori(0, FT) as j:
                    for g in range(2):
                        pool.wait_ge(s_whi, j * 2 + g + 1)
                        nc.gpsimd.tensor_tensor(w_lo[g][:], w_raw[g][:], w_hi[g][:].bitcast(F32), ALU.subtract).then_inc(s_wlo, 1)

            @block.scalar
            def _(act):
                act.sem_inc(s_wlo, 2)
                act.sem_inc(s_evac, 8)
                act.sem_inc(s_conv, 2)
                act.sem_inc(s_prod, 1)

                def cut(j, g):
                    act.wait_ge(s_w[g], j * 16 + 16)
                    act.activation(w_hi[g][:], w_raw[g][:], ACT.Copy).then_inc(s_whi, 1)

                def evacuate(j, g, c):
                    act.wait_ge(s_mm, j * 8 + g * 4 + c + 1)
                    if c == 0:
                        act.wait_ge(s_conv, j * 2 + g + 1)
                    act.activation(u_pad[g][:, 1 + c * CH:1 + (c + 1) * CH], psum[:, 4 * g + c, :], ACT.Copy).then_inc(s_evac, 1)

                def silu(j):
                    act.wait_ge(s_conv, j * 2 + 3)
                    act.activation(acc[0][:], acc[0][:], ACT.Silu).then_inc(s_silu, 1)

                def channels(j, last):
                    cut(j, 1)
                    for c in range(NCH):
                        evacuate(j, 0, c)
                    if not last:
                        cut(j + 1, 0)
                    evacuate(j, 1, 0)
                    evacuate(j, 1, 1)
                    silu(j)
                    evacuate(j, 1, 2)
                    evacuate(j, 1, 3)

                cut(0, 0)
                with act.Fori(0, FT - 1) as j:
                    channels(j, False)
                channels(FT - 1, True)

            @block.tensor
            def _(pe):
                pe.wait_ge(s_par, 64)
                for i in range(2):
                    tp = pe.transpose(psum[:, 7, i * 4 * FT:(i + 1) * 4 * FT], par_rows[i][:], keep["ident"][0:4 * FT, 0:4 * FT])
                tp.then_inc(s_parT, 1)
                pe.wait_ge(s_parc, 1)
                with pe.Fori(0, FT) as j:
                    for g in range(2):
                        pe.wait_ge(s_wlo, j * 2 + g + 3)
                        for c in range(NCH):
                            pe.wait_ge(s_evac, j * 8 + g * 4 + c + 1)
                            bank, cols = psum[:, 4 * g + c, :], slice(c * CH, (c + 1) * CH)
                            for kt in range(KD):
                                pe.matmul(bank, w_hi[g][:, kt, :], h2T_hi[:, kt, cols], start=(kt == 0), stop=False)
                                pe.matmul(bank, w_hi[g][:, kt, :], h2T_lo[:, kt, cols], start=False, stop=False)
                                mm = pe.matmul(bank, w_lo[g][:, kt, :], h2T_hi[:, kt, cols], start=False, stop=(kt == KD - 1))
                            mm.then_inc(s_mm, 1)

            @block.vector
            def _(dve):
                for g in range(2):
                    for at in (0, S + 1):
                        dve.memset(u_pad[g][:, at:at + 1], 0.0).then_inc(s_pad, 1)
                dve.wait_ge(s_parT, 1)
                dve.tensor_copy(par[:], psum[:, 7, 0:8 * FT]).then_inc(s_parc, 1)
                dve.wait_ge(s_parc, 1)
                dve.wait_ge(s_pad, 4)

                def col(which, j, g):
                    return par[:, ds(j + which * 2 * FT + g * FT, 1)]

                def convolve(j, g):
                    dve.wait_ge(s_evac, j * 8 + g * 4 + 12)
                    dve.wait_ge(s_prod, j + 1)
                    dve.tensor_scalar(acc[g][:], u_pad[g][:, 1:S + 1], col(1, j, g), col(3, j, g), ALU.mult, ALU.add).then_inc(s_tap, 1)
                    dve.wait_ge(s_tap, j * 4 + g * 2 + 1)
                    dve.scalar_tensor_tensor(acc[g][:], u_pad[g][:, 0:S], col(0, j, g), acc[g][:], ALU.mult, ALU.add).then_inc(s_tap, 1)
                    dve.wait_ge(s_tap, j * 4 + g * 2 + 2)
                    dve.scalar_tensor_tensor(acc[g][:], u_pad[g][:, 2:S + 2], col(2, j, g), acc[g][:], ALU.mult, ALU.add).then_inc(s_conv, 1)

                with dve.Fori(0, FT // 2) as i:
                    for m in range(2):
                        j = i * 2 + m
                        convolve(j, 0)
                        convolve(j, 1)
                        dve.wait_ge(s_silu, j + 1)
                        dve.wait_ge(s_conv, j * 2 + 4)
                        dve.wait_ge(s_stored[m], i * 16 + 16)
                        dve.tensor_tensor(act_out[m][:], acc[0][:], acc[1][:], ALU.mult).then_inc(s_prod, 1)


def down_projection(k, a, out, scratch):
    nc, psum = k.nc, k.psum
    with ExitStack() as ctx:
        def sb(name, shape, dt=F32):
            return ctx.enter_context(nc.sbuf_tensor(name, shape, dt))

        w_raw = [sb(f"wdown_raw{i}", [P, CH]) for i in range(2)]
        w_hi, w_lo = sb("wdown_hi", [P, FT, CH], F32R), sb("wdown_lo", [P, FT, CH], F32R)
        a_raw = [sb(f"act_raw{i}", [P, FT, P]) for i in range(2)]
        a_hi = [sb(f"act_hi{i}", [P, FT, P], F32R) for i in range(2)]
        a_lo = [sb(f"act_lo{i}", [P, FT, P], F32R) for i in range(2)]
        x2_left = sb("x2_left", [P, NB, CH])
        x2_right = [sb(f"x2_right{i}", [P, CH]) for i in range(2)]
        gated = sb("gated", [P, CH])
        g2, final_g = sb("g2_wide", [P, D]), sb("final_g_wide", [P, D])
        junk = [sb(f"x2_junk{i}", [P, CH], BF16) for i in range(2)]
        ssq = [sb(f"x2_ssq{half}", [P, NB]) for half in range(2)]
        rstd, msq = ([sb(f"x2_{n}{i}", [P, 1]) for i in range(2)] for n in ("rstd", "msq"))
        newton = sb("newton7", [P, 1])

        s_wide = k.sem("wide_vectors_landed")
        s_left = k.sem("x1_left_landed")
        s_right = [k.sem(f"x1_right_landed{i}") for i in range(2)]
        s_w = [k.sem(f"wdown_landed{i}") for i in range(2)]
        s_whi = k.sem("wdown_hi_ready")
        s_wlo = k.sem("wdown_lo_ready")
        s_a = [k.sem(f"act_landed{i}") for i in range(2)]
        s_hi = k.sem("act_hi_ready")
        s_lo = k.sem("act_lo_ready")
        s_mm = k.sem("down_accumulated")
        s_gated = k.sem("ffn_gated")
        s_x2 = k.sem("x2_ready")
        s_sq = k.sem("x2_squared")
        s_msq = k.sem("x2_mean_square_step")
        s_root = k.sem("x2_rsqrt_refined")
        s_std = k.sem("x2_std_ready")
        s_rstd = k.sem("x2_rstd_ready")
        s_out = k.sem("out_ready")
        s_stored = [k.sem(f"out_stored{i}") for i in range(2)]

        with nc.Block() as block:

            @block.sync
            def _(sp):
                sp.sem_inc(s_stored[0], 32)
                sp.sem_inc(s_stored[1], 32)

                def load(u, n, s):
                    sp.wait_ge(s_lo, u + 1)
                    sp.dma_start(a_raw[s][:], scratch["act"][ds(n, 1)].rearrange("o p k t -> p (o k) t")).then_inc(s_a[s], 16)

                def weights(half, first, last):
                    for kt in range(first, last):
                        sp.wait_ge(s_wlo, half * FT + kt + 1)
                        sp.dma_start(w_raw[kt % 2][:], a["w_down"][0, kt * P:(kt + 1) * P, half * CH:(half + 1) * CH]).then_inc(s_w[kt % 2], 16)

                load(0, 0, 0)
                weights(0, 0, 2)
                load(1, 1, 1)
                weights(0, 2, FT)
                for half, t in ((0, g2), (1, final_g)):
                    src = scratch["mod"][0:1, 5 * D:6 * D] if t is g2 else a["final_g"].rearrange("(o d) -> o d", o=1)
                    sp.dma_start(t[:], src.broadcast_to([P, D])).then_inc(s_wide, 16)
                sp.dma_start(x2_left[:], scratch["x1"][:, 0:CH].rearrange("(n p) d -> p n d", p=P)).then_inc(s_left, 16)
                with sp.Fori(0, NB // 2 - 1) as i:
                    for s in range(2):
                        load(i * 2 + s + 2, i * 2 + s + 2, s)
                for s in range(2):
                    load(NB + s, s, s)
                    sp.dma_start(x2_right[s][:], scratch["x1"][s * P:(s + 1) * P, CH:D]).then_inc(s_right[s], 16)
                weights(1, 0, FT)

                def store(n, s):
                    sp.wait_ge(s_out, n * 2 + 2)
                    sp.dma_start(out[0, ds(n * P, P), 0:CH], x2_left[:, ds(n, 1), :].rearrange("p o d -> p (o d)")).then_inc(s_stored[s], 16)
                    sp.dma_start(out[0, ds(n * P, P), CH:D], x2_right[s][:]).then_inc(s_stored[s], 16)

                with sp.Fori(0, NB // 2 - 1) as i:
                    for s in range(2):
                        load(i * 2 + s + NB + 2, i * 2 + s + 2, s)
                        store(i * 2 + s, s)
                        sp.wait_ge(s_stored[s], i * 32 + 64)
                        sp.dma_start(x2_right[s][:], scratch["x1"][ds(i * 2 * P + (s + 2) * P, P), CH:D]).then_inc(s_right[s], 16)
                for s in range(2):
                    store(NB - 2 + s, s)
                for s in range(2):
                    sp.wait_ge(s_stored[s], 32 + 32 * (NB // 2))

            @block.scalar
            def _(act):
                act.sem_inc(s_lo, 2)
                act.sem_inc(s_wlo, 2)
                act.sem_inc(s_mm, 2)

                def cut(u, s, turn):
                    act.wait_ge(s_a[s], turn * 16 + 16)
                    act.wait_ge(s_mm, u + 1)
                    act.activation(a_hi[s][:], a_raw[s][:], ACT.Copy).then_inc(s_hi, 1)

                def cut_weights(half):
                    if half:
                        act.wait_ge(s_mm, NB + 2)
                    for kt in range(FT):
                        act.wait_ge(s_w[kt % 2], (half * FT + kt) // 2 * 16 + 16)
                        act.activation(w_hi[:, kt, :], w_raw[kt % 2][:], ACT.Copy).then_inc(s_whi, 1)

                def square_left(n, s):
                    act.wait_ge(s_x2, n + 2)
                    act.activation(junk[s][:], x2_left[:, ds(n, 1), :].rearrange("p o d -> p (o d)"), ACT.Square, accum_out=ssq[0][:, ds(n, 1)]).then_inc(s_sq, 1)

                def square_right(n, s):
                    act.wait_ge(s_x2, n + NB + 2)
                    act.activation(junk[s][:], x2_right[s][:], ACT.Square, accum_out=ssq[1][:, ds(n, 1)]).then_inc(s_sq, 1)
                    act.wait_ge(s_msq, n * 2 + 2)
                    act.activation(rstd[s][:], msq[s][:], ACT.Sqrt).then_inc(s_std, 1)

                cut(0, 0, 0)
                cut_weights(0)
                cut(1, 1, 0)
                with act.Fori(0, NB // 2 - 1) as i:
                    for s in range(2):
                        cut(i * 2 + s + 2, s, i + 1)
                        square_left(i * 2 + s, s)
                cut(NB, 0, NB // 2)
                square_left(NB - 2, 0)
                cut_weights(1)
                cut(NB + 1, 1, NB // 2)
                square_left(NB - 1, 1)
                with act.Fori(0, NB // 2 - 1) as i:
                    for s in range(2):
                        cut(i * 2 + s + NB + 2, s, i + NB // 2 + 1)
                        square_right(i * 2 + s, s)
                square_right(NB - 2, 0)
                square_right(NB - 1, 1)

            @block.tensor
            def _(pe):
                def tile(u, s, bank, first):
                    pe.wait_ge(s_gated, u + 1)
                    pe.wait_ge(s_lo, u + 3)
                    for kt in range(FT):
                        if first:
                            pe.wait_ge(s_wlo, (u // NB) * FT + kt + 3)
                        pe.matmul(psum[:, bank, :], a_hi[s][:, kt, :], w_hi[:, kt, :], start=(kt == 0), stop=False)
                        pe.matmul(psum[:, bank, :], a_hi[s][:, kt, :], w_lo[:, kt, :], start=False, stop=False)
                        mm = pe.matmul(psum[:, bank, :], a_lo[s][:, kt, :], w_hi[:, kt, :], start=False, stop=(kt == FT - 1))
                    mm.then_inc(s_mm, 1)

                for half in range(2):
                    tile(half * NB, 0, 0, True)
                    with pe.Fori(half * NB // 2, (half + 1) * NB // 2 - 1) as i:
                        tile(i * 2 + 1, 1, 1, False)
                        tile(i * 2 + 2, 0, 0, False)
                    tile(half * NB + NB - 1, 1, 1, False)

            @block.vector
            def _(dve):
                dve.sem_inc(s_gated, 2)
                dve.sem_inc(s_x2, 1)

                def cut(u, s):
                    dve.wait_ge(s_hi, u + 1)
                    dve.tensor_tensor(a_lo[s][:], a_raw[s][:], a_hi[s][:].bitcast(F32), ALU.subtract).then_inc(s_lo, 1)

                def cut_weights(half):
                    for kt in range(FT):
                        dve.wait_ge(s_whi, half * FT + kt + 1)
                        dve.tensor_tensor(w_lo[:, kt, :], w_raw[kt % 2][:], w_hi[:, kt, :].bitcast(F32), ALU.subtract).then_inc(s_wlo, 1)

                def residual(u, half, bank, x2):
                    dve.wait_ge(s_mm, u + 3)
                    dve.wait_ge(s_x2, u + 1)
                    dve.tensor_tensor(gated[:], psum[:, bank, :], g2[:, half * CH:(half + 1) * CH], ALU.mult).then_inc(s_gated, 1)
                    dve.wait_ge(s_gated, u + 3)
                    dve.tensor_tensor(x2, x2, gated[:], ALU.add).then_inc(s_x2, 1)

                def left(n, s):
                    residual(n, 0, s, x2_left[:, ds(n, 1), :].rearrange("p o d -> p (o d)"))

                def right(n, s, turn):
                    dve.wait_ge(s_right[s], turn * 16 + 16)
                    residual(n + NB, 1, s, x2_right[s][:])

                def finish(n, s):
                    dve.wait_ge(s_sq, n + NB + 1)
                    dve.tensor_tensor(msq[s][:], ssq[0][:, ds(n, 1)], ssq[1][:, ds(n, 1)], ALU.add).then_inc(s_msq, 1)
                    dve.wait_ge(s_msq, n * 2 + 1)
                    dve.tensor_scalar(msq[s][:], msq[s][:], 1.0 / D, EPS, ALU.mult, ALU.add).then_inc(s_msq, 1)
                    dve.wait_ge(s_std, n + 1)
                    dve.reciprocal(rstd[s][:], rstd[s][:]).then_inc(s_rstd, 1)
                    dve.wait_ge(s_rstd, n + 1)
                    refine_rsqrt(dve, rstd[s][:], msq[s][:], newton[:], s_root, n * 4)
                    for tile, cols in ((x2_left[:, ds(n, 1), :].rearrange("p o d -> p (o d)"), slice(0, CH)), (x2_right[s][:], slice(CH, D))):
                        dve.scalar_tensor_tensor(tile, tile, rstd[s][:], final_g[:, cols], ALU.mult, ALU.mult).then_inc(s_out, 1)

                cut(0, 0)
                cut_weights(0)
                cut(1, 1)
                dve.wait_ge(s_wide, 32)
                dve.wait_ge(s_left, 16)
                with dve.Fori(0, NB // 2 - 1) as i:
                    for s in range(2):
                        left(i * 2 + s, s)
                        cut(i * 2 + s + 2, s)
                left(NB - 2, 0)
                cut(NB, 0)
                left(NB - 1, 1)
                cut_weights(1)
                cut(NB + 1, 1)
                with dve.Fori(0, NB // 2 - 1) as i:
                    for s in range(2):
                        right(i * 2 + s, s, i)
                        cut(i * 2 + s + NB + 2, s)
                        finish(i * 2 + s, s)
                for s in range(2):
                    right(NB - 2 + s, s, NB // 2 - 1)
                    finish(NB - 2 + s, s)


def build(nc, a, out):
    ctx = ExitStack()
    with ctx:
        k = Kit(nc, ctx)
        scratch = {n: k.dram(n, s, d) for n, s, d in (
            ("mod", [2, 6 * D], F32), ("xr", [D_RNN, T], F32), ("xg", [D_RNN, S], F32),
            ("qk_hi", [D_ATTN + N_KV * HEAD, T], F32), ("qk_lo", [D_ATTN + N_KV * HEAD, T], F32),
            ("v", [N_KV * HEAD, T], F32), ("mix", [D_RNN, S], F32), ("att", [S, D_ATTN], F32), ("x1", [S, D], F32), ("act", [NB, P, FT, P], F32))}
        keep = {n: k.keep(n, s, F32) for n, s in (
            ("ident", [P, P]), ("aff2", [P, 2, KD]), ("msq_attn", [P, NB]))}
        with ExitStack() as features:
            hT_hi, hT_lo = (features.enter_context(nc.sbuf_tensor(n, [P, KD, T], F32R)) for n in ("hT_hi", "hT_lo"))
            modulation_and_norm(k, a, hT_hi, hT_lo, keep, scratch)
            k.next_phase()
            input_projection(k, a, hT_hi, hT_lo, scratch)
            k.next_phase()
        mixers(k, a, keep, scratch)
        k.next_phase()
        rstd2 = k.keep("rstd2", [P, NB], F32)
        x1_life, h2T_life = ExitStack(), ExitStack()
        x1 = x1_life.enter_context(nc.sbuf_tensor("x1_tiles", [P, NB, D], F32, side="right"))
        output_projection(k, a, x1, rstd2, keep, scratch)
        k.next_phase()
        h2T_hi, h2T_lo = (h2T_life.enter_context(nc.sbuf_tensor(n, [P, KD, S], F32R)) for n in ("h2T_hi", "h2T_lo"))
        modulate_x1(k, x1, rstd2, h2T_hi, h2T_lo, keep)
        k.next_phase()
        x1_life.close()
        up_projection(k, a, h2T_hi, h2T_lo, keep, scratch)
        k.next_phase()
        h2T_life.close()
        down_projection(k, a, out, scratch)


_INS = ["x", "c", "ctx", "c_ctx", "w_mod", "b_mod", "norm1_g", "w_in", "rnn_conv_w", "rnn_conv_b", "lru_w_a", "lru_b_a",
        "lru_w_i", "lru_b_i", "lru_lam", "attn_sink", "gn_rnn", "gn_attn", "w_out", "norm2_g", "w_up", "ffn_conv_w",
        "ffn_conv_b", "w_down", "final_g"]


def shape_tables():
    half = HEAD // 4
    inv = ROPE_THETA ** (-np.arange(half, dtype=np.float32) / half)
    t = np.arange(S)
    pos = np.stack([t // GRID_W, t % GRID_W]).astype(np.float32)
    p = np.arange(P) % HEAD
    ang = (pos[p // (HEAD // 2)] * inv[p % half][:, None]).astype(np.float32)
    sign = np.where(p % (HEAD // 2) < half, -1.0, 1.0).astype(np.float32)[:, None]
    return {"rope_cos": np.cos(ang).astype(np.float32), "rope_sin": (sign * np.sin(ang)).astype(np.float32)}


def kernel(**inputs):
    import concourse.bacc as _bacc
    from concourse.bass_utils import run_bass_kernel_spmd as _run

    nc = _bacc.Bacc("TRN2", target_bir_lowering=False, num_devices=1)
    arrays, aps = {}, {}
    for name, value in [(n, inputs[n]) for n in _INS] + list(shape_tables().items()):
        v = np.ascontiguousarray(value)
        arrays[f"in_{name}"] = v
        aps[name] = nc.dram_tensor(f"in_{name}", v.shape, mybir.dt.from_np(v.dtype), kind="ExternalInput").ap()
    out = nc.dram_tensor("out", (1, S, D), F32, kind="ExternalOutput").ap()
    build(nc, aps, out)
    result = _run(nc, [arrays], core_ids=[0])
    return result.results[0]["out"]
```

```python
from contextlib import ExitStack

import numpy as np

import concourse.bass as bass
from concourse import mybir
from concourse.alu_op_type import AluOpType as ALU

F32 = mybir.dt.float32
F32R = mybir.dt.float32r
BF16 = mybir.dt.bfloat16
ACT = mybir.ActivationFunctionType
AX_X = mybir.AxisListType.X
ds = bass.ds

P = 128
D = 1024
KD = D // P
S = 2048
L = 256
T = S + L
GRID_W = 64
EPS = 1e-6
D_RNN = 512
RNN_TILES = D_RNN // P
D_ATTN = 512
HEAD = 64
N_HEADS = 8
N_KV = 2
PER_KV = N_HEADS // N_KV
SCALE = HEAD ** -0.5
ROPE_THETA = 10000.0
D_IN = 2 * D_RNN + D_ATTN + 2 * N_KV * HEAD
LRU_C = 8.0
D_FF = 2816
FT = D_FF // P
BQ = 128
NB = S // BQ
CH = 512
NCH = S // CH
NEG = -1e30
PAIRS = T // (2 * P)
MOD1 = 2 * D // CH
GELU_C = 2.0 * float(np.sqrt(2.0 / np.pi))
GELU_A = 0.044715


class Kit:

    def __init__(self, nc, ctx):
        self.nc, self.ctx = nc, ctx
        self.psum = ctx.enter_context(nc.psum_tensor("psum", [P, 8, CH], F32))
        self.phase_sems = []

    def sem(self, name):
        self.phase_sems.append(self.nc.alloc_semaphore(name))
        return self.phase_sems[-1]

    def overlaid(self, life, raw, lo):
        with self.nc.sbuf_tensor(*raw) as first:
            pass
        return first, life.enter_context(self.nc.sbuf_tensor(*lo))

    def next_phase(self):
        with self.nc.Block() as block:

            @block.gpsimd
            def _(pool):
                self.nc.clear_and_free_semaphores(self.phase_sems)

        self.phase_sems = []

    def dram(self, name, shape, dt):
        return self.nc.dram_tensor(name, shape, dt).ap()

    def keep(self, name, shape, dt):
        return self.ctx.enter_context(self.nc.sbuf_tensor(name, shape, dt))


def refine_rsqrt(dve, r, v, t, step, done):
    dve.tensor_tensor(t, r, r, ALU.mult).then_inc(step, 1)
    dve.wait_ge(step, done + 1)
    dve.tensor_tensor(t, t, v, ALU.mult).then_inc(step, 1)
    dve.wait_ge(step, done + 2)
    dve.tensor_scalar(t, t, -0.5, 1.5, ALU.mult, ALU.add).then_inc(step, 1)
    dve.wait_ge(step, done + 3)
    dve.tensor_tensor(r, r, t, ALU.mult).then_inc(step, 1)
    dve.wait_ge(step, done + 4)


def modulation_and_norm(k, a, hT_hi, hT_lo, x_raw, keep, scratch):
    nc, psum = k.nc, k.psum
    ident = keep["ident"]
    w_mod, b_mod, mod_rows = a["w_mod"], a["b_mod"], scratch["mod"]
    with ExitStack() as ctx:
        def sb(name, shape, dt=F32):
            return ctx.enter_context(nc.sbuf_tensor(name, shape, dt))

        w_slot = [sb(f"wmod{i}", [P, KD, CH]) for i in range(2)]
        row = [sb(f"mod_row{i}", [2, CH]) for i in range(2)]
        xn = [sb(f"xnorm{i}", [P, 2, D]) for i in range(2)]
        junk = [sb(f"square_junk{i}", [P, D], BF16) for i in range(2)]
        vec_rows = sb("vec_rows", [3 * KD, P])
        mod_rows_sb = sb("mod_rows_sb", [4 * KD, P])
        vec_cols = sb("vec_cols", [P, 3 * KD])
        mod_cols = sb("mod_cols", [P, 4 * KD])
        cond_silu = sb("cond_silu", [P, 2, KD])
        aff1 = sb("aff1", [P, 2, 2, KD])
        sumsq, rstd, eps_col = sb("sumsq", [P, 18]), sb("rstd", [P, 18]), sb("eps_col", [P, 1])
        t32 = [w_slot[0][:, kt, 0:2 * P] for kt in range(KD)]
        msq, newton = sb("msq", [P, 2]), sb("newton", [P, 2])

        s_vec = k.sem("vectors_landed")
        s_w = [k.sem(f"wmod_landed{i}") for i in range(2)]
        s_bias = [k.sem(f"bias_landed{i}") for i in range(2)]
        s_row_stored = [k.sem(f"mod_row_stored{i}") for i in range(2)]
        s_modrows = k.sem("mod_rows_landed")
        s_x = [k.sem(f"x_landed{i}") for i in range(2)]
        s_ident = k.sem("ident_ready")
        s_small = k.sem("small_transposed")
        s_cols = k.sem("cols_ready")
        s_silu = k.sem("silu_ready")
        s_row = k.sem("mod_row_in_psum")
        s_row_out = k.sem("mod_row_ready")
        s_aff = k.sem("affine_ready")
        s_sq = k.sem("sumsq_ready")
        s_std = k.sem("std_ready")
        s_rstd = k.sem("rstd_ready")
        s_root = k.sem("rsqrt_refined")
        s_xn = k.sem("xn_ready")
        s_tp = k.sem("x_transposed")
        s_t32 = k.sem("modulated_ready")
        s_hi = k.sem("hT_hi_ready")
        s_lo = [k.sem(f"hT_lo_ready{i}") for i in range(2)]

        ROW_BANK, SMALL_BANK, TP_BANK = (0, 1), 2, (3, 4, 5, 6)

        def raw(n):
            return x_raw[:, ds(n, 1), :].rearrange("p o d -> p (o d)").rearrange("p (j d) -> p j d", j=2)

        def part(t, n, kt):
            return t[:, ds(n, 1), kt, :].rearrange("p o t -> p (o t)")

        def pairs(eng, body):
            with eng.Fori(0, PAIRS // 2) as i:
                for s in range(2):
                    body(i * 2 + s, s, i, 0)
            body(PAIRS - 1, 0, PAIRS // 2, 1)

        with nc.Block() as block:

            @block.sync
            def _(sp):
                sp.dma_start(vec_rows[0:KD, :], a["c"].rearrange("a (k p) -> (a k) p", p=P)).then_inc(s_vec, 16)
                sp.dma_start(vec_rows[KD:2 * KD, :], a["c_ctx"].rearrange("(k p) -> k p", p=P)).then_inc(s_vec, 16)
                sp.dma_start(vec_rows[2 * KD:3 * KD, :], a["norm1_g"].rearrange("a (k p) -> (a k) p", p=P)).then_inc(s_vec, 16)

                def load_x(n, slot, src):
                    sp.dma_start(raw(n), src.rearrange("(j p) d -> p j d", p=P)).then_inc(s_x[slot], 16)

                def load_w(q, slot):
                    sp.wait_ge(s_row_out, q + 1)
                    sp.dma_start(w_slot[slot][:], w_mod[0, :, q * CH:(q + 1) * CH].rearrange("(k p) n -> p k n", p=P)).then_inc(s_w[slot], 16)

                load_w(0, 0)
                load_w(1, 1)
                load_x(0, 0, a["x"][0, 0:2 * P, :])
                load_x(1, 1, a["x"][0, 2 * P:4 * P, :])
                load_w(2, 0)
                load_w(3, 1)
                with sp.Fori(1, PAIRS // 2) as i:
                    for s in range(2):
                        sp.wait_ge(s_x[s], i * 16)
                        load_x(i * 2 + s, s, a["x"][0, ds(i * (4 * P) + s * (2 * P), 2 * P), :])
                sp.wait_ge(s_x[0], PAIRS // 2 * 16)
                load_x(PAIRS - 1, 0, a["ctx"][0])

            @block.gpsimd
            def _(pool):
                nc.gpsimd.memset(ident[:], 0.0).then_inc(s_ident, 1)
                pool.wait_ge(s_ident, 1)
                nc.gpsimd.affine_select(out=ident[:], in_=ident[:], compare_op=ALU.not_equal, fill=1.0, base=0,
                                        pattern=[[-1, P]], channel_multiplier=1).then_inc(s_ident, 1)
                nc.gpsimd.memset(keep["ones"][:], 1.0).then_inc(s_ident, 1)

                for q in range(MOD1):
                    if q >= 2:
                        pool.wait_ge(s_row_stored[q % 2], q // 2 * 16)
                    pool.dma_start(row[q % 2][:], b_mod[0:1, q * CH:(q + 1) * CH].broadcast_to([2, CH])).then_inc(s_bias[q % 2], 16)
                    if q >= 1:
                        pool.wait_ge(s_row_out, q + 2)
                        pool.dma_start(mod_rows[:, (q - 1) * CH:q * CH], row[(q - 1) % 2][:]).then_inc(s_row_stored[(q - 1) % 2], 16)
                pool.wait_ge(s_row_out, MOD1 + 2)
                pool.dma_start(mod_rows[:, (MOD1 - 1) * CH:MOD1 * CH], row[(MOD1 - 1) % 2][:]).then_inc(s_row_stored[(MOD1 - 1) % 2], 16)
                for s in range(2):
                    pool.wait_ge(s_row_stored[s], MOD1 // 2 * 16)
                for z in range(2):
                    pool.dma_start(mod_rows_sb[z * 2 * KD:(z + 1) * 2 * KD, :], mod_rows[z, 0:2 * D].rearrange("(m p) -> m p", p=P)).then_inc(s_modrows, 16)

                def cut(n, s, turn, z):
                    for kt in range(1, KD, 2):
                        pool.wait_ge(s_hi, n * KD + kt + 1)
                        nc.gpsimd.tensor_tensor(part(hT_lo, n, kt), t32[kt], part(hT_hi, n, kt).bitcast(F32), ALU.subtract).then_inc(s_lo[1], 1)

                pairs(pool, cut)

            @block.scalar
            def _(act):
                act.wait_ge(s_cols, 1)
                act.activation(cond_silu[:], vec_cols[:, 0:2 * KD].rearrange("p (a k) -> p a k", a=2), ACT.Silu).then_inc(s_silu, 1)
                act.activation(keep["cond"][:], vec_cols[:, 0:KD], ACT.Silu).then_inc(s_silu, 1)
                act.wait_ge(s_rstd, 1)

                def statistics(n, s, turn):
                    act.wait_ge(s_x[s], turn * 16 + 16)
                    for j in range(2):
                        tile = x_raw[:, ds(n, 1), j * D:(j + 1) * D].rearrange("p o d -> p (o d)")
                        act.activation(junk[j][:], tile, ACT.Square, accum_out=sumsq[:, ds(n * 2 + j, 1)]).then_inc(s_sq, 1)
                    act.wait_ge(s_sq, n * 2 + 2)
                    act.activation(rstd[:, ds(n * 2, 2)], sumsq[:, ds(n * 2, 2)], ACT.Sqrt, bias=eps_col[:], scale=1.0 / D).then_inc(s_std, 1)

                def modulate(n, z):
                    for kt in range(KD):
                        act.wait_ge(s_tp, n * KD + kt + 1 + 2 * KD)
                        act.wait_ge(s_lo[kt % 2], n * (KD // 2) + kt // 2 + 1)
                        act.activation(t32[kt], psum[:, TP_BANK[kt % 4], 0:2 * P], ACT.Identity,
                                       bias=aff1[:, z, 1, kt:kt + 1], scale=aff1[:, z, 0, kt:kt + 1]).then_inc(s_t32, 1)

                for n in range(4):
                    statistics(n, n % 2, n // 2)
                act.wait_ge(s_aff, 4)
                with act.Fori(0, PAIRS // 2 - 2) as i:
                    for s in range(2):
                        statistics(i * 2 + s + 4, s, i + 2)
                        modulate(i * 2 + s, 0)
                statistics(PAIRS - 1, 0, PAIRS // 2)
                for n in range(PAIRS - 5, PAIRS - 1):
                    modulate(n, 0)
                modulate(PAIRS - 1, 1)

            @block.tensor
            def _(pe):
                pe.wait_ge(s_ident, 3)
                pe.wait_ge(s_vec, 48)
                pe.transpose(psum[:, SMALL_BANK, 0:3 * KD], vec_rows[:], ident[0:3 * KD, 0:3 * KD]).then_inc(s_small, 1)
                pe.wait_ge(s_silu, 1)
                for q in range(MOD1):
                    pe.wait_ge(s_row_out, q + 1)
                    pe.wait_ge(s_w[q % 2], q // 2 * 16 + 16)
                    for kt in range(KD):
                        mm = pe.matmul(psum[0:2, ROW_BANK[q % 2], :], cond_silu[:, :, kt], w_slot[q % 2][:, kt, :], start=(kt == 0), stop=(kt == KD - 1))
                    mm.then_inc(s_row, 1)

                def transposes(n, s, turn, z, kts=range(KD)):
                    for kt in kts:
                        pe.wait_ge(s_xn, n * 2 + 2)
                        pe.wait_ge(s_t32, n * KD + kt + 1)
                        for j in range(2):
                            tp = pe.transpose(psum[:, TP_BANK[kt % 4], j * P:(j + 1) * P], xn[s][:, j, kt * P:(kt + 1) * P], ident[:])
                        tp.then_inc(s_tp, 1)

                pe.wait_ge(s_modrows, 32)
                pe.wait_ge(s_cols, 1)
                pe.transpose(psum[:, SMALL_BANK, 0:4 * KD], mod_rows_sb[:], ident[0:4 * KD, 0:4 * KD]).then_inc(s_small, 1)
                pairs(pe, transposes)

            @block.vector
            def _(dve):
                dve.sem_inc(s_row_out, 2)
                dve.sem_inc(s_lo[0], 4)
                dve.sem_inc(s_lo[1], 4)
                dve.sem_inc(s_t32, 4)
                dve.sem_inc(s_tp, 2 * KD)
                dve.memset(eps_col[:], EPS).then_inc(s_rstd, 1)
                dve.wait_ge(s_small, 1)
                dve.tensor_copy(vec_cols[:], psum[:, SMALL_BANK, 0:3 * KD]).then_inc(s_cols, 1)

                def take_row(q):
                    dve.wait_ge(s_row, q + 1)
                    dve.wait_ge(s_bias[q % 2], q // 2 * 16 + 16)
                    dve.tensor_tensor(row[q % 2][:], psum[0:2, ROW_BANK[q % 2], :], row[q % 2][:], ALU.add).then_inc(s_row_out, 1)

                def normalise(n, s):
                    dve.wait_ge(s_std, n + 1)
                    dve.reciprocal(rstd[:, ds(n * 2, 2)], rstd[:, ds(n * 2, 2)]).then_inc(s_rstd, 1)
                    dve.tensor_scalar(msq[:], sumsq[:, ds(n * 2, 2)], 1.0 / D, EPS, ALU.mult, ALU.add).then_inc(s_rstd, 1)
                    dve.wait_ge(s_rstd, n * 2 + 3)
                    refine_rsqrt(dve, rstd[:, ds(n * 2, 2)], msq[:], newton[:], s_root, n * 4)
                    dve.wait_ge(s_tp, n * KD + KD)
                    for j in range(2):
                        tile = x_raw[:, ds(n, 1), j * D:(j + 1) * D].rearrange("p o d -> p (o d)")
                        dve.tensor_scalar(xn[s][:, j, :], tile, rstd[:, ds(n * 2 + j, 1)], None, ALU.mult).then_inc(s_xn, 1)

                def cut(n):
                    for kt in range(KD):
                        dve.wait_ge(s_t32, n * KD + kt + 5)
                        dve.tensor_copy(part(hT_hi, n, kt), t32[kt]).then_inc(s_hi, 1)
                        if kt % 2 == 0:
                            dve.wait_ge(s_hi, n * KD + kt + 1)
                            dve.tensor_tensor(part(hT_lo, n, kt), t32[kt], part(hT_hi, n, kt).bitcast(F32), ALU.subtract).then_inc(s_lo[0], 1)

                take_row(0)
                take_row(1)
                normalise(0, 0)
                normalise(1, 1)
                take_row(2)
                take_row(3)
                dve.wait_ge(s_small, 2)
                dve.tensor_copy(mod_cols[:], psum[:, SMALL_BANK, 0:4 * KD]).then_inc(s_cols, 1)
                dve.wait_ge(s_cols, 2)
                for z in range(2):
                    at = z * 2 * KD
                    dve.scalar_tensor_tensor(aff1[:, z, 0, :], mod_cols[:, at + KD:at + 2 * KD], 1.0, vec_cols[:, 2 * KD:3 * KD], ALU.add, ALU.mult).then_inc(s_aff, 1)
                    dve.tensor_copy(aff1[:, z, 1, :], mod_cols[:, at:at + KD]).then_inc(s_aff, 1)
                with dve.Fori(0, PAIRS // 2 - 1) as i:
                    cut(i * 2)
                    normalise(i * 2 + 2, 0)
                    cut(i * 2 + 1)
                    normalise(i * 2 + 3, 1)
                cut(PAIRS - 3)
                normalise(PAIRS - 1, 0)
                cut(PAIRS - 2)
                cut(PAIRS - 1)


def input_projection(k, a, hT_hi, hT_lo, keep, scratch):
    nc, psum = k.nc, k.psum
    w_in = a["w_in"]
    with ExitStack() as ctx:
        def sb(name, shape, dt=F32):
            return ctx.enter_context(nc.sbuf_tensor(name, shape, dt))

        w_hi = [sb(f"win_hi{i}", [P, KD, P], F32R) for i in range(2)]
        w_raw, w_lo = zip(*(k.overlaid(ctx, (f"win_raw{i}", [P, KD, P], F32), (f"win_lo{i}", [P, KD, P], F32R)) for i in range(2)))
        cos, sin = sb("cos", [P, S]), sb("sin", [P, S])
        stage = [sb(f"stage{i}", [P, CH if i < NCH else L]) for i in range(NCH + 1)]
        swapped, turned = sb("swapped", [P, CH]), sb("turned", [P, CH])
        cut_hi = [sb(f"cut_hi{i}", [P, CH], F32R) for i in range(2)]
        cut_lo = [sb(f"cut_lo{i}", [P, CH], F32R) for i in range(2)]

        MOD2 = 6 * D // CH - MOD1
        piece = [t[:].bitcast(F32) for t in (*cut_hi, *cut_lo)]
        mod_sum, mod_row = turned, swapped[0:1, :]
        s_piece = [k.sem(f"wmod_piece_landed{i}") for i in range(4)]
        s_mac = k.sem("wmod_piece_added")
        s_modsum = k.sem("mod_sum_ready")
        s_modrow = k.sem("mod_row_summed")
        s_mrow_out = k.sem("mod_row2_ready")
        s_mbias = k.sem("mod_bias_landed")
        s_mstored = k.sem("mod_row2_stored")
        s_rope = k.sem("rope_tables_landed")
        s_w = [k.sem(f"win_landed{i}") for i in range(2)]
        s_hi = k.sem("win_hi_ready")
        s_lo = k.sem("win_lo_ready")
        s_acc = k.sem("projection_ready")
        s_stage = k.sem("stage_ready")
        s_free = [k.sem(f"stage_free{i}") for i in range(NCH + 1)]
        s_step = k.sem("rope_step")
        s_cut = k.sem("qk_cut")
        s_hi_cut = k.sem("qk_hi_ready")
        s_cut_stored = [k.sem(f"cut_stored{i}") for i in range(2)]

        KINDS = ((0, 4, True, False, scratch["xr"], 0, 0, 0), (4, 4, False, False, scratch["xg"], 4, 4, 0),
                 (8, 4, False, True, None, 8, 4, 0), (12, 1, True, True, None, 8, 4, 16),
                 (13, 1, True, False, scratch["v"], 13, 5, 21))
        LAST = 13

        def walk(body):
            def run(eng):
                unit = 0
                for m0, count, with_ctx, rope, dram, d0, ctx0, rope0 in KINDS:
                    per = NCH + with_ctx
                    if count > 1:
                        with eng.Fori(0, count // 2) as i:
                            for j in range(2):
                                body(eng, m0 + j + i * 2, j, i + m0 // 2, unit + per * j + i * (2 * per), with_ctx, rope, dram,
                                     j + i * 2 + (m0 - d0), ctx0 + j + i * 2, rope0 + j * NCH + i * (2 * NCH), False)
                    else:
                        body(eng, m0, m0 % 2, m0 // 2, unit, with_ctx, rope, dram, m0 - d0, ctx0, rope0, m0 == LAST)
                    unit += per * count
            return run

        def chunks(with_ctx):
            return [(c, c * CH, CH) for c in range(NCH)] + ([(NCH, S, L)] if with_ctx else [])

        def bank(slot, c):
            return 4 * slot + c if c < NCH else 4 * (1 - slot) + 3

        with nc.Block() as block:

            @block.sync
            def _(sp):
                def load(m, slot, units_before):
                    sp.wait_ge(s_acc, units_before + 1)
                    sp.dma_start(w_raw[slot][:], w_in[0, :, ds(m * P, P)].rearrange("(k p) n -> p k n", p=P)).then_inc(s_w[slot], 16)

                def body(sp, m, slot, turn, unit, with_ctx, rope, dram, row, nctx, nrope, last):
                    if not last:
                        load(m + 1, 1 - slot, unit)
                    with_mod = not rope and dram is not scratch["v"]
                    cols = ds(m * CH + MOD1 * CH, CH)
                    if with_mod:
                        sp.wait_ge(s_mstored, m * 16 + 16)
                        sp.dma_start(mod_row, a["b_mod"][0:1, cols]).then_inc(s_mbias, 16)
                        pieces(m, cols, 0, 4)
                    for c, t0, n in chunks(with_ctx):
                        if with_mod and c in (1, 2):
                            pieces(m, cols, 2 * c + 2, 2 * c + 4)
                        if rope:
                            half = c % 2
                            sp.wait_ge(s_cut, nrope + c + 1)
                            sp.sem_inc(s_free[c], 16)
                            dst = (ds(row * P, P), slice(t0, t0 + n))
                            sp.dma_start(scratch["qk_hi"][dst[0], dst[1]], cut_hi[half][:, 0:n].bitcast(F32)).then_inc(s_cut_stored[half], 16)
                            sp.dma_start(scratch["qk_lo"][dst[0], dst[1]], cut_lo[half][:, 0:n].bitcast(F32)).then_inc(s_cut_stored[half], 16)
                        else:
                            sp.wait_ge(s_stage, unit + c + 5)
                            sp.dma_start(dram[ds(row * P, P), t0:t0 + n], stage[c][:, 0:n]).then_inc(s_free[c], 16)
                    if with_mod:
                        sp.wait_ge(s_mrow_out, m + 2)
                        sp.dma_start(scratch["mod"][0:1, cols], mod_row).then_inc(s_mstored, 16)

                def pieces(m, cols, first, end):
                    for kt in range(first, end):
                        sp.wait_ge(s_mac, m * KD + kt + 1)
                        sp.dma_start(piece[kt % 4], a["w_mod"][0, kt * P:(kt + 1) * P, cols]).then_inc(s_piece[kt % 4], 16)

                sp.sem_inc(s_mstored, 16)
                load(0, 0, 0)
                sp.dma_start(cos[:], a["rope_cos"]).then_inc(s_rope, 16)
                sp.dma_start(sin[:], a["rope_sin"]).then_inc(s_rope, 16)
                walk(body)(sp)
                for c in range(NCH):
                    sp.wait_ge(s_free[c], 16 * (14 + 1))
                sp.wait_ge(s_free[NCH], 16 * (6 + 1))
                sp.wait_ge(s_cut_stored[0], 32 * (8 + 3 + 1))
                sp.wait_ge(s_cut_stored[1], 32 * (8 + 2 + 1))

            @block.gpsimd
            def _(pool):
                pool.sem_inc(s_lo, 2)
                pool.sem_inc(s_mac, 4)
                pool.sem_inc(s_mrow_out, 1)

                def cut(m, slot):
                    pool.wait_ge(s_hi, m + 1)
                    nc.gpsimd.tensor_tensor(w_lo[slot][:], w_raw[slot][:], w_hi[slot][:].bitcast(F32), ALU.subtract).then_inc(s_lo, 1)

                def body(pool, m, slot, turn, unit, with_ctx, rope, dram, row, nctx, nrope, last):
                    if not last:
                        cut(m + 1, 1 - slot)

                cut(0, 0)
                walk(body)(pool)

            @block.scalar
            def _(act):
                act.sem_inc(s_stage, 4)
                act.sem_inc(s_acc, 1)
                for c in range(NCH + 1):
                    act.sem_inc(s_free[c], 16)
                for half in range(2):
                    act.sem_inc(s_cut_stored[half], 32)

                def cut(slot, turn, units_before):
                    act.wait_ge(s_w[slot], turn * 16 + 16)
                    act.wait_ge(s_acc, units_before + 1)
                    act.activation(w_hi[slot][:], w_raw[slot][:], ACT.Copy).then_inc(s_hi, 1)

                def body(act, m, slot, turn, unit, with_ctx, rope, dram, row, nctx, nrope, last):
                    if not last:
                        cut(1 - slot, turn + slot, unit)
                    for c, t0, n in chunks(with_ctx):
                        act.wait_ge(s_acc, unit + c + 2)
                        act.wait_ge(s_free[c], ((m if c < NCH else nctx) + 1) * 16)
                        act.activation(stage[c][:, 0:n], psum[:, bank(slot, c), 0:n], ACT.Copy).then_inc(s_stage, 1)

                cut(0, 0, 0)
                walk(body)(act)

            @block.tensor
            def _(pe):
                def body(pe, m, slot, turn, unit, with_ctx, rope, dram, row, nctx, nrope, last):
                    pe.wait_ge(s_lo, m + 3)
                    with_mod = not rope and dram is not scratch["v"]
                    pe.wait_ge(s_mrow_out, m + 1 if with_mod else MOD2 + 1)
                    for c, t0, n in chunks(with_ctx):
                        if with_mod and c == NCH - 1:
                            pe.wait_ge(s_modsum, m + 1)
                            pe.matmul(psum[0:1, bank(1 - slot, 0), :], keep["ones"][:], mod_sum[:], start=True, stop=True).then_inc(s_modrow, 1)
                        pe.wait_ge(s_stage, unit + c + 1)
                        for kt in range(KD):
                            for wp, hp in ((w_hi, hT_hi), (w_hi, hT_lo), (w_lo, hT_hi)):
                                mm = pe.matmul(psum[:, bank(slot, c), 0:n], wp[slot][:, kt, :], hp[:, t0 // (2 * P):(t0 + n) // (2 * P), kt, :],
                                               start=(kt == 0 and wp is w_hi and hp is hT_hi), stop=(kt == KD - 1 and wp is w_lo))
                        mm.then_inc(s_acc, 1)

                walk(body)(pe)

            @block.vector
            def _(dve):
                def modulation_row(m, slot):
                    for kt in range(KD):
                        dve.wait_ge(s_piece[kt % 4], m * 32 + kt // 4 * 16 + 16)
                        silu_c = keep["cond"][:, kt:kt + 1]
                        if kt == 0:
                            dve.tensor_scalar(mod_sum[:], piece[0], silu_c, None, ALU.mult).then_inc(s_mac, 1)
                        else:
                            dve.wait_ge(s_mac, m * KD + kt + 4)
                            dve.scalar_tensor_tensor(mod_sum[:], piece[kt % 4], silu_c, mod_sum[:], ALU.mult, ALU.add).then_inc(s_mac, 1)
                    dve.wait_ge(s_mac, m * KD + KD + 4)
                    dve.sem_inc(s_modsum, 1)
                    dve.wait_ge(s_mbias, m * 16 + 16)
                    dve.wait_ge(s_modrow, m + 1)
                    dve.tensor_tensor(mod_row, psum[0:1, bank(1 - slot, 0), :], mod_row, ALU.add).then_inc(s_mrow_out, 1)

                def rotated(dve, m, slot, turn, unit, with_ctx, rope, dram, row, nctx, nrope, last):
                    if not rope and dram is not scratch["v"]:
                        modulation_row(m, slot)
                    if not rope:
                        return
                    dve.wait_ge(s_mstored, MOD2 * 16 + 16)
                    dve.wait_ge(s_rope, 32)
                    tq, nrope_half = row, row * 2
                    for c, t0, n in chunks(with_ctx):
                        half = c % 2
                        dve.wait_ge(s_stage, unit + c + 5)
                        done = nrope * 4 + c * 4
                        if c < NCH:
                            nc.vector.tensor_tensor(turned[:], stage[c][:], cos[:, t0:t0 + n], ALU.mult).then_inc(s_step, 1)
                            nc.vector.stream_shuffle(swapped[:], stage[c][:], [(i + 16) % 32 for i in range(32)]).then_inc(s_step, 1)
                            dve.wait_ge(s_step, done + 2)
                            nc.vector.tensor_tensor(swapped[:], swapped[:], sin[:, t0:t0 + n], ALU.mult).then_inc(s_step, 1)
                            dve.wait_ge(s_step, done + 3)
                            nc.vector.tensor_tensor(stage[c][:], turned[:], swapped[:], ALU.add).then_inc(s_step, 1)
                            dve.wait_ge(s_step, done + 4)
                        dve.wait_ge(s_cut_stored[half], nrope_half * 32 + (c // 2 + 1) * 32)
                        nc.vector.tensor_copy(cut_hi[half][:, 0:n], stage[c][:, 0:n]).then_inc(s_hi_cut, 1)
                        dve.wait_ge(s_hi_cut, nrope + c + 1)
                        nc.vector.tensor_tensor(cut_lo[half][:, 0:n], stage[c][:, 0:n], cut_hi[half][:, 0:n].bitcast(F32), ALU.subtract).then_inc(s_cut, 1)

                walk(rotated)(dve)


def mixers(k, a, keep, scratch):
    nc, psum = k.nc, k.psum
    ident = keep["ident"]
    GAP = 4
    LAT = L + GAP
    W = LAT + S
    KW = L + P + S + P
    SUB = 4
    HEADS = SUB * N_HEADS
    GROUPS = SUB * N_KV
    ROUNDS = NB // SUB
    GATE_UNITS = 4 * (NCH + 1)
    PACKETS = 5 * GROUPS
    PV_AT, PV_END, COPY_AT, TURN_AT, V_AT = 7, 8, 9, 10, 5
    STEPS = HEADS + 7
    RING = PACKETS + SUB
    SCAN_AT, CONV_AT, CONV_STEPS = (14, 15, 17, 18), 22, 8
    TANH_AT, DECAY_AT, ROOT_AT = (1, 3), (5, 7), 8
    DVE_RNN = CONV_STEPS + 4 + 6
    assert ROUNDS == RNN_TILES

    def ring(Q):
        return Q + (Q + 5) // 10

    def ring_v(n):
        return 11 * n + 5

    PRE = 3

    def event(it, kind, index):
        return (it * GROUPS + index) * 2 + (kind == "turn") + PRE

    with ExitStack() as ctx:
        def sb(name, shape, dt=F32):
            return ctx.enter_context(nc.sbuf_tensor(name, shape, dt))

        keys = sb("keys_hi_lo", [P, N_KV, KW], F32R)
        q_same = [sb(f"q_hi_lo{i}", [P, N_HEADS, P], F32R) for i in range(2)]
        q_cross = [sb(f"q_lo_hi{i}", [P, N_HEADS, P], F32R) for i in range(2)]
        prob = [sb(f"prob{i}", [P, 5 * P]) for i in range(2)]
        pT = [sb(f"probT{i}", [P, PER_KV, 5, P]) for i in range(2)]
        v_raw = [sb(f"v_raw{i}", [P, P]) for i in range(2)]
        v_ctx = sb("v_ctx", [P, 2, N_KV * HEAD])
        v_ring = sb("v_ring", [P, 4, N_KV * HEAD])
        oT = sb("oT", [P, CH])
        o_junk = sb("o_squares", [P, D_ATTN])
        o_tok = [sb(f"o_tok{i}", [P, D_ATTN]) for i in range(2)]
        ident_bf = sb("ident_bf", [P, P], BF16)
        mask_before, mask_after = sb("mask_before", [P, P], BF16), sb("mask_after", [P, P], BF16)
        mask_first, mask_last = sb("mask_first", [P, ROUNDS, P], BF16), sb("mask_last", [P, ROUNDS, P], BF16)
        sink = sb("sink", [P, N_HEADS])
        neg_sink = sb("neg_sink", [P, N_HEADS])
        row_max, neg_max, row_sum, sink_in, sink_exp, inv_sum = (
            [sb(f"{n}{i}", [P, N_HEADS]) for i in range(2)] for n in ("row_max", "neg_max", "row_sum", "sink_in", "sink_exp", "inv_sum"))
        gate_raw = sb("gate_raw", [P, 4, P])
        gate_hi, gate_lo = sb("gate_hi", [P, 4, P], F32R), sb("gate_lo", [P, 4, P], F32R)
        g_r = [sb("decay_gate0", [P, W + GAP]), sb("decay_gate1", [P, W + GAP])]
        g_i = [sb(f"input_gate{d}", [P, W]) for d in range(2)]
        th = [sb(f"tanh_half{d}", [P, W]) for d in range(2)]
        x_pad = g_r[1]
        xc, xc_hi, xc_lo = sb("xc", [P, W]), sb("xc_hi", [P, W], F32R), sb("xc_lo", [P, W], F32R)
        xg, gel = sb("xg_sb", [P, S]), sb("gelu_sb", [P, S])
        par_rows, par = sb("rnn_rows", [44, P]), sb("rnn_cols", [P, 44])
        sp_e, sp_s, sp_p, sp_pos = (sb(n, [P, 8]) for n in ("sp_e", "sp_s", "sp_p", "sp_pos"))
        c_exp, c_tanh = sb("c_exp", [P, 8]), sb("c_tanh", [P, 8])
        CONV_W, CONV_B, B_A, B_I, LAM = 0, 16, 20, 28, 36

        sem = k.sem
        s_setup, s_par, s_parT, s_parc = sem("setup_ready"), sem("params_landed"), sem("params_transposed"), sem("params_step")
        s_keys, s_pads, s_sink = sem("keys_landed"), sem("pads_ready"), sem("sink_landed")
        s_mask = sem("masks_ready")
        s_q = [sem(f"q_landed{i}") for i in range(2)]
        s_vraw = [sem(f"v_landed{i}") for i in range(2)]
        s_vt = sem("v_transposed")
        s_misc = sem("shared_bank_taken")
        s_sc = sem("scores_ready")
        s_mx, s_nm = sem("row_max_ready"), sem("neg_max_ready")
        s_exp = sem("prob_ready")
        s_pt, s_pttail = sem("prob_packet_transposed"), sem("prob_tail_transposed")
        s_ptout = sem("probT_or_v_copied")
        s_pv, s_turn = sem("pv_ready"), sem("oT_turned")
        s_sin, s_ses, s_den, s_inv = sem("sink_in_ready"), sem("sink_exp_ready"), sem("sum_ready"), sem("inv_sum_ready")
        s_ssq, s_msq = sem("o_sumsq_ready"), sem("o_mean_square_ready")
        s_gbias, s_gelu_turn = sem("gate_biases_ready"), sem("gelu_square_seen")
        o_ssq, gate_bias = sb("o_ssq", [P, 1]), sb("gate_bias", [P, 4])
        s_ostored = [sem(f"o_stored{i}") for i in range(2)]
        s_gw, s_gwhi, s_gwlo = sem("gate_w_landed"), sem("gate_hi_ready"), sem("gate_lo_ready")
        s_gacc, s_gout = sem("gate_in_psum"), sem("gate_out")
        s_xr, s_xg = sem("xr_landed"), sem("xg_landed")
        s_pre, s_sg, s_gelu = sem("gelu_arg_ready"), sem("gelu_sigmoid_ready"), sem("gelu_ready")
        s_xi = sem("gated_x_ready")
        s_th, s_a, s_sq = sem("tanh_ready"), sem("decay_ready"), sem("sqrt_ready")
        s_v, s_hi, s_lo = sem("rnn_vector_step"), sem("xc_hi_ready"), sem("xc_lo_ready")
        s_u, s_both = sem("scan_input_ready"), sem("states_added")
        s_y, s_ystored = sem("y_ready"), sem("y_stored")
        s_pad0 = sem("x_pad_zeroed")
        s_gap = sem("gaps_filled")
        s_series = sem("series_step")

        GATE_BANKS, PT_BANKS, MISC = (0, 1, 2, 3), (4, 5, 7), 6
        S_SLOT = [psum[:, 2 * i:2 * i + 2, :].rearrange("p b c -> p (b c)")[:, P:6 * P] for i in range(2)]

        def packets_of(w):
            return [w // 4 * 5 + p for p in ((0,), (1,), (2,), (3, 4))[w % 4]]

        def packet_of(tile, Q):
            return tile[Q // 5 % 2][:].rearrange("p h b q -> p (h b q)")[:, (Q % 5) * CH:(Q % 5 + 1) * CH]

        def rnn_chunks():
            return [(0, 0, L)] + [(1 + c, LAT + c * CH, CH) for c in range(NCH)]

        def rounds(eng, body):
            with eng.Fori(0, ROUNDS - 1) as it:
                body(it, False)
            body(ROUNDS - 1, True)

        def unit_of(v):
            return v // (2 * (NCH + 1)), v // (NCH + 1) % 2, rnn_chunks()[v % (NCH + 1)]

        def gate_share(u):
            k0, steps = u - HEADS - 1, STEPS - HEADS - 1
            return k0 * GATE_UNITS // steps, (k0 + 1) * GATE_UNITS // steps

        with nc.Block() as block:

            @block.sync
            def _(sp):
                rows = (("rnn_conv_w", 16), ("rnn_conv_b", 4), ("lru_b_a", 8), ("lru_b_i", 8), ("lru_lam", 8))
                at = 0
                for name, n in rows:
                    src = a[name][0] if name != "rnn_conv_b" else a[name]
                    sp.dma_start(par_rows[at:at + n, :], src.rearrange("a (j p) -> (a j) p", p=P)).then_inc(s_par, 16)
                    at += n

                def load_q(n, par_):
                    tok = ds(n * P, P)
                    hi = scratch["qk_hi"][0:D_ATTN, tok].rearrange("(h d) t -> d h t", d=HEAD)
                    lo = scratch["qk_lo"][0:D_ATTN, tok].rearrange("(h d) t -> d h t", d=HEAD)
                    for tile, top, low in ((q_same, hi, lo), (q_cross, lo, hi)):
                        sp.dma_start(tile[par_][0:HEAD, :, :].bitcast(F32), top).then_inc(s_q[par_], 16)
                        sp.dma_start(tile[par_][HEAD:P, :, :].bitcast(F32), low).then_inc(s_q[par_], 16)

                def load_v(col, slot):
                    sp.dma_start(v_raw[slot][:], scratch["v"][:, col]).then_inc(s_vraw[slot], 16)

                load_v(ds(S, P), 0)
                load_v(ds(S + P, P), 1)
                load_q(0, 0)
                sp.wait_ge(s_vt, 1)
                load_v(ds(0, P), 0)

                def body(it, last):
                    for n in range(SUB):
                        sp.wait_ge(s_vt, it * SUB + n + 2)
                        load_v(ds(it * (SUB * P) + (n + 1) * P, P), (n + 1) % 2)
                        if not (last and n == SUB - 1):
                            sp.wait_ge(s_sc, it * HEADS + n * N_HEADS + 1)
                            load_q(it * SUB + n + 1, (n + 1) % 2)
                        if n:
                            store(it, n - 1)
                        if n == SUB - 1:
                            sp.wait_ge(s_y, it + 1)
                            sp.dma_start(scratch["mix"][ds(it * P, P), :], g_i[0][:, LAT:W]).then_inc(s_ystored, 16)
                    store(it, SUB - 1)

                def store(it, n):
                    sp.wait_ge(s_misc, event(it, "turn", 2 * n + 1) + 2)
                    sp.dma_start(scratch["att"][ds(it * (SUB * P) + n * P, P), :], o_tok[n % 2][:]).then_inc(s_ostored[n % 2], 16)

                rounds(sp, body)
                for i in range(2):
                    sp.wait_ge(s_ostored[i], 16 * (NB // 2 + 1))
                sp.wait_ge(s_ystored, 16 * (ROUNDS + 1))

            @block.gpsimd
            def _(pool):
                nc.gpsimd.memset(gate_raw[:], 0.0).then_inc(s_setup, 1)
                pool.wait_ge(s_setup, 1)

                def load_gates(it):
                    for g, name in enumerate(("lru_w_a", "lru_w_i")):
                        for b in range(2):
                            pool.dma_start(gate_raw[b * 64:(b + 1) * 64, 2 * g:2 * g + 2, b * 64:(b + 1) * 64],
                                           a[name][0, :, ds(it * 2 + b, 1), :, :].rearrange("d o c e -> c (d o) e")).then_inc(s_gw, 16)

                def load_xr(it):
                    pool.dma_start(x_pad[:, 2:2 + L], scratch["xr"][ds(it * P, P), S:T]).then_inc(s_xr, 16)
                    pool.dma_start(x_pad[:, 2 + LAT:2 + W], scratch["xr"][ds(it * P, P), 0:S]).then_inc(s_xr, 16)

                def load_xg(it):
                    pool.dma_start(xg[:], scratch["xg"][ds(it * P, P), :]).then_inc(s_xg, 16)

                load_xr(0)
                load_gates(0)
                load_xg(0)
                nc.gpsimd.memset(mask_before[:], 0.0).then_inc(s_mask, 1)
                nc.gpsimd.memset(mask_after[:], 0.0).then_inc(s_mask, 1)
                nc.gpsimd.tensor_copy(ident_bf[:], ident[:]).then_inc(s_mask, 1)
                pool.wait_ge(s_mask, 3)
                nc.gpsimd.affine_select(out=mask_before[:], in_=mask_before[:], compare_op=ALU.is_ge, fill=NEG, base=0,
                                        pattern=[[1, P]], channel_multiplier=-1).then_inc(s_mask, 1)
                nc.gpsimd.affine_select(out=mask_after[:], in_=mask_after[:], compare_op=ALU.is_ge, fill=NEG, base=0,
                                        pattern=[[-1, P]], channel_multiplier=1).then_inc(s_mask, 1)
                pool.wait_ge(s_mask, 5)
                for r in range(ROUNDS):
                    if r == 0:
                        nc.gpsimd.memset(mask_first[:, r, :], NEG).then_inc(s_mask, 1)
                    else:
                        nc.gpsimd.tensor_copy(mask_first[:, r, :], mask_before[:]).then_inc(s_mask, 1)
                    if r == ROUNDS - 1:
                        nc.gpsimd.memset(mask_last[:, r, :], NEG).then_inc(s_mask, 1)
                    else:
                        nc.gpsimd.tensor_copy(mask_last[:, r, :], mask_after[:]).then_inc(s_mask, 1)

                def gelu_argument(it):
                    pool.wait_ge(s_xg, it * 16 + 16)
                    nc.gpsimd.tensor_tensor(gel[:], xg[:], xg[:], ALU.mult).then_inc(s_pre, 1)
                    pool.wait_ge(s_pre, it * 3 + 1)
                    pool.sem_inc(s_gelu_turn, 1)
                    nc.gpsimd.tensor_scalar(gel[:], gel[:], GELU_A, 1.0, ALU.mult, ALU.add).then_inc(s_pre, 1)
                    pool.wait_ge(s_pre, it * 3 + 2)
                    nc.gpsimd.tensor_tensor(gel[:], gel[:], xg[:], ALU.mult).then_inc(s_pre, 1)

                gelu_argument(0)

                def body(it, last):
                    pool.wait_ge(s_gout, it * GATE_UNITS + GATE_UNITS + 4)
                    for d in range(2):
                        nc.gpsimd.tensor_tensor(g_i[d][:], g_i[d][:], xc[:], ALU.mult).then_inc(s_xi, 1)
                    pool.wait_ge(s_sg, it + 1)
                    nc.gpsimd.tensor_tensor(gel[:], gel[:], xg[:], ALU.mult).then_inc(s_gelu, 1)
                    if not last:
                        load_gates(it + 1)
                        pool.wait_ge(s_gelu, it + 1)
                        load_xg(it + 1)
                    for d in range(2):
                        pool.wait_ge(s_xi, it * 2 + d + 1)
                        pool.wait_ge(s_v, it * DVE_RNN + CONV_STEPS + 2 * d + 2)
                        nc.gpsimd.tensor_tensor(th[d][:], th[d][:], g_i[d][:], ALU.mult).then_inc(s_u, 1)
                    pool.wait_ge(s_v, it * DVE_RNN + CONV_STEPS + 10)
                    if not last:
                        load_xr(it + 1)
                    nc.gpsimd.tensor_tensor(g_i[0][:, LAT:W], g_i[0][:, LAT:W], g_i[1][:, LAT:W], ALU.add).then_inc(s_both, 1)
                    pool.wait_ge(s_both, it + 1)
                    nc.gpsimd.tensor_tensor(g_i[0][:, LAT:W], g_i[0][:, LAT:W], gel[:], ALU.mult).then_inc(s_y, 1)
                    pool.wait_ge(s_y, it + 1)
                    if not last:
                        gelu_argument(it + 1)
                        pool.wait_ge(s_hi, it + 2)
                        nc.gpsimd.tensor_tensor(xc_lo[:], xc[:], xc_hi[:].bitcast(F32), ALU.subtract).then_inc(s_lo, 1)

                rounds(pool, body)

            @block.scalar
            def _(act):
                act.dma_start(sink[:], a["attn_sink"].broadcast_to([P, N_HEADS])).then_inc(s_sink, 16)
                for kv in range(N_KV):
                    rows = slice(D_ATTN + kv * HEAD, D_ATTN + (kv + 1) * HEAD)
                    for half, src in ((0, scratch["qk_hi"]), (1, scratch["qk_lo"])):
                        dst = keys[half * HEAD:(half + 1) * HEAD, kv, :].bitcast(F32)
                        act.dma_start(dst[:, 0:L], src[rows, S:T]).then_inc(s_keys, 16)
                        act.dma_start(dst[:, L + P:L + P + S], src[rows, 0:S]).then_inc(s_keys, 16)
                act.wait_ge(s_parc, 1)
                act.activation(sp_e[:], par[:, LAM:LAM + 8], ACT.Abs).then_inc(s_parc, 1)
                act.wait_ge(s_parc, 2)
                act.activation(sp_e[:], sp_e[:], ACT.Exp, scale=-1.0).then_inc(s_parc, 1)
                act.sem_inc(s_gout, 4)
                act.sem_inc(s_exp, 2)
                act.sem_inc(s_misc, 1)
                act.sem_inc(s_ostored[0], 16)
                act.sem_inc(s_ostored[1], 16)
                act.sem_inc(s_ystored, 16)

                def gates(it, first, end):
                    if first == 0:
                        act.wait_ge(s_ystored, it * 16 + 16)
                        act.wait_ge(s_gap, it + 4)
                        act.wait_ge(s_gbias, it + 1)
                    for v in range(first, end):
                        g, d, (c, t0, n) = unit_of(v)
                        act.wait_ge(s_gacc, it * GATE_UNITS + v + 1)
                        act.activation((g_r, g_i)[g][d][:, t0:t0 + n], psum[:, GATE_BANKS[v % 4], 0:n], ACT.Sigmoid,
                                       bias=gate_bias[:, g * 2 + d:g * 2 + d + 1]).then_inc(s_gout, 1)
                        if v == GATE_UNITS // 2 - 1:
                            act.wait_ge(s_pre, it * 3 + 3)
                            act.activation(gel[:], gel[:], ACT.Sigmoid, scale=GELU_C).then_inc(s_sg, 1)

                def body(it, last):
                    for u in range(STEPS):
                        if 3 <= u < HEADS + 3:
                            for Q in packets_of(u - 3):
                                act.wait_ge(s_pt, it * PACKETS + Q + 1)
                                act.wait_ge(s_pv, it * GROUPS + Q // 5 + 1)
                                act.activation(packet_of(pT, Q), psum[:, PT_BANKS[ring(Q) % 3], :], ACT.Copy).then_inc(s_ptout, 1)
                        if u % 8 == V_AT + 1 and u < HEADS:
                            n = u // 8
                            act.wait_ge(s_vt, it * SUB + n + 4)
                            act.activation(v_ring[:, (n + 1) % 4], psum[:, PT_BANKS[ring_v(n) % 3], 0:P], ACT.Copy).then_inc(s_ptout, 1)
                        if 1 <= u <= HEADS:
                            w = u - 1
                            s, h, n = w % 2, w % 8, (w // 8) % 2
                            act.wait_ge(s_nm, it * HEADS + w + 1)
                            if w % 4 == 1 and w > 4:
                                act.wait_ge(s_pt, it * PACKETS + w // 4 * 5)
                            elif w >= 2:
                                act.wait_ge(s_pttail, it * 3 * GROUPS + (w - 2) // 4 * 3 + (w - 2) % 4 + 1)
                            act.activation(prob[s][:], S_SLOT[s], ACT.Exp, bias=neg_max[n][:, h:h + 1], scale=SCALE,
                                           accum_out=row_sum[n][:, h:h + 1]).then_inc(s_exp, 1)
                        if u % 4 == 0 and 4 <= u <= HEADS:
                            G = u // 4 - 1
                            n, kv = (G // 2) % 2, G % 2
                            act.wait_ge(s_sin, it * GROUPS + G + 1)
                            act.activation(sink_exp[n][:, kv * 4:kv * 4 + 4], sink_in[n][:, kv * 4:kv * 4 + 4], ACT.Exp).then_inc(s_ses, 1)
                        if u in TANH_AT:
                            d = TANH_AT.index(u)
                            act.activation(th[d][:], g_r[d][:, 0:W], ACT.Tanh, scale=c_tanh[:, ds(it + d * RNN_TILES, 1)]).then_inc(s_th, 1)
                        if u in DECAY_AT:
                            d = DECAY_AT.index(u)
                            act.wait_ge(s_th, it * 2 + d + 1)
                            act.activation(g_r[d][:, 0:W], g_r[d][:, 0:W], ACT.Exp, scale=c_exp[:, ds(it + d * RNN_TILES, 1)]).then_inc(s_a, 1)
                        if u == ROOT_AT:
                            for d in range(2):
                                act.activation(th[d][:], th[d][:], ACT.Sqrt).then_inc(s_sq, 1)
                        if u > HEADS and not last:
                            gates(it + 1, *gate_share(u))

                gates(0, 0, GATE_UNITS)
                act.wait_ge(s_parc, 13)
                rounds(act, body)

            @block.tensor
            def _(pe):
                pe.wait_ge(s_par, 80)
                pe.transpose(psum[:, 7, 0:44], par_rows[:], ident[0:44, 0:44]).then_inc(s_parT, 1)

                def turn_v(bank, slot, landed):
                    pe.wait_ge(s_vraw[slot], landed)
                    pe.transpose(psum[:, bank, 0:P], v_raw[slot][:], ident[:]).then_inc(s_vt, 1)

                def gates(it, first, end):
                    if first == 0:
                        pe.wait_ge(s_gwlo, it + 1)
                        pe.wait_ge(s_lo, it + 1)
                        pe.wait_ge(s_exp, it * HEADS + 2)
                    for v in range(first, end):
                        g, d, (c, t0, n) = unit_of(v)
                        pe.wait_ge(s_gout, it * GATE_UNITS + v + 1)
                        for i, (wt, xt) in enumerate(((gate_hi, xc_hi), (gate_hi, xc_lo), (gate_lo, xc_hi))):
                            mm = pe.matmul(psum[:, GATE_BANKS[v % 4], 0:n], wt[:, g * 2 + d, :], xt[:, t0:t0 + n], start=(i == 0), stop=(i == 2))
                        mm.then_inc(s_gacc, 1)
                    if end == GATE_UNITS:
                        pe.wait_ge(s_gout, it * GATE_UNITS + GATE_UNITS + 4)

                gates(0, 0, GATE_UNITS)
                for i, slot in enumerate((0, 1, 0)):
                    pe.wait_ge(s_misc, i + 1)
                    turn_v(MISC, slot, i // 2 * 16 + 16)
                pe.wait_ge(s_keys, 16 * 8)
                pe.wait_ge(s_pads, 2 * N_KV + 2)
                pe.wait_ge(s_mask, 5 + 2 * ROUNDS)

                def body(it, last):
                    def times_v(G, blocks):
                        n, kv = G // 2, G % 2
                        for b in blocks:
                            v_block = v_ring[:, (n - 1 + b) % 4] if b < 3 else v_ctx[:, b - 3]
                            v_b = v_block[:, kv * HEAD:(kv + 1) * HEAD]
                            mm = pe.matmul(psum[0:HEAD, MISC, :], v_b, pT[G % 2][:, :, b, :], start=(b == 0), stop=(b == 4))
                        return mm

                    for u in range(STEPS):
                        if u >= TURN_AT and (u - TURN_AT) % 4 == 0 and (u - TURN_AT) // 4 < GROUPS:
                            G = (u - TURN_AT) // 4
                            pe.wait_ge(s_misc, event(it, "turn", G) + 1)
                            for h in range(PER_KV):
                                tp = pe.transpose(psum[:, MISC, h * P:(h + 1) * P], oT[:, h * P:(h + 1) * P], ident[:])
                            tp.then_inc(s_turn, 1)
                        if u < HEADS:
                            s, h, n = u % 2, u % 8, u // 8
                            kv, slot = h // PER_KV, n % 2
                            if h == 0:
                                pe.wait_ge(s_q[slot], (it * 2 + n // 2) * 64 + 64)
                            pe.wait_ge(s_exp, it * HEADS + u + 1)
                            local = ds(it * (SUB * P) + n * P + L, 3 * P)
                            before = mask_first[:, ds(it, 1), :].rearrange("p o c -> p (o c)") if n == 0 else mask_before[:]
                            after = mask_last[:, ds(it, 1), :].rearrange("p o c -> p (o c)") if n == SUB - 1 else mask_after[:]
                            band, context = S_SLOT[s][:, 0:3 * P], S_SLOT[s][:, 3 * P:5 * P]
                            pe.matmul(band, q_same[slot][:, h, :], keys[:, kv, local], start=True, stop=False)
                            pe.matmul(band, q_cross[slot][:, h, :], keys[:, kv, local], start=False, stop=False)
                            pe.matmul(band[:, 0:P], ident_bf[:], before, start=False, stop=False)
                            pe.matmul(band[:, 2 * P:3 * P], ident_bf[:], after, start=False, stop=True)
                            pe.matmul(context, q_same[slot][:, h, :], keys[:, kv, 0:L], start=True, stop=False)
                            pe.matmul(context, q_cross[slot][:, h, :], keys[:, kv, 0:L], start=False, stop=True).then_inc(s_sc, 1)
                        if 2 <= u < HEADS + 2:
                            w = u - 2
                            pe.wait_ge(s_exp, it * HEADS + w + 3)
                            for b in range(5):
                                i = w % 4 * 5 + b
                                Q = w // 4 * 5 + i // 4
                                if i % 4 == 0:
                                    pe.wait_ge(s_ptout, it * RING + ring(Q) + 1)
                                tp = pe.transpose(psum[:, PT_BANKS[ring(Q) % 3], i % 4 * P:(i % 4 + 1) * P], prob[w % 2][:, b * P:(b + 1) * P], ident[:])
                                if i % 4 == 3:
                                    tp.then_inc(s_pt, 1)
                                elif b == 4:
                                    tp.then_inc(s_pttail, 1)
                        if u % 8 == V_AT and u < HEADS:
                            n = u // 8
                            slot = (n + 1) % 2
                            pe.wait_ge(s_ptout, it * RING + ring_v(n) + 1)
                            turn_v(PT_BANKS[ring_v(n) % 3], slot, (it * 2 + n // 2) * 16 + (32 if slot == 1 else 48))
                        if u >= PV_AT and (u - PV_AT) % 4 == 0 and (u - PV_AT) // 4 < GROUPS:
                            G = (u - PV_AT) // 4
                            n, kv = G // 2, G % 2
                            pe.wait_ge(s_ptout, it * RING + (ring_v(n) if kv == 0 else ring(5 * G + 4)) + 4)
                            pe.wait_ge(s_misc, event(it, "pv", G) + 1)
                            times_v(G, (0, 1))
                        if u >= PV_END and (u - PV_END) % 4 == 0 and (u - PV_END) // 4 < GROUPS:
                            times_v((u - PV_END) // 4, (2, 3, 4)).then_inc(s_pv, 1)
                        if u > HEADS and not last:
                            gates(it + 1, *gate_share(u))

                rounds(pe, body)

            @block.vector
            def _(dve):
                dve.sem_inc(s_ptout, 3)
                dve.sem_inc(s_pv, 2)
                dve.sem_inc(s_turn, 1)
                dve.sem_inc(s_ssq, 1)
                dve.sem_inc(s_msq, 1)
                for kv in range(N_KV):
                    for at in (L, L + P + S):
                        dve.memset(keys[:, kv, at:at + P].bitcast(F32), 0.0).then_inc(s_pads, 1)
                dve.memset(v_ring[:, 3], 0.0).then_inc(s_pads, 1)
                dve.memset(oT[HEAD:P, :], 0.0).then_inc(s_pads, 1)
                for t in (g_r[0], g_i[0], g_i[1]):
                    dve.memset(t[:, L:LAT], 0.5).then_inc(s_gap, 1)
                dve.wait_ge(s_parT, 1)
                dve.tensor_copy(par[:], psum[:, 7, 0:44]).then_inc(s_parc, 1)
                def convolve(it, step):
                    j, half = step // 2, slice(step % 2 * (W // 2), (step % 2 + 1) * (W // 2))
                    shifted = x_pad[:, half.start + j:half.stop + j]
                    if step == 0:
                        for at, n in ((0, 2), (2 + L, GAP), (2 + W, 1)):
                            dve.memset(x_pad[:, at:at + n], 0.0).then_inc(s_pad0, 1)
                        dve.wait_ge(s_pad0, it * 3 + 3)
                        dve.wait_ge(s_xr, it * 32 + 32)
                    if j == 0:
                        dve.tensor_scalar(xc[:, half], shifted, par[:, ds(it + CONV_W, 1)], par[:, ds(it + CONV_B, 1)], ALU.mult, ALU.add).then_inc(s_v, 1)
                    else:
                        dve.wait_ge(s_v, it * DVE_RNN + step - 1)
                        dve.scalar_tensor_tensor(xc[:, half], shifted, par[:, ds(it + CONV_W + j * RNN_TILES, 1)], xc[:, half], ALU.mult, ALU.add).then_inc(s_v, 1)
                    if step == CONV_STEPS - 1:
                        dve.wait_ge(s_v, it * DVE_RNN + CONV_STEPS)
                        dve.memset(x_pad[:, L:LAT], 0.5).then_inc(s_gap, 1)

                def gate_biases(it):
                    dve.tensor_copy(gate_bias[:].rearrange("p (g o) -> p g o", o=1),
                                    par[:, B_A:B_A + 4 * RNN_TILES].rearrange("p (g f) -> p g f", f=RNN_TILES)[:, :, ds(it, 1)]).then_inc(s_gbias, 1)

                def cut_x(it):
                    dve.tensor_copy(xc_hi[:], xc[:]).then_inc(s_hi, 1)

                def cut_gates(it):
                    dve.wait_ge(s_gw, it * 64 + 64)
                    dve.tensor_copy(gate_hi[:], gate_raw[:]).then_inc(s_gwhi, 1)
                    dve.wait_ge(s_gwhi, it + 1)
                    dve.tensor_tensor(gate_lo[:], gate_raw[:], gate_hi[:].bitcast(F32), ALU.subtract).then_inc(s_gwlo, 1)

                for step in range(CONV_STEPS):
                    convolve(0, step)
                cut_x(0)
                dve.wait_ge(s_hi, 1)
                dve.tensor_tensor(xc_lo[:], xc[:], xc_hi[:].bitcast(F32), ALU.subtract).then_inc(s_lo, 1)
                cut_gates(0)
                gate_biases(0)

                dve.wait_ge(s_sink, 16)
                dve.tensor_scalar(neg_sink[:], sink[:], -1.0, None, ALU.mult).then_inc(s_mx, 1)
                dve.wait_ge(s_parc, 3)
                dve.tensor_scalar(sp_s[:], sp_e[:], 2.0, None, ALU.add).then_inc(s_parc, 1)
                dve.wait_ge(s_parc, 4)
                dve.reciprocal(sp_s[:], sp_s[:]).then_inc(s_parc, 1)
                dve.wait_ge(s_parc, 5)
                dve.tensor_tensor(sp_s[:], sp_s[:], sp_e[:], ALU.mult).then_inc(s_parc, 1)
                dve.wait_ge(s_parc, 6)
                dve.tensor_tensor(sp_e[:], sp_s[:], sp_s[:], ALU.mult).then_inc(s_parc, 1)
                dve.memset(sp_p[:], 1.0 / 17).then_inc(s_parc, 1)
                dve.wait_ge(s_parc, 8)
                for j, odd in enumerate((15, 13, 11, 9, 7, 5, 3, 1)):
                    dve.tensor_tensor(sp_p[:], sp_p[:], sp_e[:], ALU.mult).then_inc(s_series, 1)
                    dve.wait_ge(s_series, 2 * j + 1)
                    dve.tensor_scalar(sp_p[:], sp_p[:], 1.0 / odd, None, ALU.add).then_inc(s_series, 1)
                    dve.wait_ge(s_series, 2 * j + 2)
                dve.scalar_tensor_tensor(sp_p[:], sp_p[:], 2.0, sp_s[:], ALU.mult, ALU.mult).then_inc(s_parc, 1)
                dve.tensor_scalar(sp_pos[:], par[:, LAM:LAM + 8], -1.0, 0.0, ALU.mult, ALU.max).then_inc(s_parc, 1)
                dve.wait_ge(s_parc, 10)
                dve.tensor_tensor(sp_p[:], sp_p[:], sp_pos[:], ALU.add).then_inc(s_parc, 1)
                dve.wait_ge(s_parc, 11)
                dve.tensor_scalar(c_exp[:], sp_p[:], -LRU_C, None, ALU.mult).then_inc(s_parc, 1)
                dve.tensor_scalar(c_tanh[:], sp_p[:], LRU_C / 2, None, ALU.mult).then_inc(s_parc, 1)
                for count, v_block in enumerate((v_ctx[:, 0], v_ctx[:, 1], v_ring[:, 0])):
                    dve.wait_ge(s_vt, count + 1)
                    dve.tensor_copy(v_block, psum[:, MISC, 0:P]).then_inc(s_misc, 1)


                def body(it, last):
                    base = it * DVE_RNN + CONV_STEPS
                    for u in range(STEPS):
                        if u >= COPY_AT and (u - COPY_AT) % 4 == 0 and (u - COPY_AT) // 4 < GROUPS:
                            G = (u - COPY_AT) // 4
                            dve.wait_ge(s_pv, it * GROUPS + G + 3)
                            dve.wait_ge(s_turn, it * GROUPS + G + 1)
                            dve.tensor_copy(oT[0:HEAD, :], psum[0:HEAD, MISC, :]).then_inc(s_misc, 1)
                        if u < HEADS:
                            s, h, n = u % 2, u % 8, (u // 8) % 2
                            dve.wait_ge(s_sc, it * HEADS + u + 1)
                            dve.reduce_max(row_max[n][:, h:h + 1], S_SLOT[s], AX_X).then_inc(s_mx, 1)
                        if u < HEADS:
                            dve.wait_ge(s_mx, it * HEADS + u + 2)
                            dve.tensor_scalar(neg_max[n][:, h:h + 1], row_max[n][:, h:h + 1], -SCALE, neg_sink[:, h:h + 1], ALU.mult, ALU.min).then_inc(s_nm, 1)
                            if u % 4 == 3:
                                kv = h // 4
                                dve.wait_ge(s_nm, it * HEADS + u + 1)
                                dve.tensor_tensor(sink_in[n][:, kv * 4:kv * 4 + 4], sink[:, kv * 4:kv * 4 + 4], neg_max[n][:, kv * 4:kv * 4 + 4], ALU.add).then_inc(s_sin, 1)
                        if u % 4 == 1 and 5 <= u <= HEADS + 1:
                            G = u // 4 - 1
                            n, kv = (G // 2) % 2, G % 2
                            cols = slice(kv * 4, kv * 4 + 4)
                            dve.wait_ge(s_ses, it * GROUPS + G + 1)
                            dve.tensor_tensor(inv_sum[n][:, cols], sink_exp[n][:, cols], row_sum[n][:, cols], ALU.add).then_inc(s_den, 1)
                            dve.wait_ge(s_den, it * GROUPS + G + 1)
                            dve.reciprocal(inv_sum[n][:, cols], inv_sum[n][:, cols]).then_inc(s_inv, 1)
                        if u >= TURN_AT and (u - TURN_AT) % 4 == 0 and (u - TURN_AT) // 4 < GROUPS:
                            G = (u - TURN_AT) // 4
                            n, kv = (G // 2) % 2, G % 2
                            dve.wait_ge(s_turn, it * GROUPS + G + 2)
                            dve.wait_ge(s_inv, it * GROUPS + G + 1)
                            dve.wait_ge(s_ostored[n], (it * 2 + G // 4) * 16 + 16)
                            dve.tensor_tensor(o_tok[n][:, kv * 256:(kv + 1) * 256].rearrange("p (h d) -> p h d", h=PER_KV),
                                              psum[:, MISC, :].rearrange("p (h d) -> p h d", h=PER_KV)[:, :, 0:HEAD],
                                              inv_sum[n][:, kv * 4:kv * 4 + 4].rearrange("p (h o) -> p h o", o=1).broadcast_to([P, PER_KV, HEAD]), ALU.mult).then_inc(s_misc, 1)
                            if kv == 1:
                                dve.wait_ge(s_misc, event(it, "turn", G) + 2)
                                dve.wait_ge(s_ssq, it * SUB + G // 2 + 1)
                                dve.wait_ge(s_msq, it * SUB + G // 2 + 1)
                                dve.tensor_tensor_reduce(o_junk[:], o_tok[n][:], o_tok[n][:], 1.0, 0.0, ALU.mult, ALU.add,
                                                         o_ssq[:]).then_inc(s_ssq, 1)
                                dve.wait_ge(s_ssq, it * SUB + G // 2 + 2)
                                dve.tensor_scalar(keep["msq_attn"][:, ds(it * SUB + G // 2, 1)], o_ssq[:], 1.0 / D_ATTN, EPS, ALU.mult, ALU.add).then_inc(s_msq, 1)
                        if 0 <= u - ROOT_AT - 2 < 4:
                            d, part = divmod(u - ROOT_AT - 2, 2)
                            half = slice(part * (W // 2), (part + 1) * (W // 2))
                            dve.wait_ge(s_sq, it * 2 + d + 1)
                            dve.wait_ge(s_a, it * 2 + d + 1)
                            dve.scalar_tensor_tensor(th[d][:, half], g_r[d][:, half], 1.0, th[d][:, half], ALU.add, ALU.mult).then_inc(s_v, 1)
                        if u in SCAN_AT:
                            d, part = SCAN_AT.index(u) // 2, SCAN_AT.index(u) % 2
                            dve.wait_ge(s_u, it * 2 + d + 1)
                            if d == 0:
                                pieces = ((0, L, 0.0), (LAT, S // 2, g_i[0][:, L - 1:L]), (LAT + S // 2, S // 2, g_i[0][:, LAT + S // 2 - 1:LAT + S // 2]))
                            else:
                                pieces = ((0, L, 0.0), (LAT + S // 2, S // 2, g_i[1][:, 0:1]), (LAT, S // 2, g_i[1][:, LAT + S // 2:LAT + S // 2 + 1]))
                            for i in ((0, 1), (2,))[part]:
                                t0, n, state = pieces[i]
                                dve.wait_ge(s_v, base + 4 + 3 * d + i)
                                tok, forward = slice(t0, t0 + n), slice(None, None, 1 - 2 * d)
                                dve.tensor_tensor_scan(g_i[d][:, tok][:, forward], g_r[d][:, tok][:, forward], th[d][:, tok][:, forward], state, ALU.mult, ALU.add).then_inc(s_v, 1)
                        if CONV_AT <= u < CONV_AT + CONV_STEPS and not last:
                            convolve(it + 1, u - CONV_AT)
                        if u == CONV_AT + CONV_STEPS and not last:
                            cut_x(it + 1)
                        if u == CONV_AT + CONV_STEPS + 1 and not last:
                            cut_gates(it + 1)
                            gate_biases(it + 1)

                rounds(dve, body)
                dve.wait_ge(s_msq, NB + 1)


def output_projection(k, a, x1, rstd2, keep, scratch):
    nc, psum = k.nc, k.psum
    with ExitStack() as ctx:
        def sb(name, shape, dt=F32):
            return ctx.enter_context(nc.sbuf_tensor(name, shape, dt))

        w_raw = [sb(f"wout_raw{i}", [P, D]) for i in range(2)]
        w_hi, w_lo = sb("wout_hi", [P, KD, D], F32R), sb("wout_lo", [P, KD, D], F32R)
        gain_rows, gain = sb("gain_rows", [4 * KD, P]), sb("gain_cols", [P, 4 * KD])
        rnn = [sb(f"rnn{i}", [P, RNN_TILES, P]) for i in range(2)]
        att = [sb(f"att{i}", [P, D_ATTN]) for i in range(2)]
        mix_hi = [sb(f"mix_hi{i}", [P, KD, P], F32R) for i in range(2)]
        mix_lo = [sb(f"mix_lo{i}", [P, KD, P], F32R) for i in range(2)]
        square, square_sum = sb("rnn_square", [P, RNN_TILES, P]), sb("rnn_square_sum", [P, P])
        x_in = [sb(f"x_in{i}", [P, D]) for i in range(2)]
        part = [sb(f"rnn_part{i}", [P, CH]) for i in range(2)]
        g1 = sb("g1_wide", [P, D])
        junk = [sb(f"x1_square_junk{i}", [P, D], BF16) for i in range(2)]
        ones, eps_col = sb("ones_col", [P, 1]), sb("eps_col4", [P, 1])
        newton, msq_r = sb("newton4", [P, NB]), sb("rnn_msq", [P, 1])
        rstd_a, rstd_r, ssq2 = sb("rstd_attn", [P, NB]), [sb(f"rstd_rnn{i}", [P, 1]) for i in range(2)], sb("ssq2", [P, NB])

        s_gain = k.sem("gains_landed")
        s_gainT = k.sem("gains_transposed")
        s_gainc = k.sem("gain_cols_ready")
        s_const = k.sem("out_constants_ready")
        s_w = [k.sem(f"wout_landed{i}") for i in range(2)]
        s_ws = k.sem("wout_scaled")
        s_whi = k.sem("wout_hi_ready")
        s_wlo = k.sem("wout_lo_ready")
        s_mix = [k.sem(f"rnn_landed{i}") for i in range(2)]
        s_att = [k.sem(f"att_landed{i}") for i in range(2)]
        s_turn = k.sem("att_turned")
        s_ahi = k.sem("att_hi_ready")
        s_alo = k.sem("att_lo_ready")
        s_root = k.sem("mixer_rsqrt_refined")
        s_x = [k.sem(f"x_in_landed{i}") for i in range(2)]
        s_g1 = k.sem("g1_landed")
        s_hi = k.sem("rnn_hi_ready")
        s_lo = k.sem("rnn_lo_ready")
        s_sq = k.sem("rnn_squared")
        s_sqs = k.sem("rnn_squares_summed")
        s_ss = k.sem("rnn_sumsq_ready")
        s_std = k.sem("rnn_std_ready")
        s_rstd = k.sem("rnn_rstd_ready")
        s_rstda = k.sem("attn_rstd_ready")
        s_acc = k.sem("out_accumulated")
        s_part = k.sem("rnn_part_ready")
        s_mid = k.sem("parts_joined")
        s_gated = k.sem("mixer_gated")
        s_x1 = k.sem("x1_ready")
        s_ss2 = k.sem("x1_squared")
        s_x1st = k.sem("x1_stored")

        SS_BANK, TURN_BANK = 4, 6

        with nc.Block() as block:

            @block.sync
            def _(sp):
                sp.dma_start(gain_rows[0:RNN_TILES, :], a["gn_rnn"].rearrange("a (k p) -> (a k) p", p=P)).then_inc(s_gain, 16)
                sp.dma_start(gain_rows[RNN_TILES:KD, :], a["gn_attn"].rearrange("a (k p) -> (a k) p", p=P)).then_inc(s_gain, 16)

                sp.dma_start(gain_rows[KD:3 * KD, :], scratch["mod"][0, 3 * D:5 * D].rearrange("(m p) -> m p", p=P)).then_inc(s_gain, 16)
                sp.dma_start(gain_rows[3 * KD:4 * KD, :], a["norm2_g"].rearrange("a (k p) -> (a k) p", p=P)).then_inc(s_gain, 16)

                def load(n, s):
                    sp.wait_ge(s_lo, n + 1)
                    sp.wait_ge(s_sq, n + 1)
                    sp.dma_start(rnn[s][:], scratch["mix"][:, ds(n * P, P)].rearrange("(k p) t -> p k t", p=P)).then_inc(s_mix[s], 16)
                    sp.wait_ge(s_turn, n + 1)
                    sp.dma_start(att[s][:], scratch["att"][ds(n * P, P), :]).then_inc(s_att[s], 16)
                    sp.wait_ge(s_x1, n + 1)
                    sp.dma_start(x_in[s][:], a["x"][0, ds(n * P, P), :]).then_inc(s_x[s], 16)

                def store(n):
                    sp.wait_ge(s_x1, n + 3)
                    sp.dma_start(scratch["x1"][ds(n * P, P), :], x1[:, ds(n, 1), :].rearrange("p o d -> p (o d)")).then_inc(s_x1st, 16)

                for kt in range(KD):
                    sp.wait_ge(s_wlo, kt + 1)
                    sp.dma_start(w_raw[kt % 2][:], a["w_out"][0, kt * P:(kt + 1) * P, :]).then_inc(s_w[kt % 2], 16)
                    if kt == 1:
                        load(0, 0)
                        load(1, 1)
                        sp.dma_start(g1[:], scratch["mod"][0:1, 2 * D:3 * D].broadcast_to([P, D])).then_inc(s_g1, 16)
                with sp.Fori(0, NB // 2 - 1) as i:
                    for s in range(2):
                        load(i * 2 + s + 2, s)
                        store(i * 2 + s)
                store(NB - 2)
                store(NB - 1)
                sp.wait_ge(s_x1st, 16 * NB)

            @block.gpsimd
            def _(pool):
                nc.gpsimd.memset(ones[:], 1.0).then_inc(s_const, 1)
                nc.gpsimd.memset(eps_col[:], EPS).then_inc(s_const, 1)

                def cut(n, s):
                    pool.wait_ge(s_hi, n + 1)
                    nc.gpsimd.tensor_tensor(mix_lo[s][:, 0:RNN_TILES, :], rnn[s][:], mix_hi[s][:, 0:RNN_TILES, :].bitcast(F32), ALU.subtract).then_inc(s_lo, 1)

                def residual(n, s, turn):
                    pool.wait_ge(s_x[s], turn * 16 + 16)
                    pool.wait_ge(s_gated, n + 1)
                    tile = x1[:, ds(n, 1), :].rearrange("p o d -> p (o d)")
                    nc.gpsimd.tensor_tensor(tile, tile, x_in[s][:], ALU.add).then_inc(s_x1, 1)

                cut(0, 0)
                with pool.Fori(0, NB // 2 - 1) as i:
                    cut(i * 2 + 1, 1)
                    residual(i * 2, 0, i)
                    cut(i * 2 + 2, 0)
                    residual(i * 2 + 1, 1, i)
                cut(NB - 1, 1)
                residual(NB - 2, 0, NB // 2 - 1)
                residual(NB - 1, 1, NB // 2 - 1)

            @block.scalar
            def _(act):
                act.sem_inc(s_wlo, 2)
                act.sem_inc(s_lo, 2)
                act.sem_inc(s_sq, 2)
                act.sem_inc(s_x1, 2)
                act.sem_inc(s_acc, 4)
                act.sem_inc(s_turn, 2)
                act.sem_inc(s_alo, 2)
                act.sem_inc(s_mid, 2)
                act.sem_inc(s_sqs, 1)
                act.sem_inc(s_ss, 1)
                act.wait_ge(s_const, 2)
                act.activation(rstd_a[:], keep["msq_attn"][:], ACT.Sqrt).then_inc(s_rstda, 1)

                def cut(n, s, turn):
                    act.wait_ge(s_mix[s], turn * 16 + 16)
                    act.wait_ge(s_acc, n * 2 + 2)
                    act.activation(mix_hi[s][:, 0:RNN_TILES, :], rnn[s][:], ACT.Copy).then_inc(s_hi, 1)
                    act.wait_ge(s_sqs, n + 1)
                    act.activation(square[:], rnn[s][:], ACT.Square).then_inc(s_sq, 1)
                    act.wait_ge(s_turn, n + 3)
                    act.activation(mix_hi[s][:, RNN_TILES:KD, :].rearrange("p k t -> p (k t)"), psum[:, TURN_BANK + s, :], ACT.Copy).then_inc(s_ahi, 1)

                def finish(n, s):
                    act.wait_ge(s_ss, n + 2)
                    act.activation(rstd_r[s][:], psum[:, SS_BANK + s, 0:1], ACT.Sqrt, bias=eps_col[:], scale=1.0 / D_RNN).then_inc(s_std, 1)
                    act.wait_ge(s_root, n * 4 + 8)
                    for half in range(2):
                        act.wait_ge(s_acc, n * 2 + half + 5)
                        act.activation(part[half][:], psum[:, 2 * half, :], ACT.Copy, scale=rstd_r[s][:]).then_inc(s_part, 1)

                def square_x1(n, s):
                    act.wait_ge(s_x1, n + 3)
                    act.activation(junk[s][:], x1[:, ds(n, 1), :].rearrange("p o d -> p (o d)"), ACT.Square, accum_out=ssq2[:, ds(n, 1)]).then_inc(s_ss2, 1)

                cut(0, 0, 0)
                act.wait_ge(s_gainc, 1)
                for kt in range(KD):
                    act.wait_ge(s_w[kt % 2], (kt // 2) * 16 + 16)
                    act.activation(w_raw[kt % 2][:], w_raw[kt % 2][:], ACT.Copy, scale=gain[:, kt:kt + 1]).then_inc(s_ws, 1)
                    act.wait_ge(s_ws, kt + 1)
                    act.activation(w_hi[:, kt, :], w_raw[kt % 2][:], ACT.Copy).then_inc(s_whi, 1)
                cut(1, 1, 0)
                finish(0, 0)
                with act.Fori(0, NB // 2 - 1) as i:
                    cut(i * 2 + 2, 0, i + 1)
                    finish(i * 2 + 1, 1)
                    square_x1(i * 2, 0)
                    cut(i * 2 + 3, 1, i + 1)
                    finish(i * 2 + 2, 0)
                    square_x1(i * 2 + 1, 1)
                finish(NB - 1, 1)
                square_x1(NB - 2, 0)
                square_x1(NB - 1, 1)
                act.wait_ge(s_ss2, NB)
                act.activation(rstd2[:], ssq2[:], ACT.Sqrt, bias=eps_col[:], scale=1.0 / D).then_inc(s_ss2, 1)

            @block.tensor
            def _(pe):
                pe.wait_ge(s_gain, 64)
                pe.transpose(psum[:, SS_BANK, 0:4 * KD], gain_rows[:], keep["ident"][0:4 * KD, 0:4 * KD]).then_inc(s_gainT, 1)

                def turn(n, s, turn_count):
                    pe.wait_ge(s_att[s], turn_count * 16 + 16)
                    pe.wait_ge(s_alo, n + 1)
                    for f in range(KD - RNN_TILES):
                        tp = pe.transpose(psum[:, TURN_BANK + s, f * P:(f + 1) * P], att[s][:, f * P:(f + 1) * P], keep["ident"][:])
                    tp.then_inc(s_turn, 1)

                def tile(n, s, first):
                    pe.wait_ge(s_sqs, n + 2)
                    if first:
                        pe.wait_ge(s_gainc, 1)
                        pe.wait_ge(s_const, 2)
                    pe.matmul(psum[:, SS_BANK + s, 0:1], square_sum[:], ones[:], start=True, stop=True).then_inc(s_ss, 1)
                    pe.wait_ge(s_lo, n + 3)
                    pe.wait_ge(s_alo, n + 3)
                    for half in range(2):
                        pe.wait_ge(s_mid, n * 2 + half + 1)
                        for group in range(2):
                            for kt in range(group * RNN_TILES, (group + 1) * RNN_TILES):
                                if first and half == 0:
                                    pe.wait_ge(s_wlo, kt + 3)
                                at, end = kt == group * RNN_TILES, kt == (group + 1) * RNN_TILES - 1
                                cols = slice(half * CH, (half + 1) * CH)
                                pe.matmul(psum[:, 2 * half + group, :], mix_hi[s][:, kt, :], w_hi[:, kt, cols], start=at, stop=False)
                                pe.matmul(psum[:, 2 * half + group, :], mix_hi[s][:, kt, :], w_lo[:, kt, cols], start=False, stop=False)
                                mm = pe.matmul(psum[:, 2 * half + group, :], mix_lo[s][:, kt, :], w_hi[:, kt, cols], start=False, stop=end)
                        mm.then_inc(s_acc, 1)

                turn(0, 0, 0)
                turn(1, 1, 0)
                tile(0, 0, True)
                with pe.Fori(0, NB // 2 - 1) as i:
                    turn(i * 2 + 2, 0, i + 1)
                    tile(i * 2 + 1, 1, False)
                    turn(i * 2 + 3, 1, i + 1)
                    tile(i * 2 + 2, 0, False)
                tile(NB - 1, 1, False)

            @block.vector
            def _(dve):
                dve.wait_ge(s_gainT, 1)
                dve.tensor_copy(gain[:], psum[:, SS_BANK, 0:4 * KD]).then_inc(s_gainc, 1)
                dve.wait_ge(s_gainc, 1)
                dve.scalar_tensor_tensor(keep["aff2"][:, 0, :], gain[:, 2 * KD:3 * KD], 1.0, gain[:, 3 * KD:4 * KD], ALU.add, ALU.mult).then_inc(s_gainc, 1)
                dve.tensor_copy(keep["aff2"][:, 1, :], gain[:, KD:2 * KD]).then_inc(s_gainc, 1)
                dve.wait_ge(s_rstda, 1)
                dve.reciprocal(rstd_a[:], rstd_a[:]).then_inc(s_rstda, 1)
                dve.wait_ge(s_rstda, 2)
                refine_rsqrt(dve, rstd_a[:], keep["msq_attn"][:], newton[:], s_root, 0)

                def cut(n, s):
                    dve.wait_ge(s_ahi, n + 1)
                    hi = mix_hi[s][:, RNN_TILES:KD, :].rearrange("p k t -> p (k t)")
                    dve.tensor_tensor(mix_lo[s][:, RNN_TILES:KD, :].rearrange("p k t -> p (k t)"), psum[:, TURN_BANK + s, :], hi.bitcast(F32), ALU.subtract).then_inc(s_alo, 1)

                def sum_squares(n):
                    dve.wait_ge(s_sq, n + 3)
                    dve.wait_ge(s_ss, n + 1)
                    dve.tensor_reduce(square_sum[:], square[:].rearrange("p f t -> p t f"), AX_X, ALU.add).then_inc(s_sqs, 1)

                def finish(n, s):
                    dve.wait_ge(s_std, n + 1)
                    dve.tensor_scalar(msq_r[:], psum[:, SS_BANK + s, 0:1], 1.0 / D_RNN, EPS, ALU.mult, ALU.add).then_inc(s_rstd, 1)
                    dve.reciprocal(rstd_r[s][:], rstd_r[s][:]).then_inc(s_rstd, 1)
                    dve.wait_ge(s_rstd, n * 2 + 2)
                    refine_rsqrt(dve, rstd_r[s][:], msq_r[:], newton[:, 0:1], s_root, n * 4 + 4)
                    for half in range(2):
                        dve.wait_ge(s_part, n * 2 + half + 1)
                        dve.scalar_tensor_tensor(x1[:, ds(n, 1), half * CH:(half + 1) * CH].rearrange("p o d -> p (o d)"), psum[:, 2 * half + 1, :],
                                                 rstd_a[:, ds(n, 1)], part[half][:], ALU.mult, ALU.add).then_inc(s_mid, 1)
                    dve.wait_ge(s_mid, n * 2 + 4)
                    tile = x1[:, ds(n, 1), :].rearrange("p o d -> p (o d)")
                    dve.tensor_tensor(tile, tile, g1[:], ALU.mult).then_inc(s_gated, 1)

                sum_squares(0)
                cut(0, 0)
                for kt in range(KD):
                    dve.wait_ge(s_whi, kt + 1)
                    dve.tensor_tensor(w_lo[:, kt, :], w_raw[kt % 2][:], w_hi[:, kt, :].bitcast(F32), ALU.subtract).then_inc(s_wlo, 1)
                sum_squares(1)
                cut(1, 1)
                dve.wait_ge(s_g1, 16)
                finish(0, 0)
                with dve.Fori(0, NB // 2 - 1) as i:
                    sum_squares(i * 2 + 2)
                    cut(i * 2 + 2, 0)
                    finish(i * 2 + 1, 1)
                    sum_squares(i * 2 + 3)
                    cut(i * 2 + 3, 1)
                    finish(i * 2 + 2, 0)
                finish(NB - 1, 1)
                dve.wait_ge(s_ss2, NB + 1)
                dve.reciprocal(rstd2[:], rstd2[:]).then_inc(s_rstda, 1)
                dve.tensor_scalar(ssq2[:], ssq2[:], 1.0 / D, EPS, ALU.mult, ALU.add).then_inc(s_rstda, 1)
                dve.wait_ge(s_rstda, 4)
                refine_rsqrt(dve, rstd2[:], ssq2[:], newton[:], s_root, 4 + 4 * NB)


def modulate_x1(k, x1, rstd2, h2T_hi, h2T_lo, keep):
    nc, psum = k.nc, k.psum
    ident, aff2 = keep["ident"], keep["aff2"]
    QUADS = NB // 4
    with ExitStack() as ctx:
        xn = [ctx.enter_context(nc.sbuf_tensor(f"x1_norm{i}", [P, 4, 2 * P], F32)) for i in range(2)]
        t32 = [ctx.enter_context(nc.sbuf_tensor(f"t2_{i}", [P, CH], F32)) for i in range(2)]
        s_xn = k.sem("x1_normalised")
        s_tp = k.sem("x1_transposed")
        s_t32 = k.sem("x1_modulated")
        s_hi = k.sem("h2T_hi_ready")
        s_lo = k.sem("h2T_lo_ready")

        with nc.Block() as block:

            @block.gpsimd
            def _(pool):
                with pool.Fori(0, QUADS) as q:
                    for pair in range(KD // 2):
                        pool.wait_ge(s_tp, q * KD + pair * 2 + 2)
                        nc.gpsimd.tensor_tensor(xn[pair % 2][:], x1[:, ds(q * 4, 4), pair * 2 * P:(pair + 1) * 2 * P],
                                                rstd2[:, ds(q * 4, 4)].rearrange("p (n o) -> p n o", o=1).broadcast_to([P, 4, 2 * P]), ALU.mult).then_inc(s_xn, 1)

            @block.tensor
            def _(pe):
                with pe.Fori(0, QUADS) as q:
                    for kt in range(KD):
                        pe.wait_ge(s_xn, q * (KD // 2) + kt // 2 + 1)
                        pe.wait_ge(s_t32, q * KD + kt + 1)
                        for j in range(4):
                            tp = pe.transpose(psum[:, kt, j * P:(j + 1) * P], xn[kt // 2 % 2][:, j, (kt % 2) * P:(kt % 2 + 1) * P], ident[:])
                        tp.then_inc(s_tp, 1)

            @block.scalar
            def _(act):
                act.sem_inc(s_t32, KD)
                act.sem_inc(s_tp, 4)
                act.sem_inc(s_lo, 2)
                with act.Fori(0, QUADS) as q:
                    for kt in range(KD):
                        act.wait_ge(s_tp, q * KD + kt + 5)
                        act.wait_ge(s_lo, q * KD + kt + 1)
                        act.activation(t32[kt % 2][:], psum[:, kt, :], ACT.Identity, bias=aff2[:, 1, kt:kt + 1], scale=aff2[:, 0, kt:kt + 1]).then_inc(s_t32, 1)

            @block.vector
            def _(dve):
                with dve.Fori(0, QUADS) as q:
                    for kt in range(KD):
                        dve.wait_ge(s_t32, q * KD + kt + 1 + KD)
                        hi = h2T_hi[:, kt, ds(q * CH, CH)]
                        dve.tensor_copy(hi, t32[kt % 2][:]).then_inc(s_hi, 1)
                        dve.wait_ge(s_hi, q * KD + kt + 1)
                        dve.tensor_tensor(h2T_lo[:, kt, ds(q * CH, CH)], t32[kt % 2][:], hi.bitcast(F32), ALU.subtract).then_inc(s_lo, 1)


def up_projection(k, a, h2T_hi, h2T_lo, keep, scratch):
    nc, psum = k.nc, k.psum
    with ExitStack() as ctx:
        def sb(name, shape, dt=F32):
            return ctx.enter_context(nc.sbuf_tensor(name, shape, dt))

        CUT = (NCH - 1) * CH - 1
        w_raw = [sb(f"wup_raw{g}", [P, KD, P]) for g in range(2)]
        w_hi = [sb(f"wup_hi{g}", [P, KD, P], F32R) for g in range(2)]
        w_lo = [sb(f"wup_lo{g}", [P, KD, P], F32R) for g in range(2)]
        u_pad = [sb(f"u_pad{g}", [P, S + 2]) for g in range(2)]
        acc = [sb(f"conv_acc{g}", [P, S]) for g in range(2)]
        act_out = [sb(f"act_out{i}", [P, S]) for i in range(2)]
        par_rows = [sb(f"conv_rows{i}", [4 * FT, P]) for i in range(2)]
        par = sb("conv_cols", [P, 8 * FT])

        s_par = k.sem("conv_params_landed")
        s_parT = k.sem("conv_params_transposed")
        s_parc = k.sem("conv_cols_ready")
        s_pad = k.sem("pad_columns_ready")
        s_w = [k.sem(f"wup_landed{g}") for g in range(2)]
        s_whi = k.sem("wup_hi_ready")
        s_wlo = k.sem("wup_lo_ready")
        s_mm = k.sem("up_accumulated")
        s_evac = k.sem("up_evacuated")
        s_tap = k.sem("conv_tap_added")
        s_conv = k.sem("conv_ready")
        s_silu = k.sem("gate_silu_ready")
        s_prod = k.sem("act_ready")
        s_stored = [k.sem(f"act_stored{i}") for i in range(2)]
        s_last = [k.sem(f"act_last_stored{i}") for i in range(2)]

        with nc.Block() as block:

            @block.sync
            def _(sp):
                sp.sem_inc(s_stored[0], 16)
                sp.sem_inc(s_stored[1], 16)

                def load(j, g):
                    sp.wait_ge(s_wlo, j * 2 + g + 1)
                    sp.dma_start(w_raw[g][:], a["w_up"][0, :, ds(j * P + g * D_FF, P)].rearrange("(k p) n -> p k n", p=P)).then_inc(s_w[g], 16)

                def store(j, i):
                    sp.wait_ge(s_prod, j + 2)
                    sp.dma_start(scratch["act"][:, :, ds(j, 1), :].rearrange("n p o t -> p (n o) t"),
                                 act_out[i][:].rearrange("p (n t) -> p n t", t=P)).then_inc(s_stored[i], 16)

                load(0, 0)
                load(0, 1)
                for i in range(2):
                    for half in range(2):
                        src = a["ffn_conv_b"] if (i, half) == (1, 1) else a["ffn_conv_w"][:, 2 * i + half, :]
                        sp.dma_start(par_rows[i][half * 2 * FT:(half + 1) * 2 * FT, :], src.rearrange("a (t p) -> (a t) p", p=P)).then_inc(s_par, 16)
                with sp.Fori(0, FT // 2 - 1) as i:
                    for m in range(2):
                        load(i * 2 + m + 1, 0)
                        load(i * 2 + m + 1, 1)
                        store(i * 2 + m, m)
                load(FT - 1, 0)
                load(FT - 1, 1)
                store(FT - 2, 0)
                blocks = CUT // P
                for part, (n0, n1) in enumerate(((0, blocks), (blocks, NB))):
                    sp.wait_ge(s_prod, FT + 1 + part)
                    sp.dma_start(scratch["act"][n0:n1, :, FT - 1, :].rearrange("n p t -> p n t"),
                                 act_out[1][:, n0 * P:n1 * P].rearrange("p (n t) -> p n t", t=P)).then_inc(s_last[part], 16)
                sp.wait_ge(s_stored[0], 16 + 16 * (FT // 2))
                sp.wait_ge(s_stored[1], 16 * (FT // 2))
                for i in range(2):
                    sp.wait_ge(s_last[i], 16)

            @block.gpsimd
            def _(pool):
                with pool.Fori(0, FT) as j:
                    for g in range(2):
                        pool.wait_ge(s_whi, j * 2 + g + 1)
                        nc.gpsimd.tensor_tensor(w_lo[g][:], w_raw[g][:], w_hi[g][:].bitcast(F32), ALU.subtract).then_inc(s_wlo, 1)

            @block.scalar
            def _(act):
                act.sem_inc(s_wlo, 2)
                act.sem_inc(s_evac, 8)
                act.sem_inc(s_conv, 2)
                act.sem_inc(s_prod, 1)

                def cut(j, g):
                    act.wait_ge(s_w[g], j * 16 + 16)
                    act.activation(w_hi[g][:], w_raw[g][:], ACT.Copy).then_inc(s_whi, 1)

                def evacuate(j, g, c):
                    act.wait_ge(s_mm, j * 8 + g * 4 + c + 1)
                    if c == 0:
                        act.wait_ge(s_conv, j * 2 + g + 1)
                    act.activation(u_pad[g][:, 1 + c * CH:1 + (c + 1) * CH], psum[:, 4 * g + c, :], ACT.Copy).then_inc(s_evac, 1)

                def silu(j):
                    act.wait_ge(s_conv, j * 2 + 3)
                    act.activation(acc[0][:], acc[0][:], ACT.Silu).then_inc(s_silu, 1)

                def channels(j, last):
                    cut(j, 1)
                    for c in range(NCH):
                        evacuate(j, 0, c)
                    if not last:
                        cut(j + 1, 0)
                    evacuate(j, 1, 0)
                    evacuate(j, 1, 1)
                    silu(j)
                    evacuate(j, 1, 2)
                    evacuate(j, 1, 3)

                cut(0, 0)
                with act.Fori(0, FT - 1) as j:
                    channels(j, False)
                channels(FT - 1, True)

            @block.tensor
            def _(pe):
                pe.wait_ge(s_par, 64)
                for i in range(2):
                    tp = pe.transpose(psum[:, 7, i * 4 * FT:(i + 1) * 4 * FT], par_rows[i][:], keep["ident"][0:4 * FT, 0:4 * FT])
                tp.then_inc(s_parT, 1)
                pe.wait_ge(s_parc, 1)
                with pe.Fori(0, FT) as j:
                    for g in range(2):
                        pe.wait_ge(s_wlo, j * 2 + g + 3)
                        for c in range(NCH):
                            pe.wait_ge(s_evac, j * 8 + g * 4 + c + 1)
                            bank, cols = psum[:, 4 * g + c, :], slice(c * CH, (c + 1) * CH)
                            for kt in range(KD):
                                pe.matmul(bank, w_hi[g][:, kt, :], h2T_hi[:, kt, cols], start=(kt == 0), stop=False)
                                pe.matmul(bank, w_hi[g][:, kt, :], h2T_lo[:, kt, cols], start=False, stop=False)
                                mm = pe.matmul(bank, w_lo[g][:, kt, :], h2T_hi[:, kt, cols], start=False, stop=(kt == KD - 1))
                            mm.then_inc(s_mm, 1)

            @block.vector
            def _(dve):
                for g in range(2):
                    for at in (0, S + 1):
                        dve.memset(u_pad[g][:, at:at + 1], 0.0).then_inc(s_pad, 1)
                dve.wait_ge(s_parT, 1)
                dve.tensor_copy(par[:], psum[:, 7, 0:8 * FT]).then_inc(s_parc, 1)
                dve.wait_ge(s_parc, 1)
                dve.wait_ge(s_pad, 4)

                def col(which, j, g):
                    return par[:, ds(j + which * 2 * FT + g * FT, 1)]

                def convolve(j, g, t0=0, t1=S, chunks=NCH, taps=0):
                    dve.wait_ge(s_evac, j * 8 + g * 4 + 8 + chunks)
                    dve.wait_ge(s_prod, j + 1)
                    dve.tensor_scalar(acc[g][:, t0:t1], u_pad[g][:, t0 + 1:t1 + 1], col(1, j, g), col(3, j, g), ALU.mult, ALU.add).then_inc(s_tap, 1)
                    dve.wait_ge(s_tap, j * 4 + g * 2 + taps + 1)
                    dve.scalar_tensor_tensor(acc[g][:, t0:t1], u_pad[g][:, t0:t1], col(0, j, g), acc[g][:, t0:t1], ALU.mult, ALU.add).then_inc(s_tap, 1)
                    dve.wait_ge(s_tap, j * 4 + g * 2 + taps + 2)
                    dve.scalar_tensor_tensor(acc[g][:, t0:t1], u_pad[g][:, t0 + 2:t1 + 2], col(2, j, g), acc[g][:, t0:t1], ALU.mult, ALU.add).then_inc(s_conv, 1)

                def channels(i, m):
                    j = i * 2 + m
                    convolve(j, 0)
                    convolve(j, 1)
                    dve.wait_ge(s_silu, j + 1)
                    dve.wait_ge(s_conv, j * 2 + 4)
                    dve.wait_ge(s_stored[m], i * 16 + 16)
                    dve.tensor_tensor(act_out[m][:], acc[0][:], acc[1][:], ALU.mult).then_inc(s_prod, 1)

                with dve.Fori(0, FT // 2 - 1) as i:
                    channels(i, 0)
                    channels(i, 1)
                channels(FT // 2 - 1, 0)
                convolve(FT - 1, 0)
                dve.wait_ge(s_silu, FT)
                dve.wait_ge(s_stored[1], FT // 2 * 16)
                for part, (t0, t1) in enumerate(((0, CUT), (CUT, S))):
                    convolve(FT - 1, 1, t0, t1, NCH - 1 + part, part * 2)
                    dve.wait_ge(s_conv, FT * 2 + 2 + part)
                    dve.tensor_tensor(act_out[1][:, t0:t1], acc[0][:, t0:t1], acc[1][:, t0:t1], ALU.mult).then_inc(s_prod, 1)


def down_projection(k, a, out, scratch):
    nc, psum = k.nc, k.psum
    with ExitStack() as ctx:
        def sb(name, shape, dt=F32):
            return ctx.enter_context(nc.sbuf_tensor(name, shape, dt))

        EARLY = 6
        w_next = sb("wdown_next", [P, EARLY, CH])
        w_hi = sb("wdown_hi", [P, FT, CH], F32R)
        w_raw, w_lo = k.overlaid(ctx, ("wdown_raw", [P, FT, CH], F32), ("wdown_lo", [P, FT, CH], F32R))
        a_raw = sb("act_raw", [P, FT, P])
        a_hi = [sb(f"act_hi{i}", [P, FT, P], F32R) for i in range(2)]
        a_lo = [sb(f"act_lo{i}", [P, FT, P], F32R) for i in range(2)]
        x2_left = sb("x2_left", [P, NB, CH])
        x2_right = [sb(f"x2_right{i}", [P, CH]) for i in range(2)]
        gated = sb("gated", [P, CH])
        g2, final_g = sb("g2_wide", [P, D]), sb("final_g_wide", [P, D])
        junk = [sb(f"x2_junk{i}", [P, CH], BF16) for i in range(2)]
        ssq = [sb(f"x2_ssq{half}", [P, NB]) for half in range(2)]
        rstd, msq = ([sb(f"x2_{n}{i}", [P, 1]) for i in range(2)] for n in ("rstd", "msq"))
        newton = sb("newton7", [P, 1])

        s_wide = k.sem("wide_vectors_landed")
        s_left = k.sem("x1_left_landed")
        s_right = [k.sem(f"x1_right_landed{i}") for i in range(2)]
        s_w = [k.sem(f"wdown_landed{i}") for i in range(4)]
        s_w2 = [k.sem(f"wdown_second_landed{i}") for i in range(4)]
        s_early = k.sem("wdown_next_landed")
        s_left_rows = k.sem("wdown_rows_left")
        s_whi = k.sem("wdown_hi_ready")
        s_wlo = k.sem("wdown_lo_ready")
        s_a = k.sem("act_landed")
        s_hi = k.sem("act_hi_ready")
        s_lo = k.sem("act_lo_ready")
        s_mm = k.sem("down_accumulated")
        s_gated = k.sem("ffn_gated")
        s_x2 = k.sem("x2_ready")
        s_sq = k.sem("x2_squared")
        s_msq = k.sem("x2_mean_square_step")
        s_root = k.sem("x2_rsqrt_refined")
        s_std = k.sem("x2_std_ready")
        s_rstd = k.sem("x2_rstd_ready")
        s_out = k.sem("out_ready")
        s_stored = [k.sem(f"out_stored{i}") for i in range(2)]

        with nc.Block() as block:

            @block.sync
            def _(sp):
                def load(u, n):
                    sp.wait_ge(s_lo, u + 1)
                    sp.dma_start(a_raw[:], scratch["act"][ds(n, 1)].rearrange("o p k t -> p (o k) t")).then_inc(s_a, 16)

                def weights(half, first, last, where):
                    src = a["w_down"][0, first * P:last * P, half * CH:(half + 1) * CH].rearrange("(k p) n -> p k n", p=P)
                    sp.dma_start(where, src).then_inc(s_w[first // 2 % 4], 16)

                load(0, 0)
                for kt in range(0, FT, 2):
                    if kt >= 8:
                        sp.wait_ge(s_w[kt // 2 % 4], kt // 8 * 16)
                    weights(0, kt, kt + 2, w_raw[:, kt:kt + 2, :])
                load(1, 1)
                for half, t in ((0, g2), (1, final_g)):
                    src = scratch["mod"][0:1, 5 * D:6 * D] if t is g2 else a["final_g"].rearrange("(o d) -> o d", o=1)
                    sp.dma_start(t[:], src.broadcast_to([P, D])).then_inc(s_wide, 16)
                sp.dma_start(x2_left[:], scratch["x1"][:, 0:CH].rearrange("(n p) d -> p n d", p=P)).then_inc(s_left, 16)
                sp.dma_start(w_next[:], a["w_down"][0, 0:EARLY * P, CH:D].rearrange("(k p) n -> p k n", p=P)).then_inc(s_early, 16)
                with sp.Fori(2, NB) as n:
                    load(n, n)
                load(NB, 0)
                for kt in range(EARLY, FT, 2):
                    m = (kt - EARLY) // 2
                    if kt < FT - 2:
                        sp.wait_ge(s_left_rows, (kt + 2) // 2)
                    else:
                        sp.wait_ge(s_mm, NB + 2)
                    if m >= 4:
                        sp.wait_ge(s_w2[m % 4], m // 4 * 16)
                    sp.dma_start(w_raw[:, kt:kt + 2, :],
                                 a["w_down"][0, kt * P:(kt + 2) * P, CH:D].rearrange("(k p) n -> p k n", p=P)).then_inc(s_w2[m % 4], 16)
                load(NB + 1, 1)
                with sp.Fori(2, NB) as n:
                    load(n + NB, n)

            @block.gpsimd
            def _(pool):
                def load_right(n, s):
                    pool.dma_start(x2_right[s][:], scratch["x1"][ds(n * P, P), CH:D]).then_inc(s_right[s], 16)

                def store(n, s):
                    pool.wait_ge(s_out, n * 2 + 2)
                    pool.dma_start(out[0, ds(n * P, P), 0:CH], x2_left[:, ds(n, 1), :].rearrange("p o d -> p (o d)")).then_inc(s_stored[s], 16)
                    pool.dma_start(out[0, ds(n * P, P), CH:D], x2_right[s][:]).then_inc(s_stored[s], 16)

                for s in range(2):
                    load_right(s, s)
                with pool.Fori(0, NB // 2 - 1) as i:
                    for s in range(2):
                        store(i * 2 + s, s)
                        pool.wait_ge(s_stored[s], i * 32 + 32)
                        load_right(i * 2 + s + 2, s)
                for s in range(2):
                    store(NB - 2 + s, s)
                for s in range(2):
                    pool.wait_ge(s_stored[s], 32 * (NB // 2))

            @block.scalar
            def _(act):
                act.sem_inc(s_lo, 1)
                act.sem_inc(s_mm, 2)

                def cut(u, s):
                    act.wait_ge(s_a, u * 16 + 16)
                    act.wait_ge(s_mm, u + 1)
                    act.activation(a_hi[s][:], a_raw[:], ACT.Copy).then_inc(s_hi, 1)

                def cut_weights(half):
                    for kt in range(0, FT, 2):
                        if half == 0:
                            act.wait_ge(s_w[kt // 2 % 4], kt // 8 * 16 + 16)
                        elif kt < EARLY:
                            act.wait_ge(s_early, 16)
                            act.wait_ge(s_left_rows, (kt + 2) // 2)
                        else:
                            act.wait_ge(s_w2[(kt - EARLY) // 2 % 4], (kt - EARLY) // 8 * 16 + 16)
                        raw = w_next[:, kt:kt + 2, :] if half and kt < EARLY else w_raw[:, kt:kt + 2, :]
                        act.activation(w_hi[:, kt:kt + 2, :], raw, ACT.Copy).then_inc(s_whi, 1)

                def square_left(n, s):
                    act.wait_ge(s_x2, n + 2)
                    act.activation(junk[s][:], x2_left[:, ds(n, 1), :].rearrange("p o d -> p (o d)"), ACT.Square, accum_out=ssq[0][:, ds(n, 1)]).then_inc(s_sq, 1)

                def square_right(n, s):
                    act.wait_ge(s_x2, n + NB + 2)
                    act.activation(junk[s][:], x2_right[s][:], ACT.Square, accum_out=ssq[1][:, ds(n, 1)]).then_inc(s_sq, 1)
                    act.wait_ge(s_msq, n * 2 + 2)
                    act.activation(rstd[s][:], msq[s][:], ACT.Sqrt).then_inc(s_std, 1)

                cut(0, 0)
                cut_weights(0)
                cut(1, 1)
                with act.Fori(0, NB // 2 - 1) as i:
                    for s in range(2):
                        cut(i * 2 + s + 2, s)
                        square_left(i * 2 + s, s)
                cut(NB, 0)
                square_left(NB - 2, 0)
                cut_weights(1)
                cut(NB + 1, 1)
                square_left(NB - 1, 1)
                with act.Fori(0, NB // 2 - 1) as i:
                    for s in range(2):
                        cut(i * 2 + s + NB + 2, s)
                        square_right(i * 2 + s, s)
                square_right(NB - 2, 0)
                square_right(NB - 1, 1)

            @block.tensor
            def _(pe):
                def tile(u, s, bank, first, leaving=False):
                    pe.wait_ge(s_gated, u + 1)
                    pe.wait_ge(s_lo, u + 2)
                    for kt in range(FT):
                        if first and kt % 2 == 0:
                            pe.wait_ge(s_wlo, (u // NB) * (FT // 2) + kt // 2 + 1)
                        pe.matmul(psum[:, bank, :], a_hi[s][:, kt, :], w_hi[:, kt, :], start=(kt == 0), stop=False)
                        pe.matmul(psum[:, bank, :], a_hi[s][:, kt, :], w_lo[:, kt, :], start=False, stop=False)
                        mm = pe.matmul(psum[:, bank, :], a_lo[s][:, kt, :], w_hi[:, kt, :], start=False, stop=(kt == FT - 1))
                        if leaving and kt % 2 == 1 and kt < FT - 1:
                            mm.then_inc(s_left_rows, 1)
                    mm.then_inc(s_mm, 1)

                for half in range(2):
                    tile(half * NB, 0, 0, True)
                    with pe.Fori(half * NB // 2, (half + 1) * NB // 2 - 1) as i:
                        tile(i * 2 + 1, 1, 1, False)
                        tile(i * 2 + 2, 0, 0, False)
                    tile(half * NB + NB - 1, 1, 1, False, leaving=(half == 0))

            @block.vector
            def _(dve):
                dve.sem_inc(s_gated, 2)
                dve.sem_inc(s_x2, 1)

                def cut(u, s):
                    dve.wait_ge(s_hi, u + 1)
                    dve.tensor_tensor(a_lo[s][:], a_raw[:], a_hi[s][:].bitcast(F32), ALU.subtract).then_inc(s_lo, 1)

                def cut_weights(half):
                    for kt in range(0, FT, 2):
                        dve.wait_ge(s_whi, half * (FT // 2) + kt // 2 + 1)
                        raw = w_next[:, kt:kt + 2, :] if half and kt < EARLY else w_raw[:, kt:kt + 2, :]
                        dve.tensor_tensor(w_lo[:, kt:kt + 2, :], raw, w_hi[:, kt:kt + 2, :].bitcast(F32), ALU.subtract).then_inc(s_wlo, 1)

                def residual(u, half, bank, x2):
                    dve.wait_ge(s_mm, u + 3)
                    dve.wait_ge(s_x2, u + 1)
                    dve.tensor_tensor(gated[:], psum[:, bank, :], g2[:, half * CH:(half + 1) * CH], ALU.mult).then_inc(s_gated, 1)
                    dve.wait_ge(s_gated, u + 3)
                    dve.tensor_tensor(x2, x2, gated[:], ALU.add).then_inc(s_x2, 1)

                def left(n, s):
                    residual(n, 0, s, x2_left[:, ds(n, 1), :].rearrange("p o d -> p (o d)"))

                def right(n, s, turn):
                    dve.wait_ge(s_right[s], turn * 16 + 16)
                    residual(n + NB, 1, s, x2_right[s][:])

                def finish(n, s):
                    dve.wait_ge(s_sq, n + NB + 1)
                    dve.tensor_tensor(msq[s][:], ssq[0][:, ds(n, 1)], ssq[1][:, ds(n, 1)], ALU.add).then_inc(s_msq, 1)
                    dve.wait_ge(s_msq, n * 2 + 1)
                    dve.tensor_scalar(msq[s][:], msq[s][:], 1.0 / D, EPS, ALU.mult, ALU.add).then_inc(s_msq, 1)
                    dve.wait_ge(s_std, n + 1)
                    dve.reciprocal(rstd[s][:], rstd[s][:]).then_inc(s_rstd, 1)
                    dve.wait_ge(s_rstd, n + 1)
                    refine_rsqrt(dve, rstd[s][:], msq[s][:], newton[:], s_root, n * 4)
                    for tile, cols in ((x2_left[:, ds(n, 1), :].rearrange("p o d -> p (o d)"), slice(0, CH)), (x2_right[s][:], slice(CH, D))):
                        dve.scalar_tensor_tensor(tile, tile, rstd[s][:], final_g[:, cols], ALU.mult, ALU.mult).then_inc(s_out, 1)

                cut(0, 0)
                cut_weights(0)
                cut(1, 1)
                dve.wait_ge(s_wide, 32)
                dve.wait_ge(s_left, 16)
                with dve.Fori(0, NB // 2 - 1) as i:
                    for s in range(2):
                        left(i * 2 + s, s)
                        cut(i * 2 + s + 2, s)
                left(NB - 2, 0)
                cut(NB, 0)
                left(NB - 1, 1)
                cut_weights(1)
                cut(NB + 1, 1)
                with dve.Fori(0, NB // 2 - 1) as i:
                    for s in range(2):
                        right(i * 2 + s, s, i)
                        cut(i * 2 + s + NB + 2, s)
                        finish(i * 2 + s, s)
                for s in range(2):
                    right(NB - 2 + s, s, NB // 2 - 1)
                    finish(NB - 2 + s, s)


def build(nc, a, out):
    ctx = ExitStack()
    with ctx:
        k = Kit(nc, ctx)
        scratch = {n: k.dram(n, s, d) for n, s, d in (
            ("mod", [2, 6 * D], F32), ("xr", [D_RNN, T], F32), ("xg", [D_RNN, S], F32),
            ("qk_hi", [D_ATTN + N_KV * HEAD, T], F32), ("qk_lo", [D_ATTN + N_KV * HEAD, T], F32),
            ("v", [N_KV * HEAD, T], F32), ("mix", [D_RNN, S], F32), ("att", [S, D_ATTN], F32), ("x1", [S, D], F32), ("act", [NB, P, FT, P], F32))}
        keep = {n: k.keep(n, s, F32) for n, s in (
            ("ident", [P, P]), ("ones", [P, 1]), ("cond", [P, KD]), ("aff2", [P, 2, KD]), ("msq_attn", [P, NB]))}
        with ExitStack() as features:
            hT_hi = features.enter_context(nc.sbuf_tensor("hT_hi", [P, PAIRS, KD, 2 * P], F32R))
            x_raw, hT_lo = k.overlaid(features, ("x_raw", [P, PAIRS, 2 * D], F32), ("hT_lo", [P, PAIRS, KD, 2 * P], F32R))
            modulation_and_norm(k, a, hT_hi, hT_lo, x_raw, keep, scratch)
            k.next_phase()
            input_projection(k, a, hT_hi, hT_lo, keep, scratch)
            k.next_phase()
        mixers(k, a, keep, scratch)
        k.next_phase()
        rstd2 = k.keep("rstd2", [P, NB], F32)
        x1_life, h2T_life = ExitStack(), ExitStack()
        x1 = x1_life.enter_context(nc.sbuf_tensor("x1_tiles", [P, NB, D], F32, side="right"))
        output_projection(k, a, x1, rstd2, keep, scratch)
        k.next_phase()
        h2T_hi, h2T_lo = (h2T_life.enter_context(nc.sbuf_tensor(n, [P, KD, S], F32R)) for n in ("h2T_hi", "h2T_lo"))
        modulate_x1(k, x1, rstd2, h2T_hi, h2T_lo, keep)
        k.next_phase()
        x1_life.close()
        up_projection(k, a, h2T_hi, h2T_lo, keep, scratch)
        k.next_phase()
        h2T_life.close()
        down_projection(k, a, out, scratch)


_INS = ["x", "c", "ctx", "c_ctx", "w_mod", "b_mod", "norm1_g", "w_in", "rnn_conv_w", "rnn_conv_b", "lru_w_a", "lru_b_a",
        "lru_w_i", "lru_b_i", "lru_lam", "attn_sink", "gn_rnn", "gn_attn", "w_out", "norm2_g", "w_up", "ffn_conv_w",
        "ffn_conv_b", "w_down", "final_g"]


def shape_tables():
    half = HEAD // 4
    inv = ROPE_THETA ** (-np.arange(half, dtype=np.float32) / half)
    t = np.arange(S)
    pos = np.stack([t // GRID_W, t % GRID_W]).astype(np.float32)
    p = np.arange(P) % HEAD
    ang = (pos[p // (HEAD // 2)] * inv[p % half][:, None]).astype(np.float32)
    sign = np.where(p % (HEAD // 2) < half, -1.0, 1.0).astype(np.float32)[:, None]
    return {"rope_cos": np.cos(ang).astype(np.float32), "rope_sin": (sign * np.sin(ang)).astype(np.float32)}


def kernel(**inputs):
    import concourse.bacc as _bacc
    from concourse.bass_utils import run_bass_kernel_spmd as _run

    nc = _bacc.Bacc("TRN2", target_bir_lowering=False, num_devices=1)
    arrays, aps = {}, {}
    for name, value in [(n, inputs[n]) for n in _INS] + list(shape_tables().items()):
        v = np.ascontiguousarray(value)
        arrays[f"in_{name}"] = v
        aps[name] = nc.dram_tensor(f"in_{name}", v.shape, mybir.dt.from_np(v.dtype), kind="ExternalInput").ap()
    out = nc.dram_tensor("out", (1, S, D), F32, kind="ExternalOutput").ap()
    build(nc, aps, out)
    result = _run(nc, [arrays], core_ids=[0])
    return result.results[0]["out"]
```
